# Optimizing a Trainium2 kernel written in Bass

```python
import jax, jax.numpy as jnp
from jax import lax
import numpy as np
import math
import jax
import jax.numpy as jnp

D_MODEL = 1024
BATCH = 1
SEQ = 1024
DEPTH = 1

GRID_W = 64
MEM_TOKENS = 256
MLSTM_HEADS = 4
MLSTM_QK_DIM = 64
MLSTM_V_DIM = 128
MLSTM_CHUNK = 64
MLSTM_CONV = 5
NA_HEADS = 8
NA_HEAD_DIM = 32
NA_WIN_ROWS = 8
NA_WIN_COLS = 16
MEM_HEADS = 4
MEM_HEAD_DIM = 64
N_BRANCH = 3
D_FF = 4 * D_MODEL
EPS = 1e-6

MLSTM_QK_W = MLSTM_HEADS * MLSTM_QK_DIM
MLSTM_V_W = MLSTM_HEADS * MLSTM_V_DIM
NA_W = NA_HEADS * NA_HEAD_DIM
MEM_W = MEM_HEADS * MEM_HEAD_DIM
IN_SPLITS = (2 * MLSTM_QK_W, MLSTM_V_W, MLSTM_V_W, 2 * MLSTM_HEADS, 2 * MLSTM_HEADS,
             3 * NA_W, MEM_W, N_BRANCH * D_MODEL)
D_IN = sum(IN_SPLITS)


def rmsnorm(x, g):
    xf = x.astype(jnp.float32)
    y = xf * lax.rsqrt(jnp.mean(xf * xf, axis=-1, keepdims=True) + EPS)
    return (y * g.astype(jnp.float32)).astype(x.dtype)

def short_conv(x, w, b):
    c = x.shape[-1]
    y = lax.conv_general_dilated(
        x, w[:, None, :].astype(x.dtype), window_strides=(1,),
        padding=[(MLSTM_CONV // 2, MLSTM_CONV // 2)],
        dimension_numbers=('NWC', 'WIO', 'NWC'), feature_group_count=c)
    return y + b.astype(x.dtype)

def _mlstm_chunk_step(carry, inp):
    c_st, n_st, m_st = carry
    q, k, v, ig, lf = inp
    L = q.shape[-2]
    tril = jnp.tril(jnp.ones((L, L), dtype=bool))
    b = jnp.cumsum(lf, axis=-1)
    d_log = jnp.where(tril, b[..., :, None] - b[..., None, :] + ig[..., None, :], -jnp.inf)
    inter = b + m_st[..., None]
    m_t = jnp.maximum(inter, jnp.max(d_log, axis=-1))
    s = jnp.einsum('bhtd,bhsd->bhts', q, k) * jnp.exp(d_log - m_t[..., None])
    w_inter = jnp.exp(inter - m_t)
    num = (jnp.einsum('bhts,bhsv->bhtv', s, v)
           + w_inter[..., None] * jnp.einsum('bhvd,bhtd->bhtv', c_st, q))
    den = jnp.sum(s, axis=-1) + w_inter * jnp.einsum('bhd,bhtd->bht', n_st, q)
    h = num / jnp.maximum(jnp.abs(den), jnp.exp(-m_t))[..., None]
    b_last = b[..., -1]
    w_log = b_last[..., None] - b + ig
    m_new = jnp.maximum(b_last + m_st, jnp.max(w_log, axis=-1))
    decay = jnp.exp(b_last + m_st - m_new)
    ws = jnp.exp(w_log - m_new[..., None])
    c_new = decay[..., None, None] * c_st + jnp.einsum('bhs,bhsv,bhsd->bhvd', ws, v, k)
    n_new = decay[..., None] * n_st + jnp.einsum('bhs,bhsd->bhd', ws, k)
    return (c_new, n_new, m_new), h

def mlstm_chunkwise(q, k, v, ig, lf):
    bsz, s, nh, dk = q.shape
    dv = v.shape[-1]
    nc = s // MLSTM_CHUNK

    def chunks(a):
        a = a.reshape((bsz, nc, MLSTM_CHUNK, nh) + a.shape[3:])
        return jnp.swapaxes(jnp.moveaxis(a, 1, 0), 2, 3)

    init = (jnp.zeros((bsz, nh, dv, dk), jnp.float32),
            jnp.zeros((bsz, nh, dk), jnp.float32),
            jnp.full((bsz, nh), -jnp.inf, jnp.float32))
    _, hs = lax.scan(_mlstm_chunk_step, init,
                     (chunks(q), chunks(k), chunks(v), chunks(ig), chunks(lf)))
    return jnp.swapaxes(jnp.moveaxis(hs, 0, 1), 2, 3).reshape(bsz, s, nh, dv)

def neighbourhood_attention(q, k, v, rpb):
    bsz, s, nh, dh = q.shape
    rows = s // GRID_W
    win_r = min(NA_WIN_ROWS, rows)
    grid = lambda a: a.reshape(bsz, rows, GRID_W, nh, dh)
    qg, kg, vg = grid(q), grid(k), grid(v)
    row_start = jnp.clip(jnp.arange(rows) - win_r // 2, 0, rows - win_r)
    cols = jnp.arange(GRID_W)
    col_idx = (jnp.clip(cols - NA_WIN_COLS // 2, 0, GRID_W - NA_WIN_COLS)[:, None]
               + jnp.arange(NA_WIN_COLS))
    col_off = col_idx - cols[:, None] + (NA_WIN_COLS - 1)

    def one_row(r):
        rs = row_start[r]
        q_row = lax.dynamic_index_in_dim(qg, r, axis=1, keepdims=False)
        k_win = lax.dynamic_slice_in_dim(kg, rs, win_r, axis=1)[:, :, col_idx]
        v_win = lax.dynamic_slice_in_dim(vg, rs, win_r, axis=1)[:, :, col_idx]
        row_off = rs + jnp.arange(win_r) - r + (NA_WIN_ROWS - 1)
        bias = rpb[:, row_off[None, :, None], col_off[:, None, :]]
        sc = (jnp.einsum('bchd,bicjhd->bhcij', q_row, k_win).astype(jnp.float32)
              + bias.astype(jnp.float32)[None])
        p = jax.nn.softmax(sc.reshape(bsz, nh, GRID_W, win_r * NA_WIN_COLS), axis=-1)
        p = p.reshape(sc.shape).astype(v.dtype)
        return jnp.einsum('bhcij,bicjhd->bchd', p, v_win)

    out = lax.map(one_row, jnp.arange(rows))
    return jnp.moveaxis(out, 0, 1).reshape(bsz, s, nh * dh)

def memory_cross_attention(q, mem_n, w_mem_kv, g_mem_q, g_mem_k):
    bsz, s, _ = q.shape
    m = mem_n.shape[1]
    k, v = jnp.split(mem_n @ w_mem_kv, 2, axis=-1)
    q = rmsnorm(q.reshape(bsz, s, MEM_HEADS, MEM_HEAD_DIM), g_mem_q) * (MEM_HEAD_DIM ** -0.5)
    k = rmsnorm(k.reshape(bsz, m, MEM_HEADS, MEM_HEAD_DIM), g_mem_k)
    v = v.reshape(bsz, m, MEM_HEADS, MEM_HEAD_DIM)
    sc = jnp.einsum('bshd,bmhd->bhsm', q, k).astype(jnp.float32)
    p = jax.nn.softmax(sc, axis=-1).astype(v.dtype)
    return jnp.einsum('bhsm,bmhd->bshd', p, v).reshape(bsz, s, MEM_W)

def hybrid_layer(x, mem, g_mix, w_in, conv_w, conv_b, b_igate, b_fgate, g_mlstm, w_proj_mlstm,
                 g_na_q, g_na_k, rpb, w_proj_na, g_mem, w_mem_kv, g_mem_q, g_mem_k,
                 w_proj_mem, w_out, g_ffn, w_up, w_down):
    bsz, s, _ = x.shape
    h = rmsnorm(x, g_mix)
    z = h @ w_in
    split_idx = np.cumsum(np.array(IN_SPLITS))[:-1]
    qk_m, v_m, o_m, i_pre, f_pre, qkv_na, q_mem, gate_pre = jnp.split(z, split_idx, axis=-1)

    qk_m = jax.nn.silu(short_conv(qk_m, conv_w, conv_b))
    q_m, k_m = jnp.split(qk_m, 2, axis=-1)
    q_m = q_m.reshape(bsz, s, MLSTM_HEADS, MLSTM_QK_DIM).astype(jnp.float32) * (MLSTM_QK_DIM ** -0.5)
    k_m = k_m.reshape(bsz, s, MLSTM_HEADS, MLSTM_QK_DIM).astype(jnp.float32)
    vv = v_m.reshape(bsz, s, MLSTM_HEADS, MLSTM_V_DIM).astype(jnp.float32)
    i_log = i_pre.reshape(bsz, s, 2, MLSTM_HEADS).astype(jnp.float32) + b_igate.astype(jnp.float32)
    f_log = jax.nn.log_sigmoid(f_pre.reshape(bsz, s, 2, MLSTM_HEADS).astype(jnp.float32)
                               + b_fgate.astype(jnp.float32))
    flip = lambda a: jnp.flip(a, axis=1)
    h_fwd = mlstm_chunkwise(q_m, k_m, vv, i_log[:, :, 0], f_log[:, :, 0])
    h_bwd = flip(mlstm_chunkwise(flip(q_m), flip(k_m), flip(vv),
                                 flip(i_log[:, :, 1]), flip(f_log[:, :, 1])))
    h_m = rmsnorm(h_fwd + h_bwd, g_mlstm.reshape(MLSTM_HEADS, MLSTM_V_DIM))
    h_m = (h_m.reshape(bsz, s, MLSTM_V_W) * jax.nn.sigmoid(o_m.astype(jnp.float32))).astype(x.dtype)

    q_na, k_na, v_na = jnp.split(qkv_na.reshape(bsz, s, 3, NA_HEADS, NA_HEAD_DIM), 3, axis=2)
    q_na = rmsnorm(q_na[:, :, 0], g_na_q) * (NA_HEAD_DIM ** -0.5)
    k_na = rmsnorm(k_na[:, :, 0], g_na_k)
    h_na = neighbourhood_attention(q_na, k_na, v_na[:, :, 0], rpb)

    h_mem = memory_cross_attention(q_mem, rmsnorm(mem, g_mem), w_mem_kv, g_mem_q, g_mem_k)

    gates = jax.nn.sigmoid(gate_pre).reshape(bsz, s, N_BRANCH, D_MODEL)
    y = (gates[:, :, 0] * (h_m @ w_proj_mlstm)
         + gates[:, :, 1] * (h_na @ w_proj_na)
         + gates[:, :, 2] * (h_mem @ w_proj_mem))
    x = x + y @ w_out

    u = rmsnorm(x, g_ffn) @ w_up
    return x + jnp.square(jax.nn.relu(u)) @ w_down

def first_inputs(seed: int = 0) -> dict:
    key = jax.random.key(seed)
    ks = jax.random.split(key, 24)
    nrm = lambda k, shape, scale: jax.random.normal(k, shape, jnp.float32) * scale
    gain = lambda k, shape: 1.0 + 0.1 * jax.random.normal(k, shape, jnp.float32)
    L = DEPTH
    f_bias = (jnp.linspace(3.0, 6.0, MLSTM_HEADS, dtype=jnp.float32)[None, None, :]
              + nrm(ks[8], (L, 2, MLSTM_HEADS), 0.1))
    return {
        'x': nrm(ks[0], (BATCH, SEQ, D_MODEL), 1.0),
        'mem': nrm(ks[1], (BATCH, MEM_TOKENS, D_MODEL), 1.0),
        'g_mix': gain(ks[2], (L, D_MODEL)),
        'w_in': nrm(ks[3], (L, D_MODEL, D_IN), D_MODEL ** -0.5),
        'conv_w': nrm(ks[4], (L, MLSTM_CONV, 2 * MLSTM_QK_W), MLSTM_CONV ** -0.5),
        'conv_b': nrm(ks[5], (L, 2 * MLSTM_QK_W), 0.02),
        'b_igate': nrm(ks[6], (L, 2, MLSTM_HEADS), 0.1),
        'b_fgate': f_bias,
        'g_mlstm': gain(ks[7], (L, MLSTM_V_W)),
        'w_proj_mlstm': nrm(ks[9], (L, MLSTM_V_W, D_MODEL), MLSTM_V_W ** -0.5),
        'g_na_q': gain(ks[10], (L, NA_HEAD_DIM)),
        'g_na_k': gain(ks[11], (L, NA_HEAD_DIM)),
        'rpb': nrm(ks[12], (L, NA_HEADS, 2 * NA_WIN_ROWS - 1, 2 * NA_WIN_COLS - 1), 0.1),
        'w_proj_na': nrm(ks[13], (L, NA_W, D_MODEL), NA_W ** -0.5),
        'g_mem': gain(ks[14], (L, D_MODEL)),
        'w_mem_kv': nrm(ks[15], (L, D_MODEL, 2 * MEM_W), D_MODEL ** -0.5),
        'g_mem_q': gain(ks[16], (L, MEM_HEAD_DIM)),
        'g_mem_k': gain(ks[17], (L, MEM_HEAD_DIM)),
        'w_proj_mem': nrm(ks[18], (L, MEM_W, D_MODEL), MEM_W ** -0.5),
        'w_out': nrm(ks[19], (L, D_MODEL, D_MODEL), D_MODEL ** -0.5),
        'g_ffn': gain(ks[20], (L, D_MODEL)),
        'w_up': nrm(ks[21], (L, D_MODEL, D_FF), D_MODEL ** -0.5),
        'w_down': nrm(ks[22], (L, D_FF, D_MODEL), D_FF ** -0.5),
    }

def first_block(x, mem, g_mix, w_in, conv_w, conv_b, b_igate, b_fgate, g_mlstm, w_proj_mlstm,
              g_na_q, g_na_k, rpb, w_proj_na, g_mem, w_mem_kv, g_mem_q, g_mem_k,
              w_proj_mem, w_out, g_ffn, w_up, w_down):
    for l in range(DEPTH):
        x = hybrid_layer(x, mem, g_mix[l], w_in[l], conv_w[l], conv_b[l], b_igate[l], b_fgate[l],
                         g_mlstm[l], w_proj_mlstm[l], g_na_q[l], g_na_k[l], rpb[l], w_proj_na[l],
                         g_mem[l], w_mem_kv[l], g_mem_q[l], g_mem_k[l], w_proj_mem[l], w_out[l],
                         g_ffn[l], w_up[l], w_down[l])
    return x


A_DK = 128
A_DV = 128
A_HEADS = D_MODEL // (2 * A_DV)
CONV_K = 4
B_DK = 128
B_DV = 128
B_HEADS = D_MODEL // (2 * B_DV)
ROPE_BASE = 10000.0
CHUNK = 64
N_GROUPS = 8
EXPERTS_PER_GROUP = 8
N_EXPERTS = N_GROUPS * EXPERTS_PER_GROUP
TOP_K = 2
D_EXPERT = 256

A_QK = A_HEADS * A_DK
A_V = A_HEADS * A_DV
A_CONV = 2 * A_QK + A_V
B_QK = B_HEADS * B_DK
B_V = B_HEADS * B_DV
D_MIX = A_V + B_V
IN_SIZES = (A_QK, A_QK, A_V, A_V, A_HEADS, A_HEADS, B_QK, B_QK, B_V, B_V)
D_IN_2 = sum(IN_SIZES)


def rms_norm(x, w):
    xf = x.astype(jnp.float32)
    y = xf * lax.rsqrt(jnp.mean(xf * xf, axis=-1, keepdims=True) + EPS)
    return (y * w.astype(jnp.float32)).astype(x.dtype)

def l2norm(t):
    return t * lax.rsqrt(jnp.sum(t * t, axis=-1, keepdims=True) + EPS)

def to_heads(t, n_heads):
    b, s, _ = t.shape
    return t.reshape(b, s, n_heads, -1).transpose(0, 2, 1, 3)

def to_chunks(t):
    b, h, s = t.shape[:3]
    return t.reshape(b, h, s // CHUNK, CHUNK, *t.shape[3:])

def from_chunks(o):
    n, b, h, c, d = o.shape
    return jnp.moveaxis(o, 0, 2).reshape(b, h, n * c, d).transpose(0, 2, 1, 3)

def causal_conv(x, w):
    return lax.conv_general_dilated(
        x, w[:, None, :], window_strides=(1,), padding=[(CONV_K - 1, 0)],
        dimension_numbers=("NWC", "WIO", "NWC"), feature_group_count=x.shape[-1])

def rope(t, cos, sin):
    half = t.shape[-1] // 2
    t1, t2 = t[..., :half], t[..., half:]
    return jnp.concatenate([t1 * cos - t2 * sin, t1 * sin + t2 * cos], axis=-1)

def gated_delta_net(qkv, gate, beta_in, alpha_in, conv_w, a_log, dt_bias, norm_w):
    b, s, _ = qkv.shape
    qkv = jax.nn.silu(causal_conv(qkv, conv_w.astype(jnp.float32)))
    q, k, v = jnp.split(qkv, [A_QK, 2 * A_QK], axis=-1)
    q = l2norm(to_heads(q, A_HEADS)) * (A_DK ** -0.5)
    k = l2norm(to_heads(k, A_HEADS))
    v = to_heads(v, A_HEADS)
    beta = jax.nn.sigmoid(beta_in).transpose(0, 2, 1)
    g = (-jnp.exp(a_log.astype(jnp.float32))
         * jax.nn.softplus(alpha_in + dt_bias.astype(jnp.float32))).transpose(0, 2, 1)
    q, k, v, beta, g = (to_chunks(t) for t in (q, k, v, beta, g))
    gc = jnp.cumsum(g, axis=-1)
    causal = jnp.tril(jnp.ones((CHUNK, CHUNK), dtype=bool))
    strict = jnp.tril(jnp.ones((CHUNK, CHUNK), dtype=bool), -1)
    diff = gc[..., :, None] - gc[..., None, :]
    decay = jnp.where(causal, jnp.exp(jnp.where(causal, diff, 0.0)), 0.0)
    kb = k * beta[..., None]
    a_mat = jnp.where(strict, jnp.einsum("bhnid,bhnjd->bhnij", kb, k) * decay, 0.0)
    rhs = jnp.concatenate([v * beta[..., None], kb * jnp.exp(gc)[..., None]], axis=-1)
    uw = lax.linalg.triangular_solve(a_mat, rhs, left_side=True, lower=True, unit_diagonal=True)
    u, w = uw[..., :A_DV], uw[..., A_DV:]
    attn = jnp.einsum("bhnid,bhnjd->bhnij", q, k) * decay
    q_dec = q * jnp.exp(gc)[..., None]
    k_dec = k * jnp.exp(gc[..., -1:] - gc)[..., None]
    last = jnp.exp(gc[..., -1])

    def step(state, inp):
        q_c, k_c, u_c, w_c, attn_c, last_c = inp
        v_new = u_c - jnp.einsum("bhck,bhkv->bhcv", w_c, state)
        o_c = (jnp.einsum("bhck,bhkv->bhcv", q_c, state)
               + jnp.einsum("bhcj,bhjv->bhcv", attn_c, v_new))
        state = state * last_c[..., None, None] + jnp.einsum("bhck,bhcv->bhkv", k_c, v_new)
        return state, o_c

    xs = tuple(jnp.moveaxis(t, 2, 0) for t in (q_dec, k_dec, u, w, attn, last))
    s0 = jnp.zeros((b, A_HEADS, A_DK, A_DV), jnp.float32)
    _, o = lax.scan(step, s0, xs)
    o = from_chunks(o)
    o = rms_norm(o, norm_w) * jax.nn.silu(gate.reshape(b, s, A_HEADS, A_DV))
    return o.reshape(b, s, A_V)

def retention(q, k, v, gate, cos, sin, norm_w):
    b, s, _ = q.shape
    q = rope(to_heads(q, B_HEADS), cos, sin)
    k = rope(to_heads(k, B_HEADS), cos, sin) * (B_DK ** -0.5)
    v = to_heads(v, B_HEADS)
    log_gamma = jnp.log(1.0 - 2.0 ** (-5.0 - jnp.arange(B_HEADS, dtype=jnp.float32)))
    pos = jnp.arange(CHUNK, dtype=jnp.float32)
    rel = pos[:, None] - pos[None, :]
    decay = jnp.where(rel >= 0, jnp.exp(jnp.maximum(rel, 0.0) * log_gamma[:, None, None]), 0.0)
    q, k, v = (to_chunks(t) for t in (q, k, v))
    attn = jnp.einsum("bhnid,bhnjd->bhnij", q, k) * decay[None, :, None]
    inner = jnp.einsum("bhnij,bhnjv->bhniv", attn, v)
    q_dec = q * jnp.exp((pos + 1.0) * log_gamma[:, None])[None, :, None, :, None]
    k_dec = k * jnp.exp((CHUNK - 1.0 - pos) * log_gamma[:, None])[None, :, None, :, None]
    chunk_decay = jnp.exp(CHUNK * log_gamma)[None, :, None, None]

    def step(state, inp):
        q_c, k_c, v_c = inp
        o_c = jnp.einsum("bhck,bhkv->bhcv", q_c, state)
        state = state * chunk_decay + jnp.einsum("bhck,bhcv->bhkv", k_c, v_c)
        return state, o_c

    xs = tuple(jnp.moveaxis(t, 2, 0) for t in (q_dec, k_dec, v))
    s0 = jnp.zeros((b, B_HEADS, B_DK, B_DV), jnp.float32)
    _, cross = lax.scan(step, s0, xs)
    o = from_chunks(cross) + from_chunks(jnp.moveaxis(inner, 2, 0))
    o = rms_norm(o, norm_w.reshape(B_HEADS, B_DV)) * jax.nn.silu(gate.reshape(b, s, B_HEADS, B_DV))
    return o.reshape(b, s, B_V)

def hierarchical_moe(h, w_router_group, w_router_expert, w_gate, w_up, w_down):
    b, s, d = h.shape
    ht = h.reshape(b * s, d)
    hf = ht.astype(jnp.float32)
    g_logits = hf @ w_router_group.astype(jnp.float32)
    g_prob = jax.nn.softmax(g_logits, axis=-1)
    g_idx = jnp.argmax(g_logits, axis=-1)
    g_w = jnp.take_along_axis(g_prob, g_idx[:, None], axis=-1)[:, 0]
    e_logits = (hf @ w_router_expert.astype(jnp.float32)).reshape(-1, N_GROUPS, EXPERTS_PER_GROUP)
    e_logits = jnp.take_along_axis(e_logits, g_idx[:, None, None], axis=1)[:, 0]
    e_prob = jax.nn.softmax(e_logits, axis=-1)
    top_p, top_i = lax.top_k(e_prob, TOP_K)
    top_p = top_p / jnp.sum(top_p, axis=-1, keepdims=True)
    weights = (g_w[:, None] * top_p).reshape(-1)
    expert_id = (g_idx[:, None] * EXPERTS_PER_GROUP + top_i).reshape(-1).astype(jnp.int32)
    order = jnp.argsort(expert_id)
    tok = order // TOP_K
    xs = ht[tok]
    group_sizes = jnp.zeros((N_EXPERTS,), jnp.int32).at[expert_id].add(1)
    gate = lax.ragged_dot(xs, w_gate, group_sizes)
    up = lax.ragged_dot(xs, w_up, group_sizes)
    y = lax.ragged_dot((jax.nn.silu(gate) * up).astype(xs.dtype), w_down, group_sizes)
    y = y * weights[order].astype(y.dtype)[:, None]
    out = jnp.zeros_like(ht).at[tok].add(y)
    return out.reshape(b, s, d)

def second_inputs(seed: int = 0) -> dict:
    key = jax.random.key(seed)
    ks = jax.random.split(key, 20)
    f32 = jnp.float32

    def nrm(k, shape, scale):
        return jax.random.normal(k, shape, f32) * scale

    def gain(k, shape):
        return 1.0 + 0.02 * jax.random.normal(k, shape, f32)

    x = nrm(ks[0], (BATCH, SEQ, D_MODEL), 1.0)
    attn_norm = gain(ks[1], (DEPTH, D_MODEL))
    w_in = nrm(ks[2], (DEPTH, D_MODEL, D_IN_2), D_MODEL ** -0.5)
    conv_a = nrm(ks[3], (DEPTH, CONV_K, A_CONV), CONV_K ** -0.5)
    a_log = jnp.log(jax.random.uniform(ks[4], (DEPTH, A_HEADS), f32, 1.0, 16.0))
    dt = jnp.exp(jax.random.uniform(ks[5], (DEPTH, A_HEADS), f32, math.log(1e-3), math.log(1e-1)))
    dt_bias = dt + jnp.log(-jnp.expm1(-dt))
    norm_a = gain(ks[6], (DEPTH, A_DV))
    norm_b = gain(ks[7], (DEPTH, B_V))
    w_out = nrm(ks[8], (DEPTH, D_MIX, D_MODEL), D_MIX ** -0.5)
    ffn_norm = gain(ks[9], (DEPTH, D_MODEL))
    w_router_group = nrm(ks[10], (DEPTH, D_MODEL, N_GROUPS), D_MODEL ** -0.5)
    w_router_expert = nrm(ks[11], (DEPTH, D_MODEL, N_EXPERTS), D_MODEL ** -0.5)
    w_gate = nrm(ks[12], (DEPTH, N_EXPERTS, D_MODEL, D_EXPERT), D_MODEL ** -0.5)
    w_up = nrm(ks[13], (DEPTH, N_EXPERTS, D_MODEL, D_EXPERT), D_MODEL ** -0.5)
    w_down = nrm(ks[14], (DEPTH, N_EXPERTS, D_EXPERT, D_MODEL), D_EXPERT ** -0.5)
    final_norm = gain(ks[15], (D_MODEL,))
    return {"x": x, "attn_norm": attn_norm, "w_in": w_in, "conv_a": conv_a,
            "a_log": a_log, "dt_bias": dt_bias, "norm_a": norm_a, "norm_b": norm_b,
            "w_out": w_out, "ffn_norm": ffn_norm, "w_router_group": w_router_group,
            "w_router_expert": w_router_expert, "w_gate": w_gate, "w_up": w_up,
            "w_down": w_down, "final_norm": final_norm}

def second_block(x, attn_norm, w_in, conv_a, a_log, dt_bias, norm_a, norm_b, w_out, ffn_norm,
              w_router_group, w_router_expert, w_gate, w_up, w_down, final_norm):
    s = x.shape[1]
    pos = jnp.arange(s, dtype=jnp.float32)
    inv_freq = ROPE_BASE ** (-jnp.arange(0, B_DK, 2, dtype=jnp.float32) / B_DK)
    ang = pos[:, None] * inv_freq[None, :]
    cos, sin = jnp.cos(ang), jnp.sin(ang)
    offsets = [int(o) for o in np.cumsum(IN_SIZES)[:-1]]
    for l in range(DEPTH):
        h = rms_norm(x, attn_norm[l])
        proj = jnp.einsum("bsd,de->bse", h, w_in[l]).astype(jnp.float32)
        q_a, k_a, v_a, g_a, beta_a, alpha_a, q_b, k_b, v_b, g_b = jnp.split(proj, offsets, axis=-1)
        o_a = gated_delta_net(jnp.concatenate([q_a, k_a, v_a], axis=-1), g_a, beta_a, alpha_a,
                              conv_a[l], a_log[l], dt_bias[l], norm_a[l])
        o_b = retention(q_b, k_b, v_b, g_b, cos, sin, norm_b[l])
        mixed = jnp.concatenate([o_a, o_b], axis=-1).astype(x.dtype)
        x = x + jnp.einsum("bse,ed->bsd", mixed, w_out[l])
        h2 = rms_norm(x, ffn_norm[l])
        x = x + hierarchical_moe(h2, w_router_group[l], w_router_expert[l],
                                 w_gate[l], w_up[l], w_down[l])
    return rms_norm(x, final_norm)


def setup_inputs(seed=0):
    out = dict(first_inputs(seed))
    for name, value in second_inputs(seed + 1).items():
        if name != "x":
            out[name + "_2"] = value
    return out


def reference(
    x, mem, g_mix, w_in, conv_w, conv_b, b_igate, b_fgate, g_mlstm, w_proj_mlstm, g_na_q,
    g_na_k, rpb, w_proj_na, g_mem, w_mem_kv, g_mem_q, g_mem_k, w_proj_mem, w_out, g_ffn, w_up,
    w_down, attn_norm_2, w_in_2, conv_a_2, a_log_2, dt_bias_2, norm_a_2, norm_b_2, w_out_2,
    ffn_norm_2, w_router_group_2, w_router_expert_2, w_gate_2, w_up_2, w_down_2, final_norm_2,
):
    x = first_block(
        x, mem, g_mix, w_in, conv_w, conv_b, b_igate, b_fgate, g_mlstm, w_proj_mlstm, g_na_q,
        g_na_k, rpb, w_proj_na, g_mem, w_mem_kv, g_mem_q, g_mem_k, w_proj_mem, w_out, g_ffn,
        w_up, w_down,
    )
    return second_block(
        x, attn_norm_2, w_in_2, conv_a_2, a_log_2, dt_bias_2, norm_a_2, norm_b_2, w_out_2,
        ffn_norm_2, w_router_group_2, w_router_expert_2, w_gate_2, w_up_2, w_down_2,
        final_norm_2,
    )


_drawn_inputs = setup_inputs


def setup_inputs(seed=0):
    import zlib

    import numpy as np

    out = dict(_drawn_inputs(seed))
    spreads = {}
    factors = {'conv_b': 4.02,
     'b_igate': 8.0,
     'g_na_q': 4.163,
     'g_na_k': 4.412,
     'rpb': 4.382,
     'g_mem': 4.277,
     'g_mem_q': 4.787,
     'g_mem_k': 6.107,
     'attn_norm_2': 3.197,
     'norm_a_2': 6.521,
     'norm_b_2': 8.0,
     'ffn_norm_2': 4.17,
     'final_norm_2': 2.868}
    for name, (base, spread) in spreads.items():
        noise = np.random.default_rng([zlib.crc32(name.encode()), seed]).standard_normal(out[name].shape)
        drawn = base * np.exp(spread * noise) if base else spread * noise
        out[name] = jnp.asarray(drawn.astype(out[name].dtype))
    for name, factor in factors.items():
        out[name] = (out[name] * factor).astype(out[name].dtype)
    return out
```

```python
from contextlib import ExitStack

import numpy as np

import concourse.bass as bass
from concourse import mybir

ALU = mybir.AluOpType
ACT = mybir.ActivationFunctionType
AX = mybir.AxisListType
F32 = mybir.dt.float32
I32 = mybir.dt.int32
U32 = mybir.dt.uint32

P = 128
BANK = 512
D = 1024
S = 1024
KT = D // P
TT = S // P
MEM = 256
EPS = 1e-6
D_FF = 4096

M_HEADS, M_QK, M_V, M_CONV = 4, 64, 128, 5
NA_HEADS, NA_HD, GRID_W, WIN_R, WIN_C = 8, 32, 64, 8, 16
MEM_HEADS, MEM_HD = 4, 64
A_HEADS, A_CONV_K = 4, 4
G_DIM = 128
N_EXPERTS, N_GROUPS, PER_GROUP, D_EXPERT = 64, 8, 8, 256

RING = 2


class Steps:

    def __init__(self, nc, ctx, name):
        self.sem = ctx.enter_context(nc.semaphore(name))
        self.count = 0

    def done(self, ins):
        ins.then_inc(self.sem, 1)
        self.count += 1
        return ins

    def settle(self, eng):
        eng.wait_ge(self.sem, self.count)

    def then_wait(self, eng, ins):
        self.done(ins)
        self.settle(eng)


class Chip:

    def __init__(self, nc, ctx, io):
        self.nc, self.io, self.ctx = nc, io, ctx
        self.psum = ctx.enter_context(nc.psum_tensor("banks", [P, 8, BANK], F32))
        self.ring = ctx.enter_context(nc.sbuf_tensor("weight_ring", [P, RING, KT, BANK], F32))
        self.landed = [ctx.enter_context(nc.semaphore(f"weights_landed_{i}")) for i in range(RING)]
        self.used = ctx.enter_context(nc.semaphore("weights_used"))
        self.chunks = weight_chunks(io)
        self.loaded = 0
        self.consts_landed = ctx.enter_context(nc.semaphore("consts_landed"))
        self.n_consts = 0
        self.k = {}

    def bank(self, i, n=BANK, parts=P):
        return self.psum[0:parts, i, 0:n]

    def sb(self, mem, name, shape, dt=F32):
        return mem.enter_context(self.nc.sbuf_tensor(name, shape, dt))

    def sem(self, mem, name):
        return mem.enter_context(self.nc.semaphore(name))

    def load_chunks(self, sp, upto):
        while self.loaded < min(upto, len(self.chunks)):
            j = self.loaded
            src, kt, n = self.chunks[j]
            if j >= RING:
                sp.wait_ge(self.used, j - RING + 1)
            sp.dma_start(self.ring[:, j % RING, 0:kt, 0:n], src).then_inc(self.landed[j % RING], 16)
            self.loaded += 1

    def wait_chunk(self, pe, j):
        pe.wait_ge(self.landed[j % RING], 16 * (j // RING + 1))

    def chunk(self, j):
        return self.ring[:, j % RING, :, :]


IN1 = dict(qk=0, v=512, o=1024, gates_if=1536, na_qk=1552, na_v_qmem=2064, branch=2576)
IN2 = dict(q=0, k=512, v=1024, g=1536, beta_alpha=2048, qb=2056, kb=2568, vb=3080, gb=3592)
C_QK, C_V, C_O, C_NAQK, C_NAV, C_MEMKV = range(6)
C_BRANCH = 6
C_OUT = C_BRANCH + 6
C_FFN = C_OUT + 2
C_IN2 = C_FFN + 16
C_OUT2 = C_IN2 + 8


def weight_chunks(io):
    def cols(w, c, n=BANK):
        return (w[:, c:c + n].rearrange("(k p) n -> p k n", p=P), w.shape[0] // P, n)

    w1, w2 = io["w_in"], io["w_in_2"]
    out = [cols(w1, IN1[k]) for k in ("qk", "v", "o", "na_qk", "na_v_qmem")]
    out.append(cols(io["w_mem_kv"], 0))
    out += [cols(w1, IN1["branch"] + b * D + n * BANK) for n in range(2) for b in range(3)]
    out += [cols(io["w_out"], n * BANK) for n in range(2)]
    for f in range(D_FF // D):
        out += [cols(io["w_up"], f * D + n * BANK) for n in range(2)]
        out += [cols(io["w_down"][f * D:(f + 1) * D, :], n * BANK) for n in range(2)]
    out += [cols(w2, IN2[k]) for k in ("q", "k", "v", "g", "qb", "kb", "vb", "gb")]
    out += [cols(io["w_out_2"], n * BANK) for n in range(2)]
    return out


def load_consts(c, mem, sizes):
    nc = c.nc
    for name, shape in sizes:
        c.k[name] = c.sb(mem, "c_" + name, shape)

    def load(eng, part):
        for name, shape in part:
            eng.dma_start(c.k[name][tuple(slice(None) for _ in shape)], c.io["k_" + name]).then_inc(c.consts_landed, 16)

    c.n_consts += len(sizes)
    with nc.Block() as block:
        @block.sync
        def _(sp):
            load(sp, sizes[0::2])

        @block.scalar
        def _(act):
            load(act, sizes[1::2])
            act.wait_ge(c.consts_landed, 16 * c.n_consts)


def norm_transpose(c, name, tiles, prefetch, source=None, keep=None, keep_gain=None, experts=None):
    nc, n = c.nc, len(tiles)
    XS, XN, NB = 3, 2, 4
    with ExitStack() as mem:
        loads = source == "dram"
        if loads:
            xs = c.sb(mem, name + "_x", [P, XS, D])
            landed = [c.sem(mem, f"{name}_x_landed_{i}") for i in range(XS)]
        junk = c.sb(mem, name + "_squares", [P, 2, D])
        xn = c.sb(mem, name + "_xn", [P, XN, D])
        ss = c.sb(mem, name + "_ss", [P, n])
        ms = c.sb(mem, name + "_ms", [P, n])
        rstd = c.sb(mem, name + "_rstd", [P, n])
        half = c.sb(mem, name + "_half", [P, 1])
        squared = c.sem(mem, name + "_squared")
        rstd_ready = c.sem(mem, name + "_rstd_ready")
        normed = c.sem(mem, name + "_normed")
        transposed = c.sem(mem, name + "_transposed")
        copied = c.sem(mem, name + "_copied")
        if keep is not None:
            kt = c.sb(mem, name + "_kept_tiles", [P, 2, D])
            kept = c.sem(mem, name + "_kept")
            kept_stored = [c.sem(mem, f"{name}_kept_stored_{i}") for i in range(2)]
        pool = Steps(nc, mem, name + "_pool_steps")

        def tile(i):
            return xs[:, i % XS, :] if loads else tiles[i][0]

        def x_there(eng, i):
            if loads:
                eng.wait_ge(landed[i % XS], 16 * (i // XS + 1))

        block = mem.enter_context(nc.Block())

        @block.sync
        def _(sp):
            if loads:
                for i in range(n):
                    if i >= XS:
                        sp.wait_ge(normed, i - XS + 1)
                    sp.dma_start(xs[:, i % XS, :], tiles[i][0]).then_inc(landed[i % XS], 16)
            c.load_chunks(sp, prefetch)
            if keep is not None:
                for i in range(n):
                    sp.wait_ge(kept, i + 1)
                    sp.dma_start(keep[i * P:(i + 1) * P, :], kt[:, i % 2, :]).then_inc(kept_stored[i % 2], 16)
                    if 0 < i < SLOTS:
                        experts.load(sp, i, i)
                for i in range(2):
                    sp.wait_ge(kept_stored[i], 16 * (n // 2))

        @block.scalar
        def _(act):
            for i in range(n):
                x_there(act, i)
                if i >= 2:
                    act.wait_ge(squared, i - 1)
                nc.scalar.activation(junk[:, i % 2, :], tile(i), ACT.Square, accum_out=ss[:, i:i + 1]).then_inc(squared, 1)

        @block.gpsimd
        def _(pl):
            pool.then_wait(pl, nc.gpsimd.memset(half[:, :], -0.5))
            for i in range(n):
                pl.wait_ge(squared, i + 1)
                pool.then_wait(pl, nc.gpsimd.tensor_scalar(ms[:, i:i + 1], ss[:, i:i + 1], 1.0 / D, EPS, ALU.mult, ALU.add))
                nc.gpsimd.tensor_tensor(rstd[:, i:i + 1], ms[:, i:i + 1], half[:, :], ALU.pow).then_inc(rstd_ready, 1)

        @block.vector
        def _(dve):
            def copy(i):
                _, gain, dst, at = tiles[i]
                for g in range(2):
                    dve.wait_ge(transposed, 2 * i + g + 1)
                    nc.vector.tensor_tensor(
                        dst[:, 4 * g:4 * g + 4, at:at + P],
                        c.bank((2 * i + g) % NB).rearrange("p (a b) -> p a b", a=4),
                        gain[:, 4 * g:4 * g + 4].unsqueeze(2).to_broadcast([P, 4, P]),
                        ALU.mult).then_inc(copied, 1)

            for i in range(n):
                dve.wait_ge(rstd_ready, i + 1)
                if i >= XN:
                    dve.wait_ge(transposed, 2 * (i - XN + 1))
                nc.vector.tensor_scalar(xn[:, i % XN, :], tile(i), rstd[:, i:i + 1], None, ALU.mult).then_inc(normed, 1)
                if keep is not None:
                    dve.wait_ge(normed, i + 1)
                    if i >= 2:
                        dve.wait_ge(kept_stored[i % 2], 16 * (i // 2))
                    nc.vector.tensor_tensor(kt[:, i % 2, :], xn[:, i % XN, :], keep_gain, ALU.mult).then_inc(kept, 1)
                if i:
                    copy(i - 1)
            copy(n - 1)

        @block.tensor
        def _(pe):
            for i in range(n):
                pe.wait_ge(normed, i + 1)
                for g in range(2):
                    b = 2 * i + g
                    if b >= NB:
                        pe.wait_ge(copied, b - NB + 1)
                    for k in range(4):
                        last = nc.tensor.transpose(c.bank(b % NB)[:, k * P:(k + 1) * P],
                                                   xn[:, i % XN, (4 * g + k) * P:(4 * g + k + 1) * P], c.k["ident"][:, :])
                    last.then_inc(transposed, 1)


def mm_tokens(pe, out, acts, m, w, kt=KT):
    for k in range(kt):
        last = pe.matmul(out, acts[:, k, m * P:(m + 1) * P], w[:, k, :], start=(k == 0), stop=(k == kt - 1))
    return last


def mm_channels(pe, out, acts, t0, nt, w, c0, kt=KT):
    for k in range(kt):
        last = pe.matmul(out, w[:, k, c0:c0 + P], acts[:, k, t0:t0 + nt], start=(k == 0), stop=(k == kt - 1))
    return last


def mlstm_inputs(c, hT, qk_raw, v_sb, og, if_tok):
    nc = c.nc
    PAD = M_CONV // 2
    NB = 6
    with ExitStack() as mem:
        product = c.sem(mem, "in1_product")
        copied = c.sem(mem, "in1_copied")
        block = mem.enter_context(nc.Block())

        @block.sync
        def _(sp):
            c.load_chunks(sp, C_O + 1 + RING)

        @block.tensor
        def _(pe):
            g = 0

            def fresh_bank():
                if g >= NB:
                    pe.wait_ge(copied, g - NB + 1)
                return c.bank(g % NB)

            c.wait_chunk(pe, C_QK)
            for ch in range(4):
                for th in range(2):
                    last = mm_channels(nc.tensor, fresh_bank(), hT, th * BANK, BANK, c.chunk(C_QK), ch * P)
                    last.then_inc(product, 1)
                    g += 1
            for j in (C_V, C_O):
                c.wait_chunk(pe, j)
                for m in range(TT):
                    last = mm_tokens(nc.tensor, fresh_bank(), hT, m, c.chunk(j))
                    last.then_inc(product, 1)
                    g += 1
            for m in range(TT):
                last = mm_tokens(nc.tensor, fresh_bank()[:, 0:16], hT, m, c.k["w_if"])
                last.then_inc(product, 1)
                g += 1

        @block.scalar
        def _(act):
            for g in range(32):
                act.wait_ge(product, g + 1)
                if g in (7, 15, 23):
                    act.sem_inc(c.used, 1)
                b = c.bank(g % NB)
                if g < 8:
                    dst = qk_raw[:, g // 2, PAD + (g % 2) * BANK:PAD + (g % 2 + 1) * BANK]
                elif g < 16:
                    dst, b = v_sb[:, g - 8, :, 0:M_V], b.rearrange("p (h v) -> p h v", h=M_HEADS)
                elif g < 24:
                    dst = og[:, g - 16, :]
                else:
                    dst, b = if_tok[:, g - 24, :], b[:, 0:16]
                nc.scalar.activation(dst, b, ACT.Sigmoid if 16 <= g < 24 else ACT.Copy).then_inc(copied, 1)

        @block.vector
        def _(dve):
            nc.vector.memset(qk_raw[:, :, 0:PAD], 0.0)
            nc.vector.memset(qk_raw[:, :, PAD + S:], 0.0)
            nc.vector.memset(v_sb[:, :, :, M_V:M_V + 1], 1.0)
            for m in range(TT):
                dve.wait_ge(copied, 16 + m + 1)
                nc.vector.tensor_tensor(og[:, m, :], og[:, m, :], c.k["g_mlstm"][:, :], ALU.mult)


def mlstm(c, qk_raw, qkT, v_sb, og, if_tok):
    nc = c.nc
    PAD = M_CONV // 2
    with ExitStack() as mem:
        m_row = c.sb(mem, "ml_m_row", [8, S])
        a_col = c.sb(mem, "ml_a_col", [P, TT, 8])
        em_col = c.sb(mem, "ml_em_col", [P, TT, 8])
        Pt = c.sb(mem, "ml_weights", [P, TT * (TT + 1) * P])
        r_den = c.sb(mem, "ml_den", [P, 2, 2])
        ss = c.sb(mem, "ml_ss", [P, TT * M_HEADS])
        ms = c.sb(mem, "ml_ms", [P, TT * M_HEADS])
        rstd = c.sb(mem, "ml_rstd", [P, TT * M_HEADS])
        junk = c.sb(mem, "ml_junk", [P, M_V])
        half = c.sb(mem, "ml_half", [P, 1])
        hs = qk_raw[:, :, PAD:PAD + S].rearrange("p c (t n) -> p c t n", n=BANK)

        s_dve = Steps(nc, mem, "ml_dve_steps")
        s_act = Steps(nc, mem, "ml_act_steps")
        s_pool = Steps(nc, mem, "ml_pool_steps")
        conv_done = c.sem(mem, "ml_conv_done")
        silu_done = c.sem(mem, "ml_silu_done")
        if_rows = c.sem(mem, "ml_if_rows")
        x_ready = c.sem(mem, "ml_x_ready")
        logf_ready = c.sem(mem, "ml_logf_ready")
        m_ready = c.sem(mem, "ml_m_ready")
        cols_there = c.sem(mem, "ml_cols_there")
        cols_copied = c.sem(mem, "ml_cols_copied")
        em_ready = c.sem(mem, "ml_em_ready")
        mrow_there = c.sem(mem, "ml_mrow_there")
        exp_done = c.sem(mem, "ml_exp_done")
        masked = c.sem(mem, "ml_masked")
        scores_there = c.sem(mem, "ml_scores_there")
        weighted = c.sem(mem, "ml_weighted")
        out_there = c.sem(mem, "ml_out_there")
        out_taken = c.sem(mem, "ml_out_taken")
        rstd_ready = c.sem(mem, "ml_rstd_ready")
        ss_ready = c.sem(mem, "ml_ss_ready")
        gated = c.sem(mem, "ml_gated")
        hT_there = c.sem(mem, "ml_hT_there")
        hT_copied = c.sem(mem, "ml_hT_copied")
        I, X, T1, DCUM, A, M = range(6)

        def row(i):
            return m_row[:, :] if i == M else Pt[0:8, i * S:(i + 1) * S]

        def w_at(d, j, t):
            base = j * (TT + 1) * P
            return base + t * P if d == 1 else base + (j + 1) * P + (t - j) * P

        def copy_out(dve, m):
            dve.wait_ge(hT_there, m + 1)
            nc.vector.tensor_copy(qkT[:, :, m * P:(m + 1) * P],
                                  c.bank(m % 2).rearrange("p (a b) -> p a b", a=4)).then_inc(hT_copied, 1)

        block = mem.enter_context(nc.Block())

        @block.tensor
        def _(pe):
            for f in range(2):
                for m in range(TT):
                    last = nc.tensor.transpose(c.bank(2 * f + m // 4, parts=8)[:, m % 4 * P:(m % 4 + 1) * P],
                                               if_tok[:, m, 8 * f:8 * f + 8], c.k["ident"][:, :])
            last.then_inc(if_rows, 1)
            pe.wait_ge(em_ready, 1)
            for which, r in ((0, A), (1, T1)):
                for m in range(TT):
                    last = nc.tensor.transpose(c.bank(4)[:, which * 64 + m * 8:which * 64 + m * 8 + 8],
                                               row(r)[:, m * P:(m + 1) * P], c.k["ident"][0:8, 0:8])
            last.then_inc(cols_there, 1)
            pe.wait_ge(silu_done, 4)
            for h in range(M_HEADS):
                if h:
                    pe.wait_ge(exp_done, 2 * TT * h)
                for d in range(2):
                    for th in range(2):
                        last = nc.tensor.matmul(c.bank(2 * d + th), c.k["pick8"][:, d * 4 + h, :],
                                                row(M)[:, th * BANK:(th + 1) * BANK], start=True, stop=True)
                last.then_inc(mrow_there, 1)
                hp = 64 * (h % 2)
                for j in range(TT):
                    n = h * TT + j
                    if n:
                        pe.wait_ge(weighted, 2 * n)
                    else:
                        pe.wait_ge(cols_copied, 2)
                    for th in range(2):
                        last = nc.tensor.matmul(c.bank(4 + th), qkT[hp:hp + 64, 2 + h // 2, j * P:(j + 1) * P],
                                                qkT[hp:hp + 64, h // 2, th * BANK:(th + 1) * BANK],
                                                start=True, stop=True)
                    last.then_inc(scores_there, 1)
                pe.wait_ge(weighted, 2 * TT * (h + 1))
                for t in range(TT):
                    n = h * TT + t
                    if n >= 2:
                        pe.wait_ge(out_taken, n - 1)
                    for d in range(2):
                        js = range(t + 1) if d == 0 else range(t, TT)
                        for j in js:
                            at = w_at(d, j, t)
                            last = nc.tensor.matmul(c.bank(6 + n % 2)[:, d * 256:d * 256 + M_V + 1], Pt[:, at:at + P],
                                                    v_sb[:, j, h, :], start=(j == js[0]), stop=(j == js[-1]))
                    last.then_inc(out_there, 1)
            for m in range(TT):
                pe.wait_ge(gated, m + 1)
                if m >= 2:
                    pe.wait_ge(hT_copied, m - 1)
                for k in range(4):
                    last = nc.tensor.transpose(c.bank(m % 2)[:, k * P:(k + 1) * P],
                                               hs[:, m // 2, m % 2, k * P:(k + 1) * P], c.k["ident"][:, :])
                last.then_inc(hT_there, 1)

        @block.vector
        def _(dve):
            dve.wait_ge(if_rows, 1)
            for th in range(2):
                cols = slice(th * BANK, (th + 1) * BANK)
                s_dve.done(nc.vector.tensor_scalar(row(I)[:, cols], c.bank(th, parts=8), c.k["b_if"][:, 0:1], None, ALU.add))
                ins = nc.vector.tensor_scalar(row(X)[:, cols], c.bank(2 + th, parts=8), c.k["b_if"][:, 1:2], None, ALU.add)
                s_dve.done(ins)
            s_dve.settle(dve)
            nc.vector.scalar_tensor_tensor(row(T1), row(X), -1.0, row(X), ALU.mult, ALU.max).then_inc(x_ready, 1)
            for ch in range(4):
                for i in range(M_CONV):
                    src = qk_raw[:, ch, i:i + S]
                    if i == 0:
                        ins = nc.vector.tensor_scalar(qkT[:, ch, :], src, c.k["conv1"][:, ch, 0:1], None, ALU.mult)
                    else:
                        ins = nc.vector.scalar_tensor_tensor(qkT[:, ch, :], src, c.k["conv1"][:, ch, i:i + 1],
                                                             qkT[:, ch, :], ALU.mult, ALU.add)
                    if i < M_CONV - 1:
                        s_dve.then_wait(dve, ins)
                ins.then_inc(conv_done, 1)
            dve.wait_ge(logf_ready, 1)
            s_dve.then_wait(dve, nc.vector.scalar_tensor_tensor(row(X), row(X), 0.0, row(T1), ALU.min, ALU.subtract))
            s_dve.then_wait(dve, nc.vector.tensor_tensor_scan(row(DCUM), c.k["ones"][0:8, 0:1].to_broadcast([8, S]), row(X), 0.0, ALU.mult, ALU.add))
            s_dve.then_wait(dve, nc.vector.scalar_tensor_tensor(row(DCUM), row(X), c.k["dir8"][:, 1:2], row(DCUM), ALU.mult, ALU.add))
            s_dve.then_wait(dve, nc.vector.scalar_tensor_tensor(row(A), row(DCUM), c.k["dir8"][:, 0:1], row(I), ALU.mult, ALU.add))
            s_dve.done(nc.vector.tensor_tensor_scan(row(T1), row(A), row(A), -3.0e38, ALU.max, ALU.max))
            s_dve.done(nc.vector.tensor_tensor_scan(row(X)[:, ::-1], row(A)[:, ::-1], row(A)[:, ::-1], -3.0e38, ALU.max, ALU.max))
            s_dve.settle(dve)
            s_dve.then_wait(dve, nc.vector.tensor_scalar(row(T1), row(T1), c.k["dir8"][:, 2:3], None, ALU.mult))
            s_dve.then_wait(dve, nc.vector.scalar_tensor_tensor(row(M), row(X), c.k["dir8"][:, 3:4], row(T1), ALU.mult, ALU.add))
            nc.vector.scalar_tensor_tensor(row(T1), row(DCUM), c.k["dir8"][:, 0:1], row(M), ALU.mult, ALU.subtract).then_inc(m_ready, 1)
            dve.wait_ge(cols_there, 1)
            nc.vector.tensor_copy(a_col[:, :, :], c.bank(4)[:, 0:64].rearrange("p (t c) -> p t c", c=8)).then_inc(cols_copied, 1)
            nc.vector.tensor_copy(em_col[:, :, :], c.bank(4)[:, 64:128].rearrange("p (t c) -> p t c", c=8)).then_inc(cols_copied, 1)
            for h in range(M_HEADS):
                for j in range(TT):
                    n = h * TT + j
                    dve.wait_ge(scores_there, n + 1)
                    dve.wait_ge(masked, 2 * n + 2)
                    base = j * (TT + 1) * P
                    back = Pt[:, base:base + (j + 1) * P]
                    nc.vector.scalar_tensor_tensor(
                        back, c.psum[:, 4:6, :].rearrange("p b n -> p (b n)")[:, 0:(j + 1) * P],
                        M_QK ** -0.5, back, ALU.mult, ALU.mult).then_inc(weighted, 1)
                    forth = Pt[:, base + (j + 1) * P:base + (TT + 1) * P]
                    nc.vector.scalar_tensor_tensor(
                        forth, c.psum[:, 4:6, :].rearrange("p b n -> p (b n)")[:, j * P:],
                        M_QK ** -0.5, forth, ALU.mult, ALU.mult).then_inc(weighted, 1)
                for t in range(TT):
                    n = h * TT + t
                    dve.wait_ge(out_there, n + 1)
                    o = c.bank(6 + n % 2).rearrange("p (d v) -> p d v", d=2)
                    r = r_den[:, n % 2, :]
                    ins = nc.vector.scalar_tensor_tensor(r, o[:, :, M_V], -1.0, em_col[:, t, h::4], ALU.mult, ALU.max)
                    s_dve.then_wait(dve, ins)
                    s_dve.then_wait(dve, nc.vector.tensor_tensor(r, o[:, :, M_V], r, ALU.max))
                    s_dve.then_wait(dve, nc.vector.reciprocal(r, r))
                    dst = hs[:, t // 2, t % 2, h * M_V:(h + 1) * M_V]
                    s_dve.then_wait(dve, nc.vector.tensor_scalar(dst, o[:, 0, 0:M_V], r[:, 0:1], None, ALU.mult))
                    nc.vector.scalar_tensor_tensor(dst, o[:, 1, 0:M_V], r[:, 1:2], dst, ALU.mult, ALU.add).then_inc(out_taken, 1)
            for t in range(TT):
                dve.wait_ge(rstd_ready, 1)
                for h in range(M_HEADS):
                    dst = hs[:, t // 2, t % 2, h * M_V:(h + 1) * M_V]
                    i = h * TT + t
                    ins = nc.vector.scalar_tensor_tensor(dst, dst, rstd[:, i:i + 1], og[:, t, h * M_V:(h + 1) * M_V],
                                                         ALU.mult, ALU.mult)
                ins.then_inc(gated, 1)
                if t:
                    copy_out(dve, t - 1)
            copy_out(dve, TT - 1)

        @block.scalar
        def _(act):
            act.wait_ge(x_ready, 1)
            s_act.then_wait(act, nc.scalar.activation(row(T1), row(T1), ACT.Exp, scale=-1.0))
            nc.scalar.activation(row(T1), row(T1), ACT.Ln, bias=1.0).then_inc(logf_ready, 1)
            act.wait_ge(m_ready, 1)
            nc.scalar.activation(row(T1), row(T1), ACT.Exp).then_inc(em_ready, 1)
            for ch in range(4):
                act.wait_ge(conv_done, ch + 1)
                nc.scalar.activation(qkT[:, ch, :], qkT[:, ch, :], ACT.Silu, bias=c.k["conv1_b"][:, ch:ch + 1]).then_inc(silu_done, 1)
            act.wait_ge(cols_copied, 1)
            for h in range(M_HEADS):
                act.wait_ge(mrow_there, h + 1)
                if h:
                    act.wait_ge(out_taken, TT * h)
                for j in range(TT):
                    base = j * (TT + 1) * P
                    for d, at, lo, hi in ((1, base, 0, (j + 1) * P), (0, base + (j + 1) * P, j * P, S)):
                        nc.scalar.activation(
                            Pt[:, at:at + hi - lo],
                            c.psum[:, 2 * d:2 * d + 2, :].rearrange("p b n -> p (b n)")[:, lo:hi],
                            ACT.Exp, bias=a_col[:, j, d * 4 + h:d * 4 + h + 1], scale=-1.0).then_inc(exp_done, 1)
            for t in range(TT):
                for h in range(M_HEADS):
                    i = h * TT + t
                    act.wait_ge(out_taken, i + 1)
                    s_act.settle(act)
                    s_act.done(nc.scalar.activation(junk[:, :], hs[:, t // 2, t % 2, h * M_V:(h + 1) * M_V], ACT.Square,
                                         accum_out=ss[:, i:i + 1]))
            s_act.settle(act)
            nc.scalar.activation(ms[:, :], ss[:, :], ACT.Copy, scale=1.0 / M_V).then_inc(ss_ready, 1)

        @block.gpsimd
        def _(pl):
            s_pool.then_wait(pl, nc.gpsimd.memset(half[:, :], -0.5))
            for h in range(M_HEADS):
                for j in range(TT):
                    n = h * TT + j
                    pl.wait_ge(exp_done, 2 * n + 1)
                    at = w_at(1, j, j)
                    nc.gpsimd.affine_select(out=Pt[:, at:at + P], in_=Pt[:, at:at + P], compare_op=ALU.is_ge, fill=0.0,
                                            base=0, pattern=[[-1, P]], channel_multiplier=1).then_inc(masked, 1)
                    pl.wait_ge(exp_done, 2 * n + 2)
                    at = w_at(0, j, j)
                    nc.gpsimd.affine_select(out=Pt[:, at:at + P], in_=Pt[:, at:at + P], compare_op=ALU.is_ge, fill=0.0,
                                            base=0, pattern=[[1, P]], channel_multiplier=-1).then_inc(masked, 1)
            pl.wait_ge(ss_ready, 1)
            s_pool.then_wait(pl, nc.gpsimd.tensor_scalar(ms[:, :], ms[:, :], EPS, None, ALU.add))
            nc.gpsimd.tensor_tensor(rstd[:, :], ms[:, :], half[:, :].to_broadcast([P, TT * M_HEADS]), ALU.pow).then_inc(rstd_ready, 1)


def attention_inputs(c, hT, memT, naT, v_na, qmT, kmT, v_mem):
    nc = c.nc
    units = [(C_NAQK, hT, m, 512, NA_HD, naT, 0) for m in range(TT)]
    units += [(C_NAV, hT, m, 256, MEM_HD, qmT, 4) for m in range(TT)]
    units += [(C_MEMKV, memT, m, 256, MEM_HD, kmT, 6) for m in range(MEM // P)]
    n = len(units)
    NB, NR, G = 4, 3, 512 // NA_HD
    with ExitStack() as mem:
        raw = c.sb(mem, "at_raw", [P, NR, BANK])
        sq = c.sb(mem, "at_squares", [P, NR, BANK])
        ss = c.sb(mem, "at_ss", [P, n, G])
        ms = c.sb(mem, "at_ms", [P, n, G])
        rstd = c.sb(mem, "at_rstd", [P, n, G])
        half = c.sb(mem, "at_half", [P, 1])
        pool = Steps(nc, mem, "at_pool_steps")
        product = c.sem(mem, "at_product")
        taken = c.sem(mem, "at_taken")
        summed = c.sem(mem, "at_summed")
        rstd_ready = c.sem(mem, "at_rstd_ready")
        normed = c.sem(mem, "at_normed")
        turned = c.sem(mem, "at_turned")
        turned_copied = c.sem(mem, "at_turned_copied")
        block = mem.enter_context(nc.Block())

        @block.sync
        def _(sp):
            c.load_chunks(sp, C_MEMKV + 1 + RING)

        @block.tensor
        def _(pe):
            def turn(i):
                w = units[i][3]
                pe.wait_ge(normed, i + 1)
                if i >= 2:
                    pe.wait_ge(turned_copied, i - 1)
                for k in range(w // P):
                    last = nc.tensor.transpose(c.bank(NB + i % 2)[:, k * P:(k + 1) * P],
                                               raw[:, i % NR, k * P:(k + 1) * P], c.k["ident"][:, :])
                last.then_inc(turned, 1)

            for i, (j, acts, m, *_) in enumerate(units):
                if m == 0:
                    c.wait_chunk(pe, j)
                if i >= NB:
                    pe.wait_ge(taken, i - NB + 1)
                mm_tokens(nc.tensor, c.bank(i % NB), acts, m, c.chunk(j)).then_inc(product, 1)
                if i >= 2:
                    turn(i - 2)
            turn(n - 2)
            turn(n - 1)

        @block.scalar
        def _(act):
            for i, (j, _, m, w, *_) in enumerate(units):
                act.wait_ge(product, i + 1)
                if i + 1 == n or units[i + 1][0] != j:
                    act.sem_inc(c.used, 1)
                if i >= NR:
                    act.wait_ge(turned, i - NR + 1)
                b = c.bank(i % NB)
                part = b[:, 0:w] if j != C_NAV else b[:, 256:512]
                nc.scalar.activation(raw[:, i % NR, 0:w], part, ACT.Copy)
                if j == C_NAV:
                    nc.scalar.activation(v_na[:, m, :], b[:, 0:256], ACT.Copy)
                if j == C_MEMKV:
                    nc.scalar.activation(v_mem[:, m, :], b[:, 256:512], ACT.Copy)
                nc.scalar.activation(sq[:, i % NR, 0:w], part, ACT.Square).then_inc(taken, 1)

        @block.gpsimd
        def _(pl):
            pool.then_wait(pl, nc.gpsimd.memset(half[:, :], -0.5))
            for i, (_, _, _, w, hd, *_) in enumerate(units):
                g = w // hd
                pl.wait_ge(summed, i + 1)
                pool.then_wait(pl, nc.gpsimd.tensor_scalar(ms[:, i, 0:g], ss[:, i, 0:g], 1.0 / hd, EPS, ALU.mult, ALU.add))
                nc.gpsimd.tensor_tensor(rstd[:, i, 0:g], ms[:, i, 0:g], half[:, :].to_broadcast([P, g]), ALU.pow).then_inc(rstd_ready, 1)

        @block.vector
        def _(dve):
            def copy(i):
                _, _, m, w, _, dst, gain = units[i]
                dve.wait_ge(turned, i + 1)
                nb = w // P
                nc.vector.tensor_tensor(dst[:, 0:nb, m * P:(m + 1) * P],
                                        c.bank(NB + i % 2)[:, 0:w].rearrange("p (a b) -> p a b", a=nb),
                                        c.k["g_heads"][:, gain:gain + nb].unsqueeze(2).to_broadcast([P, nb, P]),
                                        ALU.mult).then_inc(turned_copied, 1)

            for i, (j, _, m, w, hd, *_) in enumerate(units):
                g = w // hd
                dve.wait_ge(taken, i + 1)
                nc.vector.tensor_reduce(ss[:, i, 0:g], sq[:, i % NR, 0:w].rearrange("p (g d) -> p g d", d=hd),
                                        AX.X, ALU.add).then_inc(summed, 1)
                if i >= 2:
                    copy(i - 2)
                dve.wait_ge(rstd_ready, i + 1)
                for lo, hi, q in ((0, 256, j != C_MEMKV), (256, 512, False)):
                    if lo < w:
                        v = raw[:, i % NR, lo:hi].rearrange("p (g d) -> p g d", d=hd)
                        r = rstd[:, i, lo // hd:hi // hd].unsqueeze(2).to_broadcast([P, 256 // hd, hd])
                        ins = nc.vector.scalar_tensor_tensor(v, v, hd ** -0.5 if q else 1.0, r, ALU.mult, ALU.mult)
                ins.then_inc(normed, 1)
            copy(n - 2)
            copy(n - 1)


def window_tiles(t):
    rows_n = S // GRID_W
    lo = min(max(2 * t - WIN_R // 2, 0), rows_n - WIN_R)
    hi = min(max(2 * t + 1 - WIN_R // 2, 0), rows_n - WIN_R) + WIN_R
    return lo // 2, (hi + 1) // 2


NA_WIDE = 5 * P
NA_EDGE = [0, 1, TT - 2, TT - 1]
NA_TABLE = NA_WIDE + len(NA_EDGE) * 4 * P


def bias_at(t):
    return NA_WIDE + NA_EDGE.index(t) * 4 * P if t in NA_EDGE else 0


def neighbourhood(c, naT, v_na, h_tok):
    nc = c.nc
    units = [(h, t) for h in range(NA_HEADS) for t in range(TT)]
    n = len(units)
    NS = 3
    with ExitStack() as mem:
        bias = c.sb(mem, "na_bias", [P, 2, NA_TABLE])
        sc = c.sb(mem, "na_scores", [P, NS, NA_WIDE])
        pT = c.sb(mem, "na_pT", [P, 2, NA_WIDE])
        mx = c.sb(mem, "na_max", [P, n])
        nmx = c.sb(mem, "na_negmax", [P, n])
        den = c.sb(mem, "na_den", [P, n])
        rden = c.sb(mem, "na_rden", [P, n])
        bias_there = [c.sem(mem, f"na_bias_there_{i}") for i in range(2)]
        scores = c.sem(mem, "na_scores_there")
        biased = c.sem(mem, "na_biased")
        max_ready = c.sem(mem, "na_max_ready")
        exp_done = c.sem(mem, "na_exp_done")
        turned = c.sem(mem, "na_turned")
        turned_copied = c.sem(mem, "na_turned_copied")
        out_there = c.sem(mem, "na_out_there")
        rden_ready = c.sem(mem, "na_rden_ready")
        out_taken = c.sem(mem, "na_out_taken")
        block = mem.enter_context(nc.Block())

        def pair(i):
            return c.psum[:, 2 * i:2 * i + 2, :].rearrange("p b n -> p (b n)")

        @block.sync
        def _(sp):
            for h in range(NA_HEADS):
                if h >= 2:
                    sp.wait_ge(biased, TT * (h - 1))
                sp.dma_start(bias[:, h % 2, :], c.io["na_bias"][h]).then_inc(bias_there[h % 2], 16)

        @block.tensor
        def _(pe):
            def score(i):
                h, t = units[i]
                k0, k1 = window_tiles(t)
                hp = NA_HD * (h % 4)
                if i >= 2:
                    pe.wait_ge(biased, i - 1)
                keys = (k1 - k0) * P
                for lo in range(0, keys, BANK):
                    hi = min(lo + BANK, keys)
                    last = nc.tensor.matmul(pair(i % 2)[:, lo:hi], naT[hp:hp + NA_HD, h // 4, t * P:(t + 1) * P],
                                            naT[hp:hp + NA_HD, 2 + h // 4, k0 * P + lo:k0 * P + hi], start=True, stop=True,
                                            tile_position=(hp, 0))
                last.then_inc(scores, 1)

            def turn(i):
                h, t = units[i]
                k0, k1 = window_tiles(t)
                pe.wait_ge(exp_done, i + 1)
                if i >= 2:
                    pe.wait_ge(out_taken, i - 1)
                for k in range(k1 - k0):
                    last = nc.tensor.transpose(pair(2 + i % 2)[:, k * P:(k + 1) * P], sc[:, i % NS, k * P:(k + 1) * P], c.k["ident"][:, :])
                last.then_inc(turned, 1)

            def values(i):
                h, t = units[i]
                k0, k1 = window_tiles(t)
                pe.wait_ge(turned_copied, i + 1)
                for k in range(k1 - k0):
                    last = nc.tensor.matmul(pair(2 + i % 2)[:, 768:768 + NA_HD], pT[:, i % 2, k * P:(k + 1) * P],
                                            v_na[:, k0 + k, h * NA_HD:(h + 1) * NA_HD], start=(k == 0), stop=(k == k1 - k0 - 1))
                last.then_inc(out_there, 1)

            for i in range(n + 2):
                if i < n:
                    score(i)
                if 1 <= i <= n:
                    turn(i - 1)
                if i >= 2:
                    values(i - 2)

        @block.vector
        def _(dve):
            def finish(i):
                h, t = units[i]
                dve.wait_ge(exp_done, i + 1)
                nc.vector.reciprocal(rden[:, i:i + 1], den[:, i:i + 1]).then_inc(rden_ready, 1)
                dve.wait_ge(rden_ready, i + 1)
                dve.wait_ge(out_there, i + 1)
                nc.vector.tensor_scalar(h_tok[:, t, h * NA_HD:(h + 1) * NA_HD], pair(2 + i % 2)[:, 768:768 + NA_HD],
                                        rden[:, i:i + 1], None, ALU.mult).then_inc(out_taken, 1)

            for i, (h, t) in enumerate(units):
                k0, k1 = window_tiles(t)
                w, at = (k1 - k0) * P, bias_at(t)
                if t == 0:
                    dve.wait_ge(bias_there[h % 2], 16 * (h // 2 + 1))
                dve.wait_ge(scores, i + 1)
                if i >= NS:
                    dve.wait_ge(turned, i - NS + 1)
                nc.vector.tensor_tensor_reduce(sc[:, i % NS, 0:w], pair(i % 2)[:, 0:w], bias[:, h % 2, at:at + w],
                                               1.0, -3.0e38, ALU.add, ALU.max, mx[:, i:i + 1]).then_inc(biased, 1)
                dve.wait_ge(biased, i + 1)
                nc.vector.tensor_scalar(nmx[:, i:i + 1], mx[:, i:i + 1], -1.0, None, ALU.mult).then_inc(max_ready, 1)
                if i >= 3:
                    finish(i - 3)
            for i in range(n - 3, n):
                finish(i)

        @block.scalar
        def _(act):
            def copy(i):
                k0, k1 = window_tiles(units[i][1])
                w = (k1 - k0) * P
                act.wait_ge(turned, i + 1)
                if i >= 2:
                    act.wait_ge(out_there, i - 1)
                nc.scalar.activation(pT[:, i % 2, 0:w], pair(2 + i % 2)[:, 0:w], ACT.Copy).then_inc(turned_copied, 1)

            for i, (h, t) in enumerate(units):
                k0, k1 = window_tiles(t)
                w = (k1 - k0) * P
                act.wait_ge(max_ready, i + 1)
                nc.scalar.activation(sc[:, i % NS, 0:w], sc[:, i % NS, 0:w], ACT.Exp, bias=nmx[:, i:i + 1],
                                     accum_out=den[:, i:i + 1]).then_inc(exp_done, 1)
                if i:
                    copy(i - 1)
            copy(n - 1)


def memory_attention(c, qmT, kmT, v_mem, h_tok):
    nc = c.nc
    MK = MEM // P
    with ExitStack() as mem:
        pr = c.sb(mem, "me_p", [P, 2, MEM_HEADS, MEM])
        pT = c.sb(mem, "me_pT", [P, 2, MEM_HEADS * MEM])
        nmx = c.sb(mem, "me_negmax", [P, TT, MEM_HEADS])
        den = c.sb(mem, "me_den", [P, TT, MEM_HEADS])
        rden = c.sb(mem, "me_rden", [P, TT, MEM_HEADS])
        scores = c.sem(mem, "me_scores_there")
        max_ready = c.sem(mem, "me_max_ready")
        exp_done = c.sem(mem, "me_exp_done")
        turned = c.sem(mem, "me_turned")
        turned_copied = c.sem(mem, "me_turned_copied")
        out_there = c.sem(mem, "me_out_there")
        rden_ready = c.sem(mem, "me_rden_ready")
        out_taken = c.sem(mem, "me_out_taken")
        block = mem.enter_context(nc.Block())

        def pair(i):
            return c.psum[:, 2 * i:2 * i + 2, :].rearrange("p b n -> p (b n)")

        def slot(h):
            return 2 * (h % 2) + h // 2

        @block.tensor
        def _(pe):
            for i in range(TT + 1):
                if i < TT:
                    if i >= 2:
                        pe.wait_ge(exp_done, MEM_HEADS * (i - 1))
                    for h in range(MEM_HEADS):
                        hp = MEM_HD * (h % 2)
                        last = nc.tensor.matmul(pair(i % 2)[:, slot(h) * MEM:(slot(h) + 1) * MEM], qmT[hp:hp + MEM_HD, h // 2, i * P:(i + 1) * P],
                                                kmT[hp:hp + MEM_HD, h // 2, :], start=True, stop=True)
                    last.then_inc(scores, 1)
                if i:
                    u = i - 1
                    pe.wait_ge(exp_done, MEM_HEADS * i)
                    if u:
                        pe.wait_ge(turned_copied, u)
                    for h in range(MEM_HEADS):
                        for k in range(MK):
                            at = (h * MK + k) * P
                            last = nc.tensor.transpose(pair(2)[:, at:at + P], pr[:, u % 2, h, k * P:(k + 1) * P], c.k["ident"][:, :])
                    last.then_inc(turned, 1)
                    pe.wait_ge(turned_copied, u + 1)
                    if u >= 2:
                        pe.wait_ge(out_taken, u - 1)
                    for h in range(MEM_HEADS):
                        for k in range(MK):
                            at = (h * MK + k) * P
                            last = nc.tensor.matmul(c.bank(6 + u % 2)[:, h * MEM_HD:(h + 1) * MEM_HD], pT[:, u % 2, at:at + P],
                                                    v_mem[:, k, h * MEM_HD:(h + 1) * MEM_HD], start=(k == 0), stop=(k == MK - 1))
                    last.then_inc(out_there, 1)

        @block.vector
        def _(dve):
            for i in range(TT + 1):
                if i < TT:
                    dve.wait_ge(scores, i + 1)
                    nc.vector.tensor_reduce(nmx[:, i, :], pair(i % 2).rearrange("p (h k) -> p h k", k=MEM), AX.X, ALU.max,
                                            negate=True).then_inc(max_ready, 1)
                if i:
                    u = i - 1
                    dve.wait_ge(exp_done, MEM_HEADS * i)
                    nc.vector.reciprocal(rden[:, u, :], den[:, u, :]).then_inc(rden_ready, 1)
                    dve.wait_ge(rden_ready, i)
                    dve.wait_ge(out_there, i)
                    nc.vector.tensor_tensor(h_tok[:, u, :].rearrange("p (h d) -> p h d", d=MEM_HD),
                                            c.bank(6 + u % 2)[:, 0:256].rearrange("p (h d) -> p h d", d=MEM_HD),
                                            rden[:, u, :].unsqueeze(2).to_broadcast([P, MEM_HEADS, MEM_HD]),
                                            ALU.mult).then_inc(out_taken, 1)

        @block.scalar
        def _(act):
            for i in range(TT + 1):
                if i < TT:
                    act.wait_ge(max_ready, i + 1)
                    if i >= 2:
                        act.wait_ge(turned, i - 1)
                    for h in range(MEM_HEADS):
                        nc.scalar.activation(pr[:, i % 2, h, :], pair(i % 2)[:, slot(h) * MEM:(slot(h) + 1) * MEM], ACT.Exp,
                                             bias=nmx[:, i, slot(h):slot(h) + 1],
                                             accum_out=den[:, i, h:h + 1]).then_inc(exp_done, 1)
                if i:
                    u = i - 1
                    act.wait_ge(turned, i)
                    if u >= 2:
                        act.wait_ge(out_there, u - 1)
                    nc.scalar.activation(pT[:, u % 2, :], pair(2), ACT.Copy).then_inc(turned_copied, 1)


def transpose_tokens(c, name, pairs):
    nc = c.nc
    units = [(src, dst, m, w) for src, dst, w in pairs for m in range(TT)]
    NB = 4
    with ExitStack() as mem:
        turned = c.sem(mem, name + "_turned")
        copied = c.sem(mem, name + "_copied")
        block = mem.enter_context(nc.Block())

        @block.tensor
        def _(pe):
            for i, (src, dst, m, w) in enumerate(units):
                if i >= NB:
                    pe.wait_ge(copied, i - NB + 1)
                for k in range(w // P):
                    last = nc.tensor.transpose(c.bank(i % NB)[:, k * P:(k + 1) * P], src[:, m, k * P:(k + 1) * P], c.k["ident"][:, :])
                last.then_inc(turned, 1)

        @block.vector
        def _(dve):
            for i, (src, dst, m, w) in enumerate(units):
                dve.wait_ge(turned, i + 1)
                nc.vector.tensor_copy(dst[:, 0:w // P, m * P:(m + 1) * P],
                                      c.bank(i % NB)[:, 0:w].rearrange("p (a b) -> p a b", b=P)).then_inc(copied, 1)


def gated_branches(c, hT, branches, yT):
    nc = c.nc
    parts = [(n, b, ch, th) for n in range(2) for b in range(3) for ch in range(4) for th in range(2)]
    NB = 4
    with ExitStack() as mem:
        pw = c.sb(mem, "br_proj", [P, 2, 4, BANK])
        gate = c.sb(mem, "br_gate", [P, 3, BANK])
        prod = c.sb(mem, "br_product", [P, 2, BANK])
        pw_there = [c.sem(mem, f"br_proj_there_{i}") for i in range(2)]
        gate_there = c.sem(mem, "br_gate_there")
        proj_there = c.sem(mem, "br_proj_out_there")
        gate_done = c.sem(mem, "br_gate_done")
        multiplied = c.sem(mem, "br_multiplied")
        added = c.sem(mem, "br_added")
        block = mem.enter_context(nc.Block())

        @block.sync
        def _(sp):
            for i in range(6):
                n, b = i // 3, i % 3
                w = branches[b][1]
                if i >= 2:
                    sp.wait_ge(multiplied, 8 * (i - 1))
                sp.dma_start(pw[:, i % 2, 0:w.shape[0] // P, :],
                             w[:, n * BANK:(n + 1) * BANK].rearrange("(k p) n -> p k n", p=P)).then_inc(pw_there[i % 2], 16)
                c.load_chunks(sp, C_BRANCH + i + RING)
            c.load_chunks(sp, C_OUT + RING)

        @block.tensor
        def _(pe):
            for i, (n, b, ch, th) in enumerate(parts):
                q = i // 8
                if i % 8 == 0:
                    c.wait_chunk(pe, C_BRANCH + q)
                    pe.wait_ge(pw_there[q % 2], 16 * (q // 2 + 1))
                if i >= NB:
                    pe.wait_ge(multiplied, i - NB + 1)
                mm_channels(nc.tensor, c.bank(i % NB), hT, th * BANK, BANK, c.chunk(C_BRANCH + q), ch * P).then_inc(gate_there, 1)
                acts, w = branches[b]
                mm_channels(nc.tensor, c.bank(NB + i % NB), acts, th * BANK, BANK, pw[:, q % 2, :, :], ch * P,
                            kt=w.shape[0] // P).then_inc(proj_there, 1)

        @block.scalar
        def _(act):
            for i in range(len(parts)):
                act.wait_ge(gate_there, i + 1)
                if i % 8 == 7:
                    act.sem_inc(c.used, 1)
                if i >= 3:
                    act.wait_ge(multiplied, i - 2)
                nc.scalar.activation(gate[:, i % 3, :], c.bank(i % NB), ACT.Sigmoid).then_inc(gate_done, 1)

        @block.vector
        def _(dve):
            n_added = 0
            for i, (n, b, ch, th) in enumerate(parts):
                y = yT[:, 4 * n + ch, th * BANK:(th + 1) * BANK]
                dve.wait_ge(gate_done, i + 1)
                dve.wait_ge(proj_there, i + 1)
                dst = y if b == 0 else prod[:, i % 2, :]
                if n_added >= 2:
                    dve.wait_ge(added, n_added - 1)
                nc.vector.tensor_tensor(dst, gate[:, i % 3, :], c.bank(NB + i % NB), ALU.mult).then_inc(multiplied, 1)
                if b:
                    dve.wait_ge(multiplied, i + 1)
                    nc.vector.tensor_tensor(y, y, prod[:, i % 2, :], ALU.add).then_inc(added, 1)
                    n_added += 1


def project_add(c, name, acts, j0, x_sb, first_load=None):
    nc = c.nc
    NB = 4
    with ExitStack() as mem:
        product = c.sem(mem, name + "_product")
        added = c.sem(mem, name + "_added")
        x_there = c.sem(mem, name + "_x_there")
        block = mem.enter_context(nc.Block())

        @block.sync
        def _(sp):
            if first_load is not None:
                sp.dma_start(x_sb[:, :, :], first_load.rearrange("(t p) n -> p t n", p=P)).then_inc(x_there, 16)
            c.load_chunks(sp, j0 + 2 + RING)

        @block.tensor
        def _(pe):
            for i in range(2 * TT):
                n, m = i // TT, i % TT
                if m == 0:
                    c.wait_chunk(pe, j0 + n)
                if i >= NB:
                    pe.wait_ge(added, i - NB + 1)
                mm_tokens(nc.tensor, c.bank(i % NB), acts, m, c.chunk(j0 + n)).then_inc(product, 1)

        @block.vector
        def _(dve):
            if first_load is not None:
                dve.wait_ge(x_there, 16)
            for i in range(2 * TT):
                n, m = i // TT, i % TT
                dve.wait_ge(product, i + 1)
                if m == TT - 1:
                    dve.sem_inc(c.used, 1)
                x = x_sb[:, m, n * BANK:(n + 1) * BANK]
                nc.vector.tensor_tensor(x, x, c.bank(i % NB), ALU.add).then_inc(added, 1)


def ffn(c, hT, x_sb, uT):
    nc = c.nc
    NB = 6
    with ExitStack() as mem:
        r = c.sb(mem, "ff_relu", [P, 3, BANK])
        product = c.sem(mem, "ff_product")
        relu_done = c.sem(mem, "ff_relu_done")
        squared = c.sem(mem, "ff_squared")
        added = c.sem(mem, "ff_added")
        block = mem.enter_context(nc.Block())
        QUARTERS = D_FF // D

        @block.sync
        def _(sp):
            c.load_chunks(sp, C_FFN + 4 * QUARTERS + RING)

        @block.tensor
        def _(pe):
            for f in range(QUARTERS):
                for i in range(32):
                    g = 32 * f + i
                    j = C_FFN + 4 * f + i // 8
                    if i % 8 == 0:
                        c.wait_chunk(pe, j)
                    if g >= NB:
                        q, k = divmod(g - NB, 32)
                        if k < 16:
                            pe.wait_ge(relu_done, 16 * q + k + 1)
                        else:
                            pe.wait_ge(added, 16 * q + k - 16 + 1)
                    if i == 16:
                        pe.wait_ge(squared, 16 * (f + 1))
                    if i < 16:
                        ins = mm_channels(nc.tensor, c.bank(g % NB), hT, (i % 2) * BANK, BANK, c.chunk(j), (i // 2 % 4) * P)
                    else:
                        ins = mm_tokens(nc.tensor, c.bank(g % NB), uT, i % 8, c.chunk(j))
                    ins.then_inc(product, 1)

        @block.scalar
        def _(act):
            for f in range(QUARTERS):
                for i in range(16):
                    g, u = 32 * f + i, 16 * f + i
                    act.wait_ge(product, g + 1)
                    if i % 8 == 7:
                        act.sem_inc(c.used, 1)
                    if u >= 3:
                        act.wait_ge(squared, u - 2)
                    nc.scalar.activation(r[:, u % 3, :], c.bank(g % NB), ACT.Relu).then_inc(relu_done, 1)

        @block.vector
        def _(dve):
            for f in range(QUARTERS):
                for i in range(16):
                    u = 16 * f + i
                    dve.wait_ge(relu_done, u + 1)
                    nc.vector.tensor_tensor(uT[:, i // 2, (i % 2) * BANK:(i % 2 + 1) * BANK], r[:, u % 3, :], r[:, u % 3, :],
                                            ALU.mult).then_inc(squared, 1)
                for i in range(16):
                    g, u = 32 * f + 16 + i, 16 * f + i
                    dve.wait_ge(product, g + 1)
                    if i % 8 == 7:
                        dve.sem_inc(c.used, 1)
                    x = x_sb[:, i % 8, (i // 8) * BANK:(i // 8 + 1) * BANK]
                    if u >= 16:
                        dve.wait_ge(added, u - 15)
                    nc.vector.tensor_tensor(x, x, c.bank(g % NB), ALU.add).then_inc(added, 1)


def spill(c, name, sb_ap, dram, clear, cleared):
    nc = c.nc
    with ExitStack() as mem:
        stored = c.sem(mem, name + "_stored")
        block = mem.enter_context(nc.Block())

        @block.sync
        def _(sp):
            sp.dma_start(dram.rearrange("(t p) n -> p t n", p=P), sb_ap).then_inc(stored, 16)
            sp.dma_start(clear.rearrange("(p t) (a n) -> p (t a) n", p=P, n=256),
                         c.k["zeros"][:, :].unsqueeze(1).to_broadcast([P, clear.shape[0] // P * D // 256, 256])).then_inc(cleared, 16)
            sp.wait_ge(stored, 16)


def delta_inputs(c, hT, qkv, gate, small, ss):
    nc = c.nc
    PAD = A_CONV_K - 1
    NCH = 12
    with ExitStack() as mem:
        raw = c.sb(mem, "di_raw", [P, 2, PAD + S])
        cv = c.sb(mem, "di_conv", [P, 2, S])
        zeroed = c.sem(mem, "di_zeroed")
        product = c.sem(mem, "di_product")
        copied = c.sem(mem, "di_copied")
        tap = Steps(nc, mem, "di_taps")
        conv_done = c.sem(mem, "di_conv_done")
        silu_done = c.sem(mem, "di_silu_done")
        turned = c.sem(mem, "di_turned")
        turned_copied = c.sem(mem, "di_turned_copied")
        squared = c.sem(mem, "di_squared")
        junk = c.sb(mem, "di_junk", [P, G_DIM])
        block = mem.enter_context(nc.Block())
        NB = 4

        @block.sync
        def _(sp):
            c.load_chunks(sp, C_IN2 + 4 + RING)

        @block.tensor
        def _(pe):
            def turn(ch):
                pe.wait_ge(silu_done, ch + 1)
                for g in range(2):
                    b = 2 * ch + g
                    if b >= 4:
                        pe.wait_ge(turned_copied, b - 3)
                    for k in range(4):
                        last = nc.tensor.transpose(c.bank(NB + b % 4)[:, k * P:(k + 1) * P],
                                                   cv[:, ch % 2, (4 * g + k) * P:(4 * g + k + 1) * P], c.k["ident"][:, :])
                    last.then_inc(turned, 1)

            g = 0
            for ch in range(NCH):
                if ch % 4 == 0:
                    c.wait_chunk(pe, C_IN2 + ch // 4)
                for th in range(2):
                    if g >= NB:
                        pe.wait_ge(copied, g - NB + 1)
                    mm_channels(nc.tensor, c.bank(g % NB), hT, th * BANK, BANK, c.chunk(C_IN2 + ch // 4), ch % 4 * P).then_inc(product, 1)
                    g += 1
                if ch:
                    turn(ch - 1)
            c.wait_chunk(pe, C_IN2 + 3)
            for m in range(TT):
                pe.wait_ge(copied, g - NB + 1)
                mm_tokens(nc.tensor, c.bank(g % NB), hT, m, c.chunk(C_IN2 + 3)).then_inc(product, 1)
                g += 1
                if m == 0:
                    turn(NCH - 1)
            for m in range(TT):
                pe.wait_ge(copied, g - NB + 1)
                mm_tokens(nc.tensor, c.bank(g % NB)[:, 0:8], hT, m, c.k["w_ba"]).then_inc(product, 1)
                g += 1

        @block.scalar
        def _(act):
            act.wait_ge(zeroed, 1)

            def squares(ch):
                for g in range(2):
                    b = 2 * ch + g
                    act.wait_ge(turned_copied, b + 1)
                    for k in range(4):
                        if 4 * b + k:
                            act.wait_ge(squared, 4 * b + k)
                        nc.scalar.activation(junk[:, :], qkv[:, 4 * g + k, ch * P:(ch + 1) * P], ACT.Square,
                                             accum_out=ss[:, 4 * g + k, ch:ch + 1]).then_inc(squared, 1)

            def silu(ch):
                act.wait_ge(conv_done, ch + 1)
                nc.scalar.activation(cv[:, ch % 2, :], cv[:, ch % 2, :], ACT.Silu).then_inc(silu_done, 1)

            for ch in range(NCH):
                for th in range(2):
                    g = 2 * ch + th
                    act.wait_ge(product, g + 1)
                    if g % 8 == 7:
                        act.sem_inc(c.used, 1)
                    if ch >= 2 and th == 0:
                        act.wait_ge(conv_done, ch - 1)
                    nc.scalar.activation(raw[:, ch % 2, PAD + th * BANK:PAD + (th + 1) * BANK], c.bank(g % NB), ACT.Copy).then_inc(copied, 1)
                if ch:
                    silu(ch - 1)
                if 2 <= ch < 10:
                    squares(ch - 2)
            silu(NCH - 1)
            for m in range(TT):
                g = 2 * NCH + m
                act.wait_ge(product, g + 1)
                if m == TT - 1:
                    act.sem_inc(c.used, 1)
                nc.scalar.activation(gate[:, m, :], c.bank(g % NB), ACT.Silu).then_inc(copied, 1)
            for m in range(TT):
                g = 2 * NCH + TT + m
                act.wait_ge(product, g + 1)
                nc.scalar.activation(small[:, m, :], c.bank(g % NB)[:, 0:8], ACT.Copy).then_inc(copied, 1)

        @block.vector
        def _(dve):
            nc.vector.memset(raw[:, :, 0:PAD], 0.0).then_inc(zeroed, 1)
            dve.wait_ge(zeroed, 1)

            def copy(ch):
                for g in range(2):
                    b = 2 * ch + g
                    dve.wait_ge(turned, b + 1)
                    nc.vector.tensor_copy(qkv[:, 4 * g:4 * g + 4, ch * P:(ch + 1) * P],
                                          c.bank(NB + b % 4).rearrange("p (a b) -> p a b", a=4)).then_inc(turned_copied, 1)

            for ch in range(NCH):
                dve.wait_ge(copied, 2 * ch + 2)
                if ch >= 2:
                    dve.wait_ge(turned, 2 * (ch - 1))
                dst = cv[:, ch % 2, :]
                for i in range(A_CONV_K):
                    src = raw[:, ch % 2, i:i + S]
                    w = c.k["conv2"][:, ch, i:i + 1]
                    if i == 0:
                        ins = nc.vector.tensor_scalar(dst, src, w, None, ALU.mult)
                    else:
                        ins = nc.vector.scalar_tensor_tensor(dst, src, w, dst, ALU.mult, ALU.add)
                    if i < A_CONV_K - 1:
                        tap.then_wait(dve, ins)
                ins.then_inc(conv_done, 1)
                if ch:
                    copy(ch - 1)
            copy(NCH - 1)
            for m in range(TT):
                dve.wait_ge(copied, 2 * NCH + m + 1)
                v = gate[:, m, :].rearrange("p (h d) -> p h d", d=P)
                nc.vector.tensor_tensor(v, v, c.k["norm_a"][:, :].unsqueeze(1).to_broadcast([P, 4, P]), ALU.mult)


def heads(ap):
    return ap.rearrange("p (h d) -> p h d", d=G_DIM)


def per_head(col):
    return col.unsqueeze(2).to_broadcast([P, 4, G_DIM])


def same_for_heads(ap):
    return ap.unsqueeze(1).to_broadcast([P, 4, G_DIM])


def head(ap, h):
    return ap[:, h * G_DIM:(h + 1) * G_DIM]


LEVELS = 7
GROUPS = 2
GW = 2 * G_DIM


def delta_rule(c, qkv, o, small, ss, scratch):
    nc = c.nc
    H, C = A_HEADS, TT
    with ExitStack() as mem:
        def tile(name):
            return c.sb(mem, "dr_" + name, [P, BANK])[:, :]

        kT, qT, kbT, qdT, kb, kbg, kdec, state = (tile(n) for n in ("kT", "qT", "kbT", "qdT", "kb", "kbg", "kdec", "state"))
        qd, decT, attnT, AT, M, X, T, U = (scratch[:, i, :] for i in range(8))
        gmask = qd
        wTn, vnew = kT, kbT
        rs = c.sb(mem, "dr_rs", [P, C, 8])
        half = c.sb(mem, "dr_half", [P, 1])
        beta = c.sb(mem, "dr_beta", [P, C, H])
        g = c.sb(mem, "dr_g", [P, C, H])
        t1 = c.sb(mem, "dr_t1", [P, C, H])
        t2 = c.sb(mem, "dr_t2", [P, C, H])
        ea = c.sb(mem, "dr_ea", [P, H])
        eg = c.sb(mem, "dr_eg", [P, 3, C, H])
        oss = c.sb(mem, "dr_oss", [P, C, H])
        ors = c.sb(mem, "dr_ors", [P, C, H])
        junk = c.sb(mem, "dr_junk", [P, G_DIM])
        V = Steps(nc, mem, "dr_dve_steps")
        A = Steps(nc, mem, "dr_act_steps")
        G = Steps(nc, mem, "dr_pool_steps")
        names = ["alpha", "abs", "log", "g", "g_sums", "eg", "rs", "kn", "qn", "kdec", "vb", "gmask", "decay_sum", "dec_exp",
                 "decT", "kb", "kbg", "qd", "turned", "turned_copied", "A_there", "attn_there", "AT", "attnT", "M", "U",
                 "T_there", "T", "X_there", "X", "TX_there", "XU_there", "w_there", "wT", "v_there", "vnew", "o_there",
                 "o_squared", "ors", "s_there", "state", "o_done"]
        s = {n: c.sem(mem, "dr_" + n) for n in names}
        block = mem.enter_context(nc.Block())

        def cols(ap, gr):
            return ap[:, gr * GW:(gr + 1) * GW]

        def n_u(m, level, gr):
            return m * 2 * LEVELS + 2 * level + gr + 1

        def n_x(m, level, gr):
            return m * 2 * (LEVELS - 1) + 2 * (level - 1) + gr + 1

        def n_t(m, level, gr):
            return m * 2 * (LEVELS - 1) + 2 * level + gr + 1

        @block.tensor
        def _(pe):
            pe.wait_ge(s["g"], 1)
            for i, mask in enumerate((c.k["mask_le"], c.k["mask_gt"], c.k["ones"])):
                last = nc.tensor.matmul(c.bank(7)[:, i * C * H:(i + 1) * C * H], mask[:, :],
                                        g[:, :, :].rearrange("p c h -> p (c h)"), start=True, stop=True)
            last.then_inc(s["g_sums"], 1)
            for m in range(C):
                pe.wait_ge(s["gmask"], m + 1)
                if m:
                    pe.wait_ge(s["dec_exp"], m)
                nc.tensor.matmul(c.bank(6), c.k["mask_gt"][:, :], gmask, start=True, stop=True).then_inc(s["decay_sum"], 1)
                k, q = qkv[:, m, BANK:2 * BANK], qkv[:, m, 0:BANK]
                if m:
                    pe.wait_ge(s["wT"], 2 * m)
                for i, (src, ready) in enumerate(((k, "kn"), (kb, "kb"), (q, "qn"), (qd, "qd"))):
                    pe.wait_ge(s[ready], m + 1)
                    for h in range(H):
                        last = nc.tensor.transpose(head(c.bank(i), h), head(src, h), c.k["ident"][:, :])
                    last.then_inc(s["turned"], 1)
                pe.wait_ge(s["turned_copied"], 4 * m + 2)
                if m:
                    pe.wait_ge(s["state"], m)
                for h in range(H):
                    last = nc.tensor.matmul(head(c.bank(4), h), head(kT, h), head(kbT, h), start=True, stop=True)
                last.then_inc(s["A_there"], 1)
                pe.wait_ge(s["turned_copied"], 4 * m + 3)
                for h in range(H):
                    last = nc.tensor.matmul(head(c.bank(5), h), head(kT, h), head(qT, h), start=True, stop=True)
                last.then_inc(s["attn_there"], 1)
                pe.wait_ge(s["turned_copied"], 4 * m + 4)
                for gr in range(GROUPS):
                    pe.wait_ge(s["U"], n_u(m, 0, gr))
                    for h in range(2):
                        last = nc.tensor.transpose(head(c.bank(2 + gr), h), head(cols(U, gr), h), c.k["ident"][:, :])
                    last.then_inc(s["T_there"], 1)
                for level in range(1, LEVELS):
                    for gr in range(GROUPS):
                        pe.wait_ge(s["M"], n_u(m, level, gr))
                        pe.wait_ge(s["T"], n_t(m, level - 1, gr))
                        for h in range(2):
                            last = nc.tensor.matmul(head(c.bank(gr), h), head(cols(M, gr), h), head(cols(T, gr), h), start=True, stop=True)
                        last.then_inc(s["X_there"], 1)
                    for gr in range(GROUPS):
                        pe.wait_ge(s["X"], n_x(m, level, gr))
                        pe.wait_ge(s["U"], n_u(m, level - 1, gr))
                        if level == 1:
                            pe.wait_ge(s["attnT"], m + 1)
                        for h in range(2):
                            last = nc.tensor.matmul(head(c.bank(4 + gr), h), head(cols(X, gr), h), head(cols(U, gr), h), start=True, stop=True)
                        last.then_inc(s["XU_there"], 1)
                        if level < LEVELS - 1:
                            for h in range(2):
                                last = nc.tensor.matmul(head(c.bank(2 + gr), h), head(cols(U, gr), h), head(cols(X, gr), h), start=True, stop=True)
                            last.then_inc(s["TX_there"], 1)
                vb = qkv[:, m, 2 * BANK:3 * BANK]
                pe.wait_ge(s["kbg"], m + 1)
                for gr in range(GROUPS):
                    pe.wait_ge(s["U"], n_u(m, LEVELS - 1, gr))
                    for h in range(2):
                        last = nc.tensor.matmul(head(c.bank(gr), h), head(cols(kbg, gr), h), head(cols(U, gr), h), start=True, stop=True)
                    last.then_inc(s["w_there"], 1)
                pe.wait_ge(s["vb"], m + 1)
                pe.wait_ge(s["state"], m + 1)
                for gr in range(GROUPS):
                    pe.wait_ge(s["wT"], 2 * m + gr + 1)
                    for h in range(2):
                        v = head(c.bank(2 + gr), h)
                        nc.tensor.matmul(v, head(cols(U, gr), h), head(cols(vb, gr), h), start=True, stop=False)
                        last = nc.tensor.matmul(v, head(cols(wTn, gr), h), head(cols(state, gr), h), start=False, stop=True)
                    last.then_inc(s["v_there"], 1)
                if m:
                    pe.wait_ge(s["o_done"], 4 * m)
                pe.wait_ge(s["kdec"], m + 1)
                pe.wait_ge(s["vnew"], 2 * m + 2)
                for h in range(H):
                    nc.tensor.matmul(head(c.bank(7), h), head(qdT, h), head(state, h), start=True, stop=False)
                    last = nc.tensor.matmul(head(c.bank(7), h), head(attnT, h), head(vnew, h), start=False, stop=True)
                last.then_inc(s["o_there"], 1)
                for h in range(H):
                    last = nc.tensor.matmul(head(c.bank(4), h), head(kdec, h), head(vnew, h), start=True, stop=True)
                last.then_inc(s["s_there"], 1)

        @block.vector
        def _(dve):
            nc.vector.memset(state, 0.0).then_inc(s["state"], 1)
            x = small[:, :, H:2 * H]
            V.then_wait(dve, nc.vector.tensor_tensor(t1[:, :, :], x, c.k["dt_bias"][:, :].unsqueeze(1).to_broadcast([P, C, H]), ALU.add))
            nc.vector.scalar_tensor_tensor(t2[:, :, :], t1[:, :, :], -1.0, t1[:, :, :], ALU.mult, ALU.max).then_inc(s["abs"], 1)
            dve.wait_ge(s["log"], 1)
            V.then_wait(dve, nc.vector.scalar_tensor_tensor(t1[:, :, :], t1[:, :, :], 0.0, t2[:, :, :], ALU.max, ALU.add))
            nc.vector.scalar_tensor_tensor(g[:, :, :], t1[:, :, :], -1.0, ea[:, :].unsqueeze(1).to_broadcast([P, C, H]),
                                           ALU.mult, ALU.mult).then_inc(s["g"], 1)
            dve.wait_ge(s["g"], 1)
            for m in range(C):
                if m:
                    dve.wait_ge(s["turned"], 4 * m)
                nc.vector.tensor_tensor(heads(gmask), same_for_heads(c.k["mask_le"][:, :]), per_head(g[:, m, :]), ALU.mult).then_inc(s["gmask"], 1)
                dve.wait_ge(s["kn"], m + 1)
                nc.vector.tensor_tensor(heads(kb), heads(qkv[:, m, BANK:2 * BANK]), per_head(beta[:, m, :]), ALU.mult).then_inc(s["kb"], 1)
                dve.wait_ge(s["qn"], m + 1)
                dve.wait_ge(s["eg"], 1)
                dve.wait_ge(s["decay_sum"], m + 1)
                nc.vector.tensor_tensor(heads(qd), heads(qkv[:, m, 0:BANK]), per_head(eg[:, 0, m, :]), ALU.mult).then_inc(s["qd"], 1)
                dve.wait_ge(s["kb"], m + 1)
                if m:
                    dve.wait_ge(s["w_there"], 2 * m)
                nc.vector.tensor_tensor(heads(kbg), heads(kb), per_head(eg[:, 0, m, :]), ALU.mult).then_inc(s["kbg"], 1)
                dve.wait_ge(s["A_there"], m + 1)
                dve.wait_ge(s["decT"], m + 1)
                nc.vector.tensor_tensor(AT, c.bank(4), decT, ALU.mult).then_inc(s["AT"], 1)
                dve.wait_ge(s["attn_there"], m + 1)
                nc.vector.tensor_tensor(attnT, c.bank(5), decT, ALU.mult).then_inc(s["attnT"], 1)
                for gr in range(GROUPS):
                    dve.wait_ge(s["M"], n_u(m, 0, gr))
                    nc.vector.tensor_tensor(cols(U, gr).rearrange("p (h d) -> p h d", h=2),
                                            c.k["ident"][:, :].unsqueeze(1).to_broadcast([P, 2, P]),
                                            cols(M, gr).rearrange("p (h d) -> p h d", h=2), ALU.subtract).then_inc(s["U"], 1)
                for gr in range(GROUPS):
                    dve.wait_ge(s["T_there"], 2 * m + gr + 1)
                    nc.vector.tensor_copy(cols(T, gr), c.bank(2 + gr)[:, 0:GW]).then_inc(s["T"], 1)
                for level in range(1, LEVELS):
                    for gr in range(GROUPS):
                        dve.wait_ge(s["XU_there"], n_x(m, level, gr))
                        if level < LEVELS - 1:
                            n = m * 2 * (LEVELS - 2) + 2 * (level - 1) + gr + 1
                            dve.wait_ge(s["TX_there"], n)
                            dve.wait_ge(s["T"], n_t(m, level - 1, gr))
                            nc.vector.tensor_tensor(cols(T, gr), cols(T, gr), c.bank(2 + gr)[:, 0:GW], ALU.subtract).then_inc(s["T"], 1)
                        dve.wait_ge(s["U"], n_u(m, level - 1, gr))
                        nc.vector.tensor_tensor(cols(U, gr), cols(U, gr), c.bank(4 + gr)[:, 0:GW], ALU.subtract).then_inc(s["U"], 1)
                dve.wait_ge(s["ors"], m + 1)
                for h in range(H):
                    nc.vector.scalar_tensor_tensor(head(o[:, m, :], h), head(c.bank(7), h), ors[:, m, h:h + 1], head(o[:, m, :], h),
                                                   ALU.mult, ALU.mult).then_inc(s["o_done"], 1)
                dve.wait_ge(s["s_there"], m + 1)
                for h in range(H):
                    ins = nc.vector.scalar_tensor_tensor(head(state, h), head(state, h), eg[:, 2, m, h:h + 1], head(c.bank(4), h),
                                                         ALU.mult, ALU.add)
                ins.then_inc(s["state"], 1)
                dve.wait_ge(s["state"], m + 2)

        @block.scalar
        def _(act):
            nc.scalar.activation(beta[:, :, :], small[:, :, 0:H], ACT.Sigmoid).then_inc(s["alpha"], 1)
            A.done(nc.scalar.activation(ea[:, :], c.k["a_log"][:, :], ACT.Exp))
            act.wait_ge(s["abs"], 1)
            A.then_wait(act, nc.scalar.activation(t2[:, :, :], t2[:, :, :], ACT.Exp, scale=-1.0))
            nc.scalar.activation(t2[:, :, :], t2[:, :, :], ACT.Ln, bias=1.0).then_inc(s["log"], 1)
            act.wait_ge(s["g_sums"], 1)
            nc.scalar.activation(eg[:, :, :, :].rearrange("p a c h -> p (a c h)"), c.bank(7)[:, 0:3 * C * H], ACT.Exp).then_inc(s["eg"], 1)
            for m in range(C):
                act.wait_ge(s["decay_sum"], m + 1)
                nc.scalar.activation(decT, c.bank(6), ACT.Exp).then_inc(s["dec_exp"], 1)
                if m:
                    act.wait_ge(s["s_there"], m)
                for i, dst in enumerate((kT, kbT, qT, qdT)):
                    act.wait_ge(s["turned"], 4 * m + i + 1)
                    nc.scalar.activation(dst, c.bank(i), ACT.Copy).then_inc(s["turned_copied"], 1)
                for level in range(1, LEVELS):
                    for gr in range(GROUPS):
                        act.wait_ge(s["X_there"], n_x(m, level, gr))
                        nc.scalar.activation(cols(X, gr), c.bank(gr)[:, 0:GW], ACT.Copy).then_inc(s["X"], 1)
                for gr in range(GROUPS):
                    act.wait_ge(s["w_there"], 2 * m + gr + 1)
                    nc.scalar.activation(cols(wTn, gr), c.bank(gr)[:, 0:GW], ACT.Copy, scale=-1.0).then_inc(s["wT"], 1)
                for gr in range(GROUPS):
                    act.wait_ge(s["v_there"], 2 * m + gr + 1)
                    nc.scalar.activation(cols(vnew, gr), c.bank(2 + gr)[:, 0:GW], ACT.Copy).then_inc(s["vnew"], 1)
                act.wait_ge(s["o_there"], m + 1)
                for h in range(H):
                    if 4 * m + h:
                        act.wait_ge(s["o_squared"], 4 * m + h)
                    nc.scalar.activation(junk[:, :], head(c.bank(7), h), ACT.Square, accum_out=oss[:, m, h:h + 1]).then_inc(s["o_squared"], 1)

        @block.gpsimd
        def _(pl):
            G.then_wait(pl, nc.gpsimd.memset(half[:, :], -0.5))
            G.then_wait(pl, nc.gpsimd.tensor_scalar(rs[:, :, :], ss[:, :, :], EPS, None, ALU.add))
            flat = rs[:, :, :].rearrange("p c h -> p (c h)")
            G.then_wait(pl, nc.gpsimd.tensor_tensor(flat, flat, half[:, :].to_broadcast([P, C * 8]), ALU.pow))
            G.then_wait(pl, nc.gpsimd.tensor_scalar(rs[:, :, 0:4], rs[:, :, 0:4], G_DIM ** -0.5, None, ALU.mult))
            pl.wait_ge(s["alpha"], 1)
            pl.wait_ge(s["eg"], 1)
            for m in range(C):
                q, k, v = (qkv[:, m, i * BANK:(i + 1) * BANK] for i in range(3))
                nc.gpsimd.tensor_tensor(heads(k), heads(k), per_head(rs[:, m, 4:8]), ALU.mult).then_inc(s["kn"], 1)
                nc.gpsimd.tensor_tensor(heads(q), heads(q), per_head(rs[:, m, 0:4]), ALU.mult).then_inc(s["qn"], 1)
                pl.wait_ge(s["dec_exp"], m + 1)
                nc.gpsimd.tensor_tensor(heads(decT), heads(decT), same_for_heads(c.k["mask_le"][:, :]), ALU.mult).then_inc(s["decT"], 1)
                for level in range(LEVELS):
                    if level == 1:
                        if m:
                            pl.wait_ge(s["s_there"], m)
                        pl.wait_ge(s["kn"], m + 1)
                        nc.gpsimd.tensor_tensor(heads(kdec), heads(k), per_head(eg[:, 1, m, :]), ALU.mult).then_inc(s["kdec"], 1)
                        nc.gpsimd.tensor_tensor(heads(v), heads(v), per_head(beta[:, m, :]), ALU.mult).then_inc(s["vb"], 1)
                    for gr in range(GROUPS):
                        if level == 0:
                            pl.wait_ge(s["AT"], m + 1)
                        elif level == 1:
                            pl.wait_ge(s["U"], n_u(m, 0, gr))
                        else:
                            pl.wait_ge(s["X_there"], n_x(m, level - 1, gr))
                        nc.gpsimd.tensor_tensor(cols(M, gr).rearrange("p (h d) -> p h d", h=2),
                                                cols(AT, gr).rearrange("p (h d) -> p h d", h=2),
                                                c.k["level_masks"][:, level, :].unsqueeze(1).to_broadcast([P, 2, P]), ALU.mult).then_inc(s["M"], 1)
                pl.wait_ge(s["o_squared"], 4 * m + 4)
                G.then_wait(pl, nc.gpsimd.tensor_scalar(ors[:, m, :], oss[:, m, :], 1.0 / G_DIM, EPS, ALU.mult, ALU.add))
                nc.gpsimd.tensor_tensor(ors[:, m, :], ors[:, m, :], half[:, :].to_broadcast([P, H]), ALU.pow).then_inc(s["ors"], 1)


def retention_inputs(c, hT, q, k, v, gate, tables):
    nc = c.nc
    NB = 4
    cos, sin = tables
    with ExitStack() as mem:
        tmp = c.sb(mem, "ri_tmp", [P, 2, BANK])
        tables_there = c.sem(mem, "ri_tables_there")
        product = c.sem(mem, "ri_product")
        taken = c.sem(mem, "ri_taken")
        turned = c.sem(mem, "ri_rotated")
        V = Steps(nc, mem, "ri_dve_steps")
        block = mem.enter_context(nc.Block())

        @block.sync
        def _(sp):
            sp.dma_start(cos[:, :, :], c.io["t_cos"]).then_inc(tables_there, 16)
            sp.dma_start(sin[:, :, :], c.io["t_sin"]).then_inc(tables_there, 16)
            c.load_chunks(sp, C_OUT2 + 2)

        @block.tensor
        def _(pe):
            for i in range(4 * TT):
                j, m = i // TT, i % TT
                if m == 0:
                    c.wait_chunk(pe, C_IN2 + 4 + j)
                if i >= NB:
                    pe.wait_ge(taken, i - NB + 1)
                mm_tokens(nc.tensor, c.bank(i % NB), hT, m, c.chunk(C_IN2 + 4 + j)).then_inc(product, 1)

        @block.vector
        def _(dve):
            dve.wait_ge(tables_there, 32)
            for i in range(2 * TT):
                m = i % TT
                dst = (q, k)[i // TT][:, m, :]
                dve.wait_ge(product, i + 1)
                if m == TT - 1:
                    dve.sem_inc(c.used, 1)
                b = c.bank(i % NB)
                V.done(nc.vector.tensor_tensor(heads(dst), heads(b), same_for_heads(cos[:, m, :]), ALU.mult))
                halves = b.rearrange("p (h two d) -> p h two d", h=4, two=2)[:, :, ::-1, :]
                for x in range(2):
                    ins = nc.vector.tensor_tensor(heads(tmp[:, i % 2, :])[:, :, x * 64:(x + 1) * 64], halves[:, :, x, :],
                                                  sin[:, m, x * 64:(x + 1) * 64].unsqueeze(1).to_broadcast([P, 4, 64]), ALU.mult)
                    if x:
                        ins.then_inc(taken, 1)
                    else:
                        V.done(ins)
                V.settle(dve)
                dve.wait_ge(taken, i + 1)
                nc.vector.tensor_tensor(dst, dst, tmp[:, i % 2, :], ALU.add).then_inc(turned, 1)
            for i in range(2 * TT, 3 * TT):
                dve.wait_ge(product, i + 1)
                if i % TT == TT - 1:
                    dve.sem_inc(c.used, 1)
                nc.vector.tensor_copy(v[:, i % TT, :], c.bank(i % NB)).then_inc(taken, 1)
            for i in range(3 * TT, 4 * TT):
                m = i % TT
                dve.wait_ge(taken, i + 1)
                nc.vector.tensor_tensor(gate[:, m, :], gate[:, m, :], c.k["norm_b"][:, :], ALU.mult)

        @block.scalar
        def _(act):
            act.wait_ge(taken, 3 * TT)
            for i in range(3 * TT, 4 * TT):
                act.wait_ge(product, i + 1)
                if i % TT == TT - 1:
                    act.sem_inc(c.used, 1)
                nc.scalar.activation(gate[:, i % TT, :], c.bank(i % NB), ACT.Silu).then_inc(taken, 1)


def retention_decay(h):
    return 1.0 - 2.0 ** (-5.0 - h)


def retention(c, q, k, v, o):
    nc = c.nc
    H, C = A_HEADS, TT
    with ExitStack() as mem:
        kT, qdT, attnT = (c.sb(mem, "rt_" + n, [P, BANK])[:, :] for n in ("kT", "qdT", "attnT"))
        kd = c.sb(mem, "rt_kd", [P, 2, BANK])
        state = c.sb(mem, "rt_state", [P, BANK])[:, :]
        decay = c.sb(mem, "rt_decay", [P, H, P])
        oss = c.sb(mem, "rt_oss", [P, C, H])
        ors = c.sb(mem, "rt_ors", [P, C, H])
        half = c.sb(mem, "rt_half", [P, 1])
        junk = c.sb(mem, "rt_junk", [P, G_DIM])
        G = Steps(nc, mem, "rt_pool_steps")
        names = ["decay", "qd", "kd", "turned", "turned_copied", "attn_there", "attnT", "o_there", "o_squared", "ors", "o_done",
                 "s_there", "state"]
        s = {n: c.sem(mem, "rt_" + n) for n in names}
        block = mem.enter_context(nc.Block())

        @block.sync
        def _(sp):
            sp.dma_start(decay[:, :, :], c.io["t_decay"]).then_inc(s["decay"], 16)

        @block.gpsimd
        def _(pl):
            G.then_wait(pl, nc.gpsimd.memset(half[:, :], -0.5))

            def norm(m):
                pl.wait_ge(s["o_squared"], 4 * m + 4)
                G.then_wait(pl, nc.gpsimd.tensor_scalar(ors[:, m, :], oss[:, m, :], 1.0 / G_DIM, EPS, ALU.mult, ALU.add))
                nc.gpsimd.tensor_tensor(ors[:, m, :], ors[:, m, :], half[:, :].to_broadcast([P, H]), ALU.pow).then_inc(s["ors"], 1)

            for m in range(C):
                nc.gpsimd.tensor_tensor(heads(q[:, m, :]), heads(q[:, m, :]), per_head(c.k["q_decay"][:, :]), ALU.mult).then_inc(s["qd"], 1)
                if m >= 2:
                    pl.wait_ge(s["s_there"], m - 1)
                nc.gpsimd.tensor_tensor(heads(kd[:, m % 2, :]), heads(k[:, m, :]), per_head(c.k["k_decay"][:, :]), ALU.mult).then_inc(s["kd"], 1)
                if m:
                    norm(m - 1)
            norm(C - 1)

        @block.tensor
        def _(pe):
            for m in range(C):
                pe.wait_ge(s["qd"], m + 1)
                for i, src in enumerate((k, q)):
                    if m:
                        pe.wait_ge(s["turned_copied"], 2 * m - 1 + i)
                    for h in range(H):
                        last = nc.tensor.transpose(head(c.bank(i), h), head(src[:, m, :], h), c.k["ident"][:, :])
                    last.then_inc(s["turned"], 1)
                pe.wait_ge(s["turned_copied"], 2 * m + 2)
                if m:
                    pe.wait_ge(s["attnT"], m)
                for h in range(H):
                    last = nc.tensor.matmul(head(c.bank(2), h), head(kT, h), head(qdT, h), start=True, stop=True)
                last.then_inc(s["attn_there"], 1)
                pe.wait_ge(s["kd"], m + 1)
                if m:
                    pe.wait_ge(s["state"], m)
                for h in range(H):
                    last = nc.tensor.matmul(head(c.bank(6 + m % 2), h), head(kd[:, m % 2, :], h), head(v[:, m, :], h), start=True, stop=True)
                last.then_inc(s["s_there"], 1)
                pe.wait_ge(s["attnT"], m + 1)
                pe.wait_ge(s["state"], m + 1)
                if m >= 2:
                    pe.wait_ge(s["o_done"], m - 1)
                for h in range(H):
                    nc.tensor.matmul(head(c.bank(4 + m % 2), h), head(qdT, h), head(state, h), start=True, stop=False)
                    last = nc.tensor.matmul(head(c.bank(4 + m % 2), h), head(attnT, h), head(v[:, m, :], h), start=False, stop=True)
                last.then_inc(s["o_there"], 1)

        @block.scalar
        def _(act):
            for m in range(C):
                if m:
                    act.wait_ge(s["o_there"], m)
                for i, dst in enumerate((kT, qdT)):
                    act.wait_ge(s["turned"], 2 * m + i + 1)
                    nc.scalar.activation(dst, c.bank(i), ACT.Copy).then_inc(s["turned_copied"], 1)
                act.wait_ge(s["o_there"], m + 1)
                for h in range(H):
                    if 4 * m + h:
                        act.wait_ge(s["o_squared"], 4 * m + h)
                    nc.scalar.activation(junk[:, :], head(c.bank(4 + m % 2), h), ACT.Square, accum_out=oss[:, m, h:h + 1]).then_inc(s["o_squared"], 1)

        @block.vector
        def _(dve):
            nc.vector.memset(state, 0.0).then_inc(s["state"], 1)
            dve.wait_ge(s["decay"], 16)
            dve.wait_ge(s["state"], 1)

            def finish(m):
                dve.wait_ge(s["ors"], m + 1)
                for h in range(H):
                    ins = nc.vector.scalar_tensor_tensor(head(o[:, m, :], h), head(c.bank(4 + m % 2), h), ors[:, m, h:h + 1],
                                                         head(o[:, m, :], h), ALU.mult, ALU.mult)
                ins.then_inc(s["o_done"], 1)

            for m in range(C):
                dve.wait_ge(s["attn_there"], m + 1)
                nc.vector.tensor_tensor(attnT, c.bank(2), decay[:, :, :].rearrange("p h k -> p (h k)"), ALU.mult).then_inc(s["attnT"], 1)
                dve.wait_ge(s["o_there"], m + 1)
                dve.wait_ge(s["s_there"], m + 1)
                for h in range(H):
                    ins = nc.vector.scalar_tensor_tensor(head(state, h), head(state, h), retention_decay(h) ** P,
                                                         head(c.bank(6 + m % 2), h), ALU.mult, ALU.add)
                ins.then_inc(s["state"], 1)
                dve.wait_ge(s["state"], m + 2)
                finish(m)


GR = N_GROUPS + N_EXPERTS
ROWS = 64
OVERFLOW = S * 2 // ROWS
PAIRS_AT = OVERFLOW + 2
BLOCKS = N_EXPERTS + OVERFLOW
SLOTS = 4
NEVER = 1.0e30


class Experts:

    def __init__(self, c, mem, places):
        self.c = c
        self.landed = [c.sem(mem, f"expert_landed_{i}") for i in range(SLOTS)]
        self.gate, self.up, self.down = [], [], []
        for p in places:
            self.gate.append(p[:, 0:KT * D_EXPERT].rearrange("p (k n) -> p k n", k=KT))
            self.up.append(p[:, KT * D_EXPERT:2 * KT * D_EXPERT].rearrange("p (k n) -> p k n", k=KT))
            self.down.append(p[:, 2 * KT * D_EXPERT:2 * KT * D_EXPERT + 2 * D].rearrange("p (k n) -> p k n", k=2))

    def load(self, sp, slot, expert):
        io = self.c.io
        pick = slice(expert, expert + 1) if isinstance(expert, int) else bass.ds(expert, 1)
        for dst, w, k in ((self.gate, "w_gate_2", KT), (self.up, "w_up_2", KT), (self.down, "w_down_2", 2)):
            src = io[w][pick, :, :].rearrange("e (k p) n -> p (e k) n", p=P)
            sp.dma_start(dst[slot], src).then_inc(self.landed[slot], 16)

    def there(self, pe, slot, uses):
        pe.wait_ge(self.landed[slot], uses * 48)


def route(c, hT, experts, weights, slots, perm, overflow):
    nc = c.nc
    with ExitStack() as mem:
        def t(name, *shape, dt=F32):
            return c.sb(mem, "ro_" + name, [P, *shape], dt)

        E, NG, PG = N_EXPERTS, N_GROUPS, PER_GROUP
        lg = t("logits", TT, GR)
        gtop, gsum, top1, top2 = (t(n, TT, 1) for n in ("gtop", "gsum", "top1", "top2"))
        gdiff, gfirst, goh = (t(n, TT, NG) for n in ("gdiff", "gfirst", "goh"))
        pick = t("pick", TT, 1)
        tmp = t("tmp", TT, E)
        esel, efirst, oh1, oh2 = (t(n, TT, PG) for n in ("esel", "efirst", "oh1", "oh2"))
        e21 = t("e21", TT, 1)
        OH = t("OH", 2, TT, E)
        M = t("M", TT, E)
        pos = t("pos", TT, E)
        cnt, ov, ovend, ovplace = (t(n, E) for n in ("cnt", "ov", "ovend", "ovplace"))
        over = t("over", E, 16)
        rank, place, place2, slotf = (t(n, TT, 2) for n in ("rank", "place", "place2", "slotf"))
        sloti, blocki, rowi = (t(n, TT * 2, dt=I32) for n in ("sloti", "blocki", "rowi"))
        blockf, rowf = (t(n, TT * 2) for n in ("blockf", "rowf"))
        ohb = t("ohb", 2, BLOCKS + 2)
        ohr = t("ohr", 2, ROWS)
        ovexp = t("ovexp", 1)
        pairs = t("pairs", 1)
        V = Steps(nc, mem, "ro_dve_steps")
        logits_there = c.sem(mem, "ro_logits_there")
        logits_copied = c.sem(mem, "ro_logits_copied")
        gdiff_ready = c.sem(mem, "ro_gdiff_ready")
        e21_ready = c.sem(mem, "ro_e21_ready")
        exps_ready = c.sem(mem, "ro_exps_ready")
        picks_ready = c.sem(mem, "ro_picks_ready")
        counted = c.sem(mem, "ro_counted")
        onehots = c.sem(mem, "ro_onehots")
        permuted = c.sem(mem, "ro_permuted")
        ovexp_ready = c.sem(mem, "ro_ovexp_ready")
        ovrow_there = c.sem(mem, "ro_ovrow_there")
        block = mem.enter_context(nc.Block())

        @block.sync
        def _(sp):
            sp.wait_ge(logits_there, TT)
            experts.load(sp, 0, 0)

        @block.tensor
        def _(pe):
            for m in range(TT):
                if m >= 4:
                    pe.wait_ge(logits_copied, m - 3)
                mm_tokens(nc.tensor, c.bank(m % 4)[:, 0:GR], hT, m, c.k["w_router"]).then_inc(logits_there, 1)
            pe.wait_ge(picks_ready, 1)
            for m in range(TT):
                for j in range(m + 1):
                    nc.tensor.matmul(c.bank(4)[:, m * E:(m + 1) * E], (c.k["mask_lt"] if j == m else c.k["ones"])[:, :], M[:, j, :],
                                     start=(j == 0), stop=(j == m))
            for j in range(TT):
                last = nc.tensor.matmul(c.bank(5)[:, 0:E], c.k["ones"][:, :], M[:, j, :], start=(j == 0), stop=(j == TT - 1))
            last.then_inc(counted, 1)
            pe.wait_ge(ovexp_ready, 1)
            nc.tensor.matmul(c.bank(6)[0:1, 0:P], ovexp[:, :], c.k["ident"][:, :], start=True, stop=True).then_inc(ovrow_there, 1)
            for i in range(2 * TT):
                pe.wait_ge(onehots, i + 1)
                last = nc.tensor.matmul(c.bank(7)[0:ROWS, 0:BLOCKS + 2], ohr[:, i % 2, :], ohb[:, i % 2, :],
                                        start=(i == 0), stop=(i == 2 * TT - 1))
                last.then_inc(permuted, 1)

        @block.scalar
        def _(act):
            for m in range(TT):
                act.wait_ge(logits_there, m + 1)
                nc.scalar.activation(lg[:, m, :], c.bank(m % 4)[:, 0:GR], ACT.Copy).then_inc(logits_copied, 1)
            act.wait_ge(gdiff_ready, 1)
            nc.scalar.activation(gdiff[:, :, :], gdiff[:, :, :], ACT.Exp).then_inc(exps_ready, 1)
            act.wait_ge(e21_ready, 1)
            nc.scalar.activation(e21[:, :, :], e21[:, :, :], ACT.Exp).then_inc(exps_ready, 1)

        @block.vector
        def _(dve):
            v = nc.vector

            def do(ins):
                V.then_wait(dve, ins)

            def wide(ap, n):
                return ap.to_broadcast([P, TT, n])

            def first_of(dst, values, top, first):
                do(v.tensor_tensor(first, values, wide(top, PG), ALU.is_equal))
                do(v.scalar_tensor_tensor(first, first, -float(PG), c.k["iota"][:, 0:PG].unsqueeze(1).to_broadcast([P, TT, PG]),
                                          ALU.mult, ALU.add))
                do(v.tensor_reduce(pick[:, :, :], first, AX.X, ALU.min))
                do(v.tensor_tensor(dst, first, wide(pick[:, :, :], PG), ALU.is_equal))

            dve.wait_ge(logits_copied, TT)
            gl = lg[:, :, 0:NG]
            do(v.tensor_reduce(gtop[:, :, :], gl, AX.X, ALU.max))
            v.tensor_tensor(gdiff[:, :, :], gl, wide(gtop[:, :, :], NG), ALU.subtract).then_inc(gdiff_ready, 1)
            first_of(goh[:, :, :], gl, gtop[:, :, :], gfirst[:, :, :])
            for m in range(TT):
                V.done(v.tensor_tensor(tmp[:, m, :].rearrange("p (g e) -> p g e", g=NG),
                                       lg[:, m, NG:GR].rearrange("p (g e) -> p g e", g=NG),
                                       goh[:, m, :].unsqueeze(2).to_broadcast([P, NG, PG]), ALU.mult))
            V.settle(dve)
            do(v.tensor_reduce(esel[:, :, :], tmp[:, :, :].rearrange("p t (g e) -> p t e g", g=NG), AX.X, ALU.add))
            do(v.tensor_reduce(top1[:, :, :], esel[:, :, :], AX.X, ALU.max))
            first_of(oh1[:, :, :], esel[:, :, :], top1[:, :, :], efirst[:, :, :])
            do(v.scalar_tensor_tensor(esel[:, :, :], oh1[:, :, :], -NEVER, esel[:, :, :], ALU.mult, ALU.add))
            do(v.tensor_reduce(top2[:, :, :], esel[:, :, :], AX.X, ALU.max))
            v.tensor_tensor(e21[:, :, :], top2[:, :, :], top1[:, :, :], ALU.subtract).then_inc(e21_ready, 1)
            first_of(oh2[:, :, :], esel[:, :, :], top2[:, :, :], efirst[:, :, :])
            for m in range(TT):
                for k, oh in enumerate((oh1, oh2)):
                    V.done(v.tensor_tensor(OH[:, k, m, :].rearrange("p (g e) -> p g e", g=NG),
                                           goh[:, m, :].unsqueeze(2).to_broadcast([P, NG, PG]),
                                           oh[:, m, :].unsqueeze(1).to_broadcast([P, NG, PG]), ALU.mult))
            V.settle(dve)
            v.tensor_tensor(M[:, :, :], OH[:, 0, :, :], OH[:, 1, :, :], ALU.add).then_inc(picks_ready, 1)
            dve.wait_ge(exps_ready, 2)
            do(v.tensor_reduce(gsum[:, :, :], gdiff[:, :, :], AX.X, ALU.add))
            do(v.scalar_tensor_tensor(gsum[:, :, :], e21[:, :, :], 1.0, gsum[:, :, :], ALU.add, ALU.mult))
            do(v.reciprocal(weights[:, 0, :], gsum[:, :, :].rearrange("p t o -> p (t o)")))
            do(v.tensor_tensor(weights[:, 1, :], weights[:, 0, :], e21[:, :, :].rearrange("p t o -> p (t o)"), ALU.mult))
            dve.wait_ge(counted, 1)
            do(v.tensor_copy(pos[:, :, :], c.bank(4).rearrange("p (t e) -> p t e", e=E)))
            do(v.tensor_copy(cnt[:, :], c.bank(5)[:, 0:E]))
            do(v.tensor_tensor(over[:, :, :], cnt[:, :].unsqueeze(2).to_broadcast([P, E, 16]),
                               c.k["thresholds"][:, :].unsqueeze(1).to_broadcast([P, E, 16]), ALU.is_gt))
            do(v.tensor_reduce(ov[:, :], over[:, :, :], AX.X, ALU.add))
            do(v.tensor_tensor_scan(ovend[:, :], c.k["ones"][:, 0:1].to_broadcast([P, E]), ov[:, :], 0.0, ALU.mult, ALU.add))
            do(v.scalar_tensor_tensor(ovplace[:, :], ovend[:, :], float(N_EXPERTS - 1), ov[:, :], ALU.add, ALU.subtract))
            do(v.tensor_scalar(cnt[:, :], ovend[:, :], c.k["iota_p"][:, 0:1], None, ALU.is_le))
            do(v.tensor_reduce(ovexp[:, :], cnt[:, :], AX.X, ALU.add))
            v.tensor_scalar(ovexp[:, :], ovexp[:, :], float(E - 1), None, ALU.min).then_inc(ovexp_ready, 1)
            do(v.tensor_scalar(pairs[:, :], ovend[:, E - 1:E], 1.0, None, ALU.add))
            do(v.tensor_scalar(pairs[:, :], pairs[:, :], 2.0, None, ALU.max))
            do(v.tensor_copy(sloti[:, 0:1], pairs[:, :]))
            do(v.tensor_scalar(overflow[0:1, PAIRS_AT:PAIRS_AT + 1], sloti[0:1, 0:1], 1, None, ALU.arith_shift_right))
            for dst, table in ((rank, None), (place, c.k["iota"]), (place2, ovplace)):
                for k in range(2):
                    other = pos[:, :, :] if table is None else table[:, 0:E].unsqueeze(1).to_broadcast([P, TT, E])
                    do(v.tensor_tensor(tmp[:, :, :], OH[:, k, :, :], other, ALU.mult))
                    do(v.tensor_reduce(dst[:, :, k:k + 1], tmp[:, :, :], AX.X, ALU.add))
            do(v.tensor_tensor(place2[:, :, :], place2[:, :, :], place[:, :, :], ALU.subtract))
            do(v.scalar_tensor_tensor(place2[:, :, :], rank[:, :, :], float(ROWS), place2[:, :, :], ALU.is_ge, ALU.mult))
            do(v.tensor_tensor(place[:, :, :], place[:, :, :], place2[:, :, :], ALU.add))
            do(v.scalar_tensor_tensor(slotf[:, :, :], place[:, :, :], float(ROWS), rank[:, :, :], ALU.mult, ALU.add))
            flat = slotf[:, :, :].rearrange("p t k -> p (t k)")
            do(v.tensor_copy(sloti[:, :], flat))
            do(v.tensor_copy(slots[:, :], flat))
            do(v.tensor_scalar(blocki[:, :], sloti[:, :], 6, None, ALU.arith_shift_right))
            do(v.tensor_scalar(rowi[:, :], sloti[:, :], ROWS - 1, None, ALU.bitwise_and))
            do(v.tensor_copy(blockf[:, :], blocki[:, :]))
            do(v.tensor_copy(rowf[:, :], rowi[:, :]))
            for i in range(2 * TT):
                if i >= 2:
                    dve.wait_ge(permuted, i - 1)
                do(v.tensor_scalar(ohr[:, i % 2, :], c.k["iota"][:, 0:ROWS], rowf[:, i:i + 1], c.k["token"][:, i // 2:i // 2 + 1],
                                   ALU.is_equal, ALU.mult))
                v.tensor_scalar(ohb[:, i % 2, :], c.k["iota"][:, 0:BLOCKS + 2], blockf[:, i:i + 1], None, ALU.is_equal).then_inc(onehots, 1)
            dve.wait_ge(ovrow_there, 1)
            do(v.tensor_copy(overflow[0:1, 0:PAIRS_AT], c.bank(6)[0:1, 0:PAIRS_AT]))
            dve.wait_ge(permuted, 2 * TT)
            do(v.tensor_copy(perm[:, :], c.bank(7)[0:ROWS, 0:BLOCKS + 2]))


def run_experts(c, experts, h_rows, y_rows, perm, overflow):
    nc = c.nc
    HT = D_EXPERT // P
    with ExitStack() as mem:
        idx = c.sb(mem, "ex_idx", [ROWS, 2], U32)
        xg = c.sb(mem, "ex_x", [ROWS, 2, D])
        xT = c.sb(mem, "ex_xT", [P, 2, KT, ROWS])
        sg = c.sb(mem, "ex_silu", [P, 2, HT * ROWS])
        h = c.sb(mem, "ex_h", [P, 2, HT * ROWS])
        y = c.sb(mem, "ex_y", [ROWS, 2, D])
        idx_ready = c.sem(mem, "ex_idx_ready")
        x_there = [c.sem(mem, f"ex_x_there_{i}") for i in range(2)]
        turned = c.sem(mem, "ex_turned")
        xT_ready = c.sem(mem, "ex_xT_ready")
        gate_up = c.sem(mem, "ex_gate_up_there")
        silu_done = c.sem(mem, "ex_silu_done")
        h_ready = c.sem(mem, "ex_h_ready")
        y_there = c.sem(mem, "ex_y_there")
        y_act = c.sem(mem, "ex_y_first_half_copied")
        y_dve = c.sem(mem, "ex_y_second_half_copied")
        stored = [c.sem(mem, f"ex_y_stored_{i}") for i in range(2)]
        passed_sp, passed_act, passed_pe, passed_pool = (c.sem(mem, "ex_passed_" + n) for n in ("sp", "act", "pe", "pool"))
        block = mem.enter_context(nc.Block())
        FIRST = N_EXPERTS // SLOTS

        def all_blocks(eng, name, one):
            for u in range(SLOTS):
                one(u, u, 1)
            with eng.Fori(1, FIRST) as i:
                for u in range(SLOTS):
                    one(i * SLOTS + u, u, i + 1)
            with eng.Fori(0, n_pairs(eng)) as i:
                for u in range(2):
                    one(i * 2 + (N_EXPERTS + u), u, i + (FIRST + 1))

        def n_pairs(eng):
            return eng.value_load(overflow[0:1, PAIRS_AT:PAIRS_AT + 1], min_val=1, max_val=OVERFLOW // 2)

        def started(b, n):
            return not isinstance(b, int) or b >= n

        @block.sync
        def _(sp):
            for u in range(SLOTS):
                sp.wait_ge(y_there, u + 1)
                experts.load(sp, u, SLOTS + u)
            with sp.Fori(2, FIRST) as i:
                for u in range(SLOTS):
                    sp.wait_ge(y_there, i * SLOTS + (u - SLOTS + 1))
                    experts.load(sp, u, i * SLOTS + u)
            for u in range(2):
                sp.wait_ge(y_there, N_EXPERTS - SLOTS + u + 1)
                experts.load(sp, u, sp.value_load(overflow[0:1, u:u + 1], min_val=0, max_val=N_EXPERTS - 1))
            with sp.Fori(0, n_pairs(sp)) as i:
                for u in range(2):
                    e = sp.value_load(overflow[0:1, bass.ds(i * 2 + (2 + u), 1)], min_val=0, max_val=N_EXPERTS - 1)
                    sp.wait_ge(y_there, i * 2 + (N_EXPERTS + u + 1))
                    experts.load(sp, u, e)
            n = n_pairs(sp)
            for u in range(2):
                sp.wait_ge(experts.landed[u], n * 48 + (FIRST + 1) * 48)
                sp.sem_inc(passed_sp, 1)
            sp.wait_ge(y_there, N_EXPERTS)

        @block.gpsimd
        def _(pl):
            def gather(b, s):
                if started(b, 2):
                    pl.wait_ge(turned, b - 1)
                col = slice(b, b + 1) if isinstance(b, int) else bass.ds(b, 1)
                nc.gpsimd.tensor_copy(idx[:, s:s + 1], perm[:, col]).then_inc(idx_ready, 1)
                pl.wait_ge(idx_ready, b + 1)
                pl.sem_inc(passed_pool, 1)
                nc.gpsimd.indirect_dma_start(
                    out=xg[:, s, :], out_offset=None, in_=h_rows,
                    in_offset=bass.IndirectOffsetOnAxis(ap=idx[:, s:s + 1], axis=0)).then_inc(x_there[s], 16)

            gather(0, 0)
            all_blocks(pl, "gather", lambda b, u, uses: gather(b + 1, (u + 1) % 2))

        @block.tensor
        def _(pe):
            def turn(b, s, n):
                if started(b, 2):
                    pe.wait_ge(xT_ready, b - 1)
                pe.wait_ge(x_there[s], n * 16)
                pe.sem_inc(passed_pe, 1)
                for k in range(KT):
                    last = nc.tensor.transpose(c.bank(s)[:, k * ROWS:(k + 1) * ROWS], xg[:, s, k * P:(k + 1) * P],
                                               c.k["ident"][0:ROWS, 0:ROWS])
                last.then_inc(turned, 1)

            def one(b, u, uses):
                s = u % 2
                experts.there(pe, u, uses)
                pe.wait_ge(xT_ready, b + 1)
                if started(b, 2):
                    pe.wait_ge(h_ready, b - 1)
                for i, w in enumerate((experts.gate, experts.up)):
                    for f in range(HT):
                        for k in range(KT):
                            at = (i * HT + f) * ROWS
                            last = nc.tensor.matmul(c.bank(2 + s)[:, at:at + ROWS], w[u][:, k, f * P:(f + 1) * P], xT[:, s, k, :],
                                                    start=(k == 0), stop=(k == KT - 1))
                last.then_inc(gate_up, 1)
                turn(b + 1, 1 - s, count_of(b + 1))
                pe.wait_ge(h_ready, b + 1)
                if started(b, 2):
                    pe.wait_ge(y_act, b - 1)
                    pe.wait_ge(y_dve, b - 1)
                for n in range(2):
                    for f in range(HT):
                        last = nc.tensor.matmul(c.bank(4 + 2 * s + n)[0:ROWS, :], h[:, s, f * ROWS:(f + 1) * ROWS],
                                                experts.down[u][:, f, n * BANK:(n + 1) * BANK], start=(f == 0), stop=(f == HT - 1))
                last.then_inc(y_there, 1)

            def count_of(b):
                return counts[0]

            counts = [None]
            turn(0, 0, 1)
            for u in range(SLOTS):
                counts[0] = (u + 1) // 2 + 1
                one(u, u, 1)
            with pe.Fori(1, FIRST) as i:
                for u in range(SLOTS):
                    counts[0] = i * 2 + ((u + 1) // 2 + 1)
                    one(i * SLOTS + u, u, i + 1)
            with pe.Fori(0, n_pairs(pe)) as i:
                for u in range(2):
                    counts[0] = i + (N_EXPERTS // 2 + (u + 1) // 2 + 1)
                    one(i * 2 + (N_EXPERTS + u), u, i + (FIRST + 1))

        @block.scalar
        def _(act):
            def copy_x(b, s):
                act.wait_ge(turned, b + 1)
                if started(b, 2):
                    act.wait_ge(gate_up, b - 1)
                nc.scalar.activation(xT[:, s, :, :].rearrange("p k r -> p (k r)"), c.bank(s), ACT.Copy).then_inc(xT_ready, 1)

            def one(b, u, uses):
                s = u % 2
                act.wait_ge(gate_up, b + 1)
                if started(b, 2):
                    act.wait_ge(h_ready, b - 1)
                nc.scalar.activation(sg[:, s, :], c.bank(2 + s)[:, 0:HT * ROWS], ACT.Silu).then_inc(silu_done, 1)
                copy_x(b + 1, 1 - s)
                act.wait_ge(y_there, b + 1)
                if started(b, 2):
                    act.wait_ge(stored[s], (store_count[0] - 1) * 16)
                nc.scalar.activation(y[:, s, 0:BANK], c.bank(4 + 2 * s)[0:ROWS, :], ACT.Copy).then_inc(y_act, 1)
                act.wait_ge(y_act, b + 1)
                act.wait_ge(y_dve, b + 1)
                rows_ = slice(b * ROWS, (b + 1) * ROWS) if isinstance(b, int) else bass.ds(b * ROWS, ROWS)
                act.dma_start(y_rows[rows_, :], y[:, s, :]).then_inc(stored[s], 16)

            store_count = [None]
            copy_x(0, 0)
            for u in range(SLOTS):
                store_count[0] = u // 2 + 1
                one(u, u, 1)
            with act.Fori(1, FIRST) as i:
                for u in range(SLOTS):
                    store_count[0] = i * 2 + (u // 2 + 1)
                    one(i * SLOTS + u, u, i + 1)
            with act.Fori(0, n_pairs(act)) as i:
                for u in range(2):
                    store_count[0] = i + (N_EXPERTS // 2 + 1)
                    one(i * 2 + (N_EXPERTS + u), u, i + (FIRST + 1))
            n = n_pairs(act)
            for s in range(2):
                act.wait_ge(stored[s], n * 16 + N_EXPERTS // 2 * 16)
                act.sem_inc(passed_act, 1)

        @block.vector
        def _(dve):
            def one(b, u, uses, store_uses):
                s = u % 2
                dve.wait_ge(silu_done, b + 1)
                if started(b, 2):
                    dve.wait_ge(y_there, b - 1)
                nc.vector.tensor_tensor(h[:, s, :], sg[:, s, :], c.bank(2 + s)[:, HT * ROWS:2 * HT * ROWS], ALU.mult).then_inc(h_ready, 1)
                dve.wait_ge(y_there, b + 1)
                if started(b, 2):
                    dve.wait_ge(stored[s], store_uses * 16)
                nc.vector.tensor_copy(y[:, s, BANK:D], c.bank(5 + 2 * s)[0:ROWS, :]).then_inc(y_dve, 1)

            for u in range(SLOTS):
                one(u, u, 1, u // 2)
            with dve.Fori(1, FIRST) as i:
                for u in range(SLOTS):
                    one(i * SLOTS + u, u, i + 1, i * 2 + u // 2)
            with dve.Fori(0, n_pairs(dve)) as i:
                for u in range(2):
                    one(i * 2 + (N_EXPERTS + u), u, i + (FIRST + 1), i + N_EXPERTS // 2)


def combine(c, x_sb, y_rows, weights, slots, out):
    nc = c.nc
    with ExitStack() as mem:
        g = c.sb(mem, "co_rows", [P, 4, D])
        junk = c.sb(mem, "co_squares", [P, 2, D])
        ss = c.sb(mem, "co_ss", [P, TT])
        rstd = c.sb(mem, "co_rstd", [P, TT])
        half = c.sb(mem, "co_half", [P, 1])
        G = Steps(nc, mem, "co_pool_steps")
        rows_there = [c.sem(mem, f"co_rows_there_{i}") for i in range(4)]
        summed = c.sem(mem, "co_summed")
        squared = c.sem(mem, "co_squared")
        rstd_ready = c.sem(mem, "co_rstd_ready")
        normed = c.sem(mem, "co_normed")
        stored = c.sem(mem, "co_stored")
        block = mem.enter_context(nc.Block())

        @block.gpsimd
        def _(pl):
            G.then_wait(pl, nc.gpsimd.memset(half[:, :], -0.5))

            def gather(i):
                if i >= 4:
                    pl.wait_ge(summed, i - 3)
                nc.gpsimd.indirect_dma_start(
                    out=g[:, i % 4, :], out_offset=None, in_=y_rows,
                    in_offset=bass.IndirectOffsetOnAxis(ap=slots[:, i:i + 1], axis=0)).then_inc(rows_there[i % 4], 16)

            for i in range(4):
                gather(i)
            for m in range(TT):
                pl.wait_ge(squared, m + 1)
                G.then_wait(pl, nc.gpsimd.tensor_scalar(rstd[:, m:m + 1], ss[:, m:m + 1], 1.0 / D, EPS, ALU.mult, ALU.add))
                nc.gpsimd.tensor_tensor(rstd[:, m:m + 1], rstd[:, m:m + 1], half[:, :], ALU.pow).then_inc(rstd_ready, 1)
                for i in (2 * m + 4, 2 * m + 5):
                    if i < 2 * TT:
                        gather(i)

        @block.vector
        def _(dve):
            def norm(m):
                dve.wait_ge(rstd_ready, m + 1)
                x = x_sb[:, m, :]
                nc.vector.scalar_tensor_tensor(x, x, rstd[:, m:m + 1], c.k["final_norm"][:, :], ALU.mult, ALU.mult).then_inc(normed, 1)

            for m in range(TT):
                for k in range(2):
                    i = 2 * m + k
                    dve.wait_ge(rows_there[i % 4], 16 * (i // 4 + 1))
                    if k:
                        dve.wait_ge(summed, i)
                    x = x_sb[:, m, :]
                    nc.vector.scalar_tensor_tensor(x, g[:, i % 4, :], weights[:, k, m:m + 1], x, ALU.mult, ALU.add).then_inc(summed, 1)
                if m:
                    norm(m - 1)
            norm(TT - 1)

        @block.scalar
        def _(act):
            for m in range(TT):
                act.wait_ge(summed, 2 * m + 2)
                if m >= 2:
                    act.wait_ge(squared, m - 1)
                nc.scalar.activation(junk[:, m % 2, :], x_sb[:, m, :], ACT.Square, accum_out=ss[:, m:m + 1]).then_inc(squared, 1)

        @block.sync
        def _(sp):
            for m in range(TT):
                sp.wait_ge(normed, m + 1)
                sp.dma_start(out[0, m * P:(m + 1) * P, :], x_sb[:, m, :]).then_inc(stored, 16)
            sp.wait_ge(stored, 16 * TT)


def recycle_semaphores(c, after=None):
    nc = c.nc
    ids = sorted(nc.released_uncleared_semaphores)
    with nc.Block() as block:
        @block.gpsimd
        def _(pl):
            if after is not None:
                pl.wait_ge(after, 16)
            start = 0
            for i in range(1, len(ids) + 1):
                if i == len(ids) or ids[i] != ids[i - 1] + 1:
                    pl.sem_clear(range(ids[start], ids[i - 1] + 1))
                    start = i


def build(nc, io, out):
    with ExitStack() as ctx:
        c = Chip(nc, ctx, io)
        load_consts(c, ctx, [("ident", [P, P]), ("ones", [P, P]), ("mask_le", [P, P]), ("mask_gt", [P, P])])
        x_rows, mem_rows = io["x"][0], io["mem"][0]

        hT = c.sb(ctx, "hT", [P, KT, S])
        x_sb = c.sb(ctx, "x", [P, TT, D])
        flat = x_sb[:, :, :].rearrange("p t n -> p (t n)")

        hmT = flat[:, 0:4 * S].rearrange("p (k n) -> p k n", k=4)
        memT = flat[:, 4 * S:6 * S].rearrange("p (k n) -> p k n", k=KT)
        hnT = flat[:, 4 * S:6 * S].rearrange("p (k n) -> p k n", k=2)
        hcT = flat[:, 6 * S:8 * S].rearrange("p (k n) -> p k n", k=2)
        first = ExitStack()
        load_consts(c, first, [
            ("pick8", [8, 8, P]), ("dir8", [8, 4]), ("b_if", [8, 2]), ("g_mix", [P, KT]), ("g_mem", [P, KT]),
            ("w_if", [P, KT, 16]), ("conv1", [P, 4, M_CONV]), ("conv1_b", [P, 4]), ("g_mlstm", [P, BANK]),
            ("g_ffn", [P, KT]), ("g_heads", [P, 8])])
        with ExitStack() as ml:
            qk_raw = c.sb(ml, "qk_raw", [P, 4, S + M_CONV - 1])
            v_sb = c.sb(ml, "v_m", [P, TT, M_HEADS, M_V + 1])
            og = c.sb(ml, "og", [P, TT, BANK])
            if_tok = c.sb(ml, "if_tok", [P, TT, 16])
            tiles = [(x_rows[i * P:(i + 1) * P, :], c.k["g_mix"], hT, i * P) for i in range(TT)]
            tiles += [(mem_rows[i * P:(i + 1) * P, :], c.k["g_mem"], memT, i * P) for i in range(MEM // P)]
            norm_transpose(c, "n1", tiles, RING, source="dram")
            mlstm_inputs(c, hT, qk_raw, v_sb, og, if_tok)
            mlstm(c, qk_raw, hmT, v_sb, og, if_tok)
        with ExitStack() as at:
            naT = c.sb(at, "naT", [P, 4, S])
            v_na = c.sb(at, "v_na", [P, TT, 256])
            qmT = c.sb(at, "qmT", [P, 2, S])
            kmT = c.sb(at, "kmT", [P, 2, MEM])
            v_mem = c.sb(at, "v_mem", [P, MEM // P, 256])
            na_tok = c.sb(at, "na_tok", [P, TT, 256])
            me_tok = c.sb(at, "me_tok", [P, TT, 256])
            attention_inputs(c, hT, memT, naT, v_na, qmT, kmT, v_mem)
            neighbourhood(c, naT, v_na, na_tok)
            memory_attention(c, qmT, kmT, v_mem, me_tok)
            transpose_tokens(c, "tr1", [(na_tok, hnT, 256), (me_tok, hcT, 256)])
        with ExitStack() as ff:
            yT = c.sb(ff, "yT", [P, KT, S])
            gated_branches(c, hT, [(hmT, io["w_proj_mlstm"]), (hnT, io["w_proj_na"]), (hcT, io["w_proj_mem"])], yT)
            project_add(c, "out1", yT, C_OUT, x_sb, first_load=x_rows)
            tiles = [(x_sb[:, i, :], c.k["g_ffn"], hT, i * P) for i in range(TT)]
            norm_transpose(c, "n2", tiles, 0)
            ffn(c, hT, x_sb, yT)
        first.close()
        recycle_semaphores(c)
        second = ExitStack()
        load_consts(c, second, [
            ("attn_norm", [P, KT]), ("level_masks", [P, LEVELS, P]), ("w_ba", [P, KT, 8]), ("conv2", [P, 12, A_CONV_K]),
            ("norm_a", [P, P]), ("norm_b", [P, BANK]), ("a_log", [P, 4]), ("dt_bias", [P, 4]), ("q_decay", [P, 4]),
            ("k_decay", [P, 4]), ("zeros", [P, 256])])
        y_rows = nc.dram_tensor("y_rows", (BLOCKS * ROWS, D), F32, kind="Internal").ap()
        x2_dram = nc.dram_tensor("x2_rows", (S, D), F32, kind="Internal").ap()
        tiles = [(x_sb[:, i, :], c.k["attn_norm"], hT, i * P) for i in range(TT)]
        norm_transpose(c, "n3", tiles, 0)
        rows_cleared = c.sem(ctx, "y_rows_cleared")
        spill(c, "x2", x_sb[:, :, :], x2_dram, clear=y_rows[N_EXPERTS * ROWS:, :], cleared=rows_cleared)
        o_a, o_b = x_sb[:, :, 0:BANK], x_sb[:, :, BANK:D]
        with ExitStack() as dr:
            qkv = c.sb(dr, "qkv_a", [P, TT, 3 * BANK])
            small = c.sb(dr, "beta_alpha", [P, TT, 8])
            ss = c.sb(dr, "dr_ss", [P, TT, 8])
            delta_inputs(c, hT, qkv, o_a, small, ss)
            delta_rule(c, qkv, o_a, small, ss, o_b)
        with ExitStack() as rt:
            q, k, v = (c.sb(rt, "rt_" + n, [P, TT, BANK]) for n in "qkv")
            with ExitStack() as tb:
                tables = c.sb(tb, "t_cos", [P, TT, P]), c.sb(tb, "t_sin", [P, TT, P])
                retention_inputs(c, hT, q, k, v, o_b, tables)
            retention(c, q, k, v, o_b)
        transpose_tokens(c, "tr2", [(o_a, hT[:, 0:4, :], BANK), (o_b, hT[:, 4:8, :], BANK)])
        project_add(c, "out2", hT, C_OUT2, x_sb, first_load=x2_dram)
        recycle_semaphores(c, after=rows_cleared)
        second.close()
        load_consts(c, ctx, [
            ("ffn_norm", [P, KT]), ("ffn_norm_row", [P, D]), ("final_norm", [P, D]), ("mask_lt", [P, P]),
            ("w_router", [P, KT, GR]), ("iota", [P, BLOCKS + 2]), ("iota_p", [P, 1]), ("thresholds", [P, 16]),
            ("token", [P, TT])])
        h_rows = nc.dram_tensor("h_rows", (S, D), F32, kind="Internal").ap()
        with ExitStack() as moe:
            weights = c.sb(moe, "mo_weights", [P, 2, TT])
            slots = c.sb(moe, "mo_slots", [P, 2 * TT], U32)
            perm = c.sb(moe, "mo_perm", [ROWS, BLOCKS + 2], U32)
            overflow = c.sb(moe, "mo_overflow", [1, PAIRS_AT + 1], I32)
            with ExitStack() as ex:
                wide = 3 * KT * D_EXPERT
                places = [hT[:, :, :].rearrange("p k n -> p (k n)"), c.ring[:, :, :, :].rearrange("p r k n -> p (r k n)")]
                places += [c.sb(ex, f"expert_{i}", [P, wide])[:, :] for i in range(2)]
                experts = Experts(c, ex, places)
                tiles = [(x_sb[:, i, :], c.k["ffn_norm"], hT, i * P) for i in range(TT)]
                norm_transpose(c, "n4", tiles, 0, keep=h_rows, keep_gain=c.k["ffn_norm_row"][:, :], experts=experts)
                route(c, hT, experts, weights, slots, perm, overflow)
                run_experts(c, experts, h_rows, y_rows, perm, overflow)
            combine(c, x_sb, y_rows, weights, slots, out)


def host_constants():
    k = {}
    k["k_ident"] = np.eye(P, dtype=np.float32)
    k["k_zeros"] = np.zeros((P, 256), np.float32)
    k["k_ones"] = np.ones((P, P), np.float32)
    pick = np.zeros((8, 8, P), np.float32)
    for r in range(8):
        pick[r, r, :] = 1.0
    k["k_pick8"] = pick
    dirs = np.zeros((8, 4), np.float32)
    dirs[0:4] = [-1.0, 0.0, 1.0, 0.0]
    dirs[4:8] = [1.0, -1.0, 0.0, 1.0]
    k["k_dir8"] = dirs
    i = np.arange(P)
    k["k_mask_le"] = (i[:, None] <= i[None]).astype(np.float32)
    k["k_mask_lt"] = (i[:, None] < i[None]).astype(np.float32)
    k["k_iota"] = np.tile(np.arange(BLOCKS + 2, dtype=np.float32), (P, 1))
    k["k_iota_p"] = i[:, None].astype(np.float32)
    k["k_thresholds"] = np.tile(np.array([ROWS * (j + 1) for j in range(16)], np.float32), (P, 1))
    k["k_token"] = (i[:, None] + P * np.arange(TT)[None]).astype(np.float32)
    k["k_mask_gt"] = (i[:, None] > i[None]).astype(np.float32)
    levels = [((i[:, None] >> (l + 1)) == (i[None] >> (l + 1))) & ((i[None] >> l) % 2 == 1) & ((i[:, None] >> l) % 2 == 0)
              for l in range(LEVELS)]
    k["k_level_masks"] = np.ascontiguousarray(np.stack(levels, axis=1).astype(np.float32))
    half = G_DIM // 2
    freq = np.float32(10000.0) ** (-np.arange(0, G_DIM, 2, dtype=np.float32) / np.float32(G_DIM))
    ang = (np.arange(S, dtype=np.float32)[:, None] * freq[None]).astype(np.float32)
    cos, sin = np.cos(ang).astype(np.float32), np.sin(ang).astype(np.float32)
    by_token = lambda a: np.ascontiguousarray(a.reshape(TT, P, -1).transpose(1, 0, 2))
    k["t_cos"] = by_token(np.concatenate([cos, cos], axis=1))
    k["t_sin"] = by_token(np.concatenate([-sin, sin], axis=1))
    gamma = np.array([retention_decay(h) for h in range(A_HEADS)])
    k["k_q_decay"] = (gamma[None] ** (i[:, None] + 1)).astype(np.float32)
    k["k_k_decay"] = (gamma[None] ** (P - 1 - i[:, None]) * G_DIM ** -0.5).astype(np.float32)
    table = gamma[None, :, None] ** -(i[:, None, None] + 1.0) * (i[:, None, None] <= i[None, None]) * G_DIM ** -0.5
    k["t_decay"] = np.ascontiguousarray(table.astype(np.float32))
    return k


def by_channel(g, tiles):
    return np.ascontiguousarray(np.asarray(g).reshape(tiles, P).T)


def rows(g):
    g = np.asarray(g).reshape(1, -1)
    return np.ascontiguousarray(np.repeat(g, P, axis=0))


def head_gains(a):
    names = ("g_na_q", "g_na_k", "g_mem_q", "g_mem_k")
    cols = [np.tile(a[n][0], P // a[n].shape[1]) for n in names for _ in range(2)]
    return np.ascontiguousarray(np.stack(cols, axis=1))


def window_bias(rpb):
    rows_n = S // GRID_W
    flat = rpb.reshape(NA_HEADS, -1)
    outside = flat.shape[1]
    flat = np.concatenate([flat, np.full((NA_HEADS, 1), -1.0e30, np.float32)], axis=1)
    index = np.full((P, NA_TABLE), outside, np.int64)
    p = np.arange(P)
    col = p % GRID_W
    c0 = np.clip(col - WIN_C // 2, 0, GRID_W - WIN_C)
    for t in [2] + NA_EDGE:
        k0, k1 = window_tiles(t)
        row = 2 * t + p // GRID_W
        r0 = np.clip(row - WIN_R // 2, 0, rows_n - WIN_R)
        key = k0 * P + np.arange((k1 - k0) * P)
        krow, kcol = key // GRID_W, key % GRID_W
        inside = ((krow[None] >= r0[:, None]) & (krow[None] < r0[:, None] + WIN_R)
                  & (kcol[None] >= c0[:, None]) & (kcol[None] < c0[:, None] + WIN_C))
        at = (krow[None] - row[:, None] + WIN_R - 1) * (2 * WIN_C - 1) + kcol[None] - col[:, None] + WIN_C - 1
        b = bias_at(t)
        index[:, b:b + len(key)] = np.where(inside, at, outside)
    return np.ascontiguousarray(flat[:, index])


def kernel(**inputs):
    import concourse.bacc as bacc
    from concourse.bass_utils import run_bass_kernel_spmd

    a = {k: np.asarray(v) for k, v in inputs.items()}
    arrays = host_constants()
    for name in ("x", "mem"):
        arrays[name] = a[name]
    for name in ("w_in", "w_proj_mlstm", "w_proj_na", "w_mem_kv", "w_proj_mem", "w_out", "w_up", "w_down",
                 "w_in_2", "w_out_2"):
        arrays[name] = a[name][0]
    arrays["k_b_if"] = np.ascontiguousarray(np.stack([a["b_igate"][0].reshape(8), a["b_fgate"][0].reshape(8)], axis=1))
    arrays["k_g_mix"] = by_channel(a["g_mix"][0], KT)
    arrays["k_g_mem"] = by_channel(a["g_mem"][0], KT)
    arrays["k_w_if"] = np.ascontiguousarray(a["w_in"][0][:, IN1["gates_if"]:IN1["gates_if"] + 16].reshape(KT, P, 16).transpose(1, 0, 2))
    arrays["k_conv1"] = np.ascontiguousarray(a["conv_w"][0].T.reshape(4, P, M_CONV).transpose(1, 0, 2))
    arrays["k_conv1_b"] = by_channel(a["conv_b"][0], 4)
    arrays["k_g_ffn"] = by_channel(a["g_ffn"][0], KT)
    arrays["k_g_heads"] = head_gains(a)
    arrays["na_bias"] = window_bias(a["rpb"][0])
    arrays["k_attn_norm"] = by_channel(a["attn_norm_2"][0], KT)
    arrays["k_w_ba"] = np.ascontiguousarray(
        a["w_in_2"][0][:, IN2["beta_alpha"]:IN2["beta_alpha"] + 8].reshape(KT, P, 8).transpose(1, 0, 2))
    arrays["k_conv2"] = np.ascontiguousarray(a["conv_a_2"][0].T.reshape(12, P, A_CONV_K).transpose(1, 0, 2))
    arrays["k_norm_a"] = rows(a["norm_a_2"][0])
    arrays["k_norm_b"] = rows(a["norm_b_2"][0])
    arrays["k_a_log"] = rows(a["a_log_2"][0])
    arrays["k_dt_bias"] = rows(a["dt_bias_2"][0])
    arrays["k_ffn_norm"] = by_channel(a["ffn_norm_2"][0], KT)
    arrays["k_ffn_norm_row"] = rows(a["ffn_norm_2"][0])
    arrays["k_final_norm"] = rows(a["final_norm_2"])
    router = np.concatenate([a["w_router_group_2"][0], a["w_router_expert_2"][0]], axis=1)
    arrays["k_w_router"] = np.ascontiguousarray(router.reshape(KT, P, GR).transpose(1, 0, 2))
    for name in ("w_gate_2", "w_up_2", "w_down_2"):
        arrays[name] = a[name][0]
    arrays["k_g_mlstm"] = rows(a["g_mlstm"][0])

    nc = bacc.Bacc("TRN2", target_bir_lowering=False, num_devices=1)
    feeds, io = {}, {}
    for name, v in arrays.items():
        v = np.ascontiguousarray(v)
        feeds["in_" + name] = v
        io[name] = nc.dram_tensor("in_" + name, v.shape, mybir.dt.from_np(v.dtype), kind="ExternalInput").ap()
    out = nc.dram_tensor("out", (1, S, D), F32, kind="ExternalOutput").ap()
    build(nc, io, out)
    r = run_bass_kernel_spmd(nc, [feeds], core_ids=[0])
    return r.results[0]["out"]
```

```python
from contextlib import ExitStack

import numpy as np

import concourse.bass as bass
from concourse import mybir

ALU = mybir.AluOpType
ACT = mybir.ActivationFunctionType
AX = mybir.AxisListType
F32 = mybir.dt.float32
I32 = mybir.dt.int32
U32 = mybir.dt.uint32
F32R = mybir.dt.float32r

P = 128
BANK = 512
D = 1024
S = 1024
KT = D // P
TT = S // P
MEM = 256
EPS = 1e-6
D_FF = 4096

M_HEADS, M_QK, M_V, M_CONV = 4, 64, 128, 5
NA_HEADS, NA_HD, GRID_W, WIN_R, WIN_C = 8, 32, 64, 8, 16
MEM_HEADS, MEM_HD = 4, 64
A_HEADS, A_CONV_K = 4, 4
G_DIM = 128
N_EXPERTS, N_GROUPS, PER_GROUP, D_EXPERT = 64, 8, 8, 256

RING = 2
HALF = BANK // 2


class Steps:

    def __init__(self, nc, ctx, name):
        self.sem = ctx.enter_context(nc.semaphore(name))
        self.count = 0

    def done(self, ins):
        ins.then_inc(self.sem, 1)
        self.count += 1
        return ins

    def settle(self, eng):
        eng.wait_ge(self.sem, self.count)

    def then_wait(self, eng, ins):
        self.done(ins)
        self.settle(eng)


class Chip:

    def __init__(self, nc, ctx, io):
        self.nc, self.io, self.ctx = nc, io, ctx
        self.psum = ctx.enter_context(nc.psum_tensor("banks", [P, 8, BANK], F32))
        self.raw = ctx.enter_context(nc.sbuf_tensor("raw_weights", [P, KT, HALF], F32))
        self.raw_landed = ctx.enter_context(nc.semaphore("raw_weights_landed"))
        self.landed = [ctx.enter_context(nc.semaphore(f"weights_landed_{i}")) for i in range(RING)]
        self.used = ctx.enter_context(nc.semaphore("weights_used"))
        self.chunks = weight_chunks(io)
        self.loaded = 0
        self.consts_landed = ctx.enter_context(nc.semaphore("consts_landed"))
        self.n_consts = 0
        self.k = {}
        self.upper_done = ctx.enter_context(nc.semaphore("weights_upper_parts_done"))
        self.split_done = ctx.enter_context(nc.semaphore("weights_split"))

    def bank(self, i, n=BANK, parts=P):
        return self.psum[0:parts, i, 0:n]

    def sb(self, mem, name, shape, dt=F32):
        return mem.enter_context(self.nc.sbuf_tensor(name, shape, dt))

    def sem(self, mem, name):
        return mem.enter_context(self.nc.semaphore(name))

    def load_chunks(self, sp, upto):
        while self.loaded < min(upto, len(self.chunks)):
            j = self.loaded
            src, kt, n = self.chunks[j]
            if j < C_BRANCH:
                if j >= RING:
                    sp.wait_ge(self.used, j - RING + 1)
                sp.dma_start(self.ring[:, j % RING, 0:kt, 0:n], src).then_inc(self.landed[j % RING], 16)
            else:
                if j > C_BRANCH:
                    sp.wait_ge(self.split_done, j - C_BRANCH)
                sp.dma_start(self.raw[:, :, :], src).then_inc(self.raw_landed, 16)
            self.loaded += 1

    def wait_chunk(self, pe, j):
        pe.wait_ge(self.landed[j % RING], 16 * (j // RING + 1))

    def chunk(self, j):
        return self.ring[:, j % RING, :, :]

    def parts(self, j):
        return [self.split_ring[:, j % RING, i, :, :] for i in range(2)]

    def split_chunk(self, dve, j):
        if j >= len(self.chunks):
            return
        upper, lower = self.parts(j)
        dve.wait_ge(self.raw_landed, 16 * (j - C_BRANCH + 1))
        if j >= C_BRANCH + RING:
            dve.wait_ge(self.used, j - RING + 1)
        take_upper(self.nc.vector, upper, self.raw[:, :, :]).then_inc(self.upper_done, 1)
        dve.wait_ge(self.upper_done, j - C_BRANCH + 1)
        take_lower(self.nc.vector, lower, self.raw[:, :, :], upper).then_inc(self.split_done, 1)

    def wait_split(self, pe, j):
        pe.wait_ge(self.split_done, j - C_BRANCH + 1)


def take_upper(engine, dst, src):
    return engine.tensor_copy(dst.bitcast(F32R), src)


def take_lower(engine, dst, whole, upper):
    return engine.tensor_tensor(dst.bitcast(F32R), whole, upper, ALU.subtract)


def split(dve, vector, steps, whole, upper, lower):
    steps.then_wait(dve, take_upper(vector, upper, whole))
    return take_lower(vector, lower, whole, upper)


IN1 = dict(qk=0, v=512, o=1024, gates_if=1536, na_qk=1552, na_v_qmem=2064, branch=2576)
IN2 = dict(q=0, k=512, v=1024, g=1536, beta_alpha=2048, qb=2056, kb=2568, vb=3080, gb=3592)
C_QK, C_V, C_O, C_NAQK, C_NAV, C_MEMKV = range(6)
C_BRANCH = 6
C_OUT = C_BRANCH + 12
C_FFN = C_OUT + 4
C_IN2 = C_FFN + 32
C_OUT2 = C_IN2 + 16


def weight_chunks(io):
    def cols(w, c, n=BANK):
        return (w[:, c:c + n].rearrange("(k p) n -> p k n", p=P), w.shape[0] // P, n)

    w1, w2 = io["w_in"], io["w_in_2"]
    out = [cols(w1, IN1[k]) for k in ("qk", "v", "o", "na_qk", "na_v_qmem")]
    out.append(cols(io["w_mem_kv"], 0))
    out += [cols(w1, IN1["branch"] + b * D + n * HALF, HALF) for n in range(4) for b in range(3)]
    out += [cols(io["w_out"], n * HALF, HALF) for n in range(4)]
    for f in range(D_FF // D):
        out += [cols(io["w_up"], f * D + n * HALF, HALF) for n in range(4)]
        out += [cols(io["w_down"][f * D:(f + 1) * D, :], n * HALF, HALF) for n in range(4)]
    out += [cols(w2, IN2[k] + n * HALF, HALF) for k in ("q", "k", "v", "g", "qb", "kb", "vb", "gb") for n in range(2)]
    out += [cols(io["w_out_2"], n * HALF, HALF) for n in range(4)]
    return out


def load_consts(c, mem, sizes):
    nc = c.nc
    for name, shape in sizes:
        c.k[name] = c.sb(mem, "c_" + name, shape)

    def load(eng, part):
        for name, shape in part:
            eng.dma_start(c.k[name][tuple(slice(None) for _ in shape)], c.io["k_" + name]).then_inc(c.consts_landed, 16)

    c.n_consts += len(sizes)
    with nc.Block() as block:
        @block.sync
        def _(sp):
            load(sp, sizes[0::2])

        @block.scalar
        def _(act):
            load(act, sizes[1::2])
            act.wait_ge(c.consts_landed, 16 * c.n_consts)


def norm_transpose(c, name, tiles, prefetch, source=None, keep=None, keep_gain=None, experts=None, upper=None, then_split=None):
    nc, n = c.nc, len(tiles)
    XS, XN, NB = 3, 2, 4
    with ExitStack() as mem:
        loads = source == "dram"
        if loads:
            xs = c.sb(mem, name + "_x", [P, XS, D])
            landed = [c.sem(mem, f"{name}_x_landed_{i}") for i in range(XS)]
        junk = c.sb(mem, name + "_squares", [P, 2, D])
        xn = c.sb(mem, name + "_xn", [P, XN, D])
        ss = c.sb(mem, name + "_ss", [P, n])
        ms = c.sb(mem, name + "_ms", [P, n])
        rstd = c.sb(mem, name + "_rstd", [P, n])
        half = c.sb(mem, name + "_half", [P, 1])
        squared = c.sem(mem, name + "_squared")
        rstd_ready = c.sem(mem, name + "_rstd_ready")
        normed = c.sem(mem, name + "_normed")
        transposed = c.sem(mem, name + "_transposed")
        copied = c.sem(mem, name + "_copied")
        if upper is not None:
            upper_taken = c.sem(mem, name + "_upper_taken")
        if keep is not None:
            kt = c.sb(mem, name + "_kept_tiles", [P, 2, D])
            kept = c.sem(mem, name + "_kept")
            kept_stored = [c.sem(mem, f"{name}_kept_stored_{i}") for i in range(2)]
        pool = Steps(nc, mem, name + "_pool_steps")

        def tile(i):
            return xs[:, i % XS, :] if loads else tiles[i][0]

        def x_there(eng, i):
            if loads:
                eng.wait_ge(landed[i % XS], 16 * (i // XS + 1))

        block = mem.enter_context(nc.Block())

        @block.sync
        def _(sp):
            if loads:
                for i in range(n):
                    if i >= XS:
                        sp.wait_ge(normed, i - XS + 1)
                    sp.dma_start(xs[:, i % XS, :], tiles[i][0]).then_inc(landed[i % XS], 16)
            c.load_chunks(sp, prefetch)
            if keep is not None:
                for i in range(n):
                    sp.wait_ge(kept, i + 1)
                    sp.dma_start(keep[i * P:(i + 1) * P, :], kt[:, i % 2, :]).then_inc(kept_stored[i % 2], 16)
                for i in range(2):
                    sp.wait_ge(kept_stored[i], 16 * (n // 2))
                for i in range(1, SLOTS):
                    experts.load(sp, i, i)

        @block.scalar
        def _(act):
            for i in range(n):
                x_there(act, i)
                if i >= 2:
                    act.wait_ge(squared, i - 1)
                nc.scalar.activation(junk[:, i % 2, :], tile(i), ACT.Square, accum_out=ss[:, i:i + 1]).then_inc(squared, 1)

        @block.gpsimd
        def _(pl):
            pool.then_wait(pl, nc.gpsimd.memset(half[:, :], -0.5))
            for i in range(n):
                pl.wait_ge(squared, i + 1)
                pool.then_wait(pl, nc.gpsimd.tensor_scalar(ms[:, i:i + 1], ss[:, i:i + 1], 1.0 / D, EPS, ALU.mult, ALU.add))
                nc.gpsimd.tensor_tensor(rstd[:, i:i + 1], ms[:, i:i + 1], half[:, :], ALU.pow).then_inc(rstd_ready, 1)

        @block.vector
        def _(dve):
            def copy(i):
                _, gain, dst, at = tiles[i]
                for g in range(2):
                    dve.wait_ge(transposed, 2 * i + g + 1)
                    if upper is not None:
                        take_upper(nc.vector, upper[:, 4 * g:4 * g + 4, at:at + P],
                                   c.bank((2 * i + g) % NB).rearrange("p (a b) -> p a b", a=4)).then_inc(upper_taken, 1)
                        dve.wait_ge(upper_taken, 2 * i + g + 1)
                        take_lower(nc.vector, dst[:, 4 * g:4 * g + 4, at:at + P],
                                   c.bank((2 * i + g) % NB).rearrange("p (a b) -> p a b", a=4),
                                   upper[:, 4 * g:4 * g + 4, at:at + P]).then_inc(copied, 1)
                        continue
                    nc.vector.tensor_tensor(
                        dst[:, 4 * g:4 * g + 4, at:at + P],
                        c.bank((2 * i + g) % NB).rearrange("p (a b) -> p a b", a=4),
                        gain[:, 4 * g:4 * g + 4].unsqueeze(2).to_broadcast([P, 4, P]),
                        ALU.mult).then_inc(copied, 1)

            for i in range(n):
                dve.wait_ge(rstd_ready, i + 1)
                if i >= XN:
                    dve.wait_ge(transposed, 2 * (i - XN + 1))
                if upper is None:
                    nc.vector.tensor_scalar(xn[:, i % XN, :], tile(i), rstd[:, i:i + 1], None, ALU.mult).then_inc(normed, 1)
                else:
                    nc.vector.scalar_tensor_tensor(xn[:, i % XN, :], tile(i), rstd[:, i:i + 1], tiles[i][1], ALU.mult, ALU.mult).then_inc(normed, 1)
                if keep is not None:
                    dve.wait_ge(normed, i + 1)
                    if i >= 2:
                        dve.wait_ge(kept_stored[i % 2], 16 * (i // 2))
                    nc.vector.tensor_tensor(kt[:, i % 2, :], xn[:, i % XN, :], keep_gain, ALU.mult).then_inc(kept, 1)
                if i:
                    copy(i - 1)
            copy(n - 1)
            if then_split is not None:
                c.split_chunk(dve, then_split)

        @block.tensor
        def _(pe):
            for i in range(n):
                pe.wait_ge(normed, i + 1)
                for g in range(2):
                    b = 2 * i + g
                    if b >= NB:
                        pe.wait_ge(copied, b - NB + 1)
                    for k in range(4):
                        last = nc.tensor.transpose(c.bank(b % NB)[:, k * P:(k + 1) * P],
                                                   xn[:, i % XN, (4 * g + k) * P:(4 * g + k + 1) * P], c.k["ident"][:, :])
                    last.then_inc(transposed, 1)


def mm_tokens(pe, out, acts, m, w, kt=KT):
    for k in range(kt):
        last = pe.matmul(out, acts[:, k, m * P:(m + 1) * P], w[:, k, :], start=(k == 0), stop=(k == kt - 1))
    return last


def mm_channels(pe, out, acts, t0, nt, w, c0, kt=KT):
    for k in range(kt):
        last = pe.matmul(out, w[:, k, c0:c0 + P], acts[:, k, t0:t0 + nt], start=(k == 0), stop=(k == kt - 1))
    return last


PASSES = ((0, 0), (0, 1), (1, 0))


def split_tokens(pe, bank, acts, pair, w, kt=KT):
    for a in range(2):
        m = 2 * pair + a
        for k in range(kt):
            for x, y in PASSES:
                last = pe.matmul(bank[:, a * HALF:(a + 1) * HALF], acts[x][:, k, m * P:(m + 1) * P].bitcast(F32R),
                                 w[y][:, k, :].bitcast(F32R), start=(k == 0 and x == y), stop=(k == kt - 1 and x == 1))
    return last


def split_channels(pe, out, acts, t0, nt, w, c0, kt=KT):
    for k in range(kt):
        for x, y in PASSES:
            last = pe.matmul(out, w[x][:, k, c0:c0 + P].bitcast(F32R), acts[y][:, k, t0:t0 + nt].bitcast(F32R),
                             start=(k == 0 and x == y), stop=(k == kt - 1 and x == 1))
    return last


def mlstm_inputs(c, hT, qk_raw, qkT, v_sb, og, row):
    nc = c.nc
    PAD = M_CONV // 2
    NB = 6
    WIDTH = 40
    with ExitStack() as mem:
        product = c.sem(mem, "in1_product")
        copied = c.sem(mem, "in1_copied")
        rows_taken = c.sem(mem, "in1_rows_taken")
        padded = c.sem(mem, "in1_padded")
        conv_done = c.sem(mem, "in1_conv_done")
        silu_done = c.sem(mem, "in1_silu_done")
        x_ready = c.sem(mem, "in1_x_ready")
        logf_ready = c.sem(mem, "in1_logf_ready")
        m_ready = c.sem(mem, "in1_m_ready")
        s_dve = Steps(nc, mem, "in1_dve_steps")
        s_act = Steps(nc, mem, "in1_act_steps")
        block = mem.enter_context(nc.Block())
        I, X, T1, DCUM, A, M = range(6)

        @block.sync
        def _(sp):
            c.load_chunks(sp, C_O + 1 + RING)

        @block.tensor
        def _(pe):
            g = 0

            def fresh_bank():
                if NB <= g < NB + 2:
                    pe.wait_ge(rows_taken, g - NB + 1)
                elif g >= NB:
                    pe.wait_ge(copied, g - NB - 2 + 1)
                return c.bank(g % NB)

            for th in range(2):
                for k in range(KT):
                    last = nc.tensor.matmul(fresh_bank()[0:WIDTH, :], c.k["w_if"][:, k, :], hT[:, k, th * BANK:(th + 1) * BANK],
                                            start=(k == 0), stop=(k == KT - 1))
                last.then_inc(product, 1)
                g += 1
            c.wait_chunk(pe, C_QK)
            for ch in range(4):
                for th in range(2):
                    last = mm_channels(nc.tensor, fresh_bank(), hT, th * BANK, BANK, c.chunk(C_QK), ch * P)
                    last.then_inc(product, 1)
                    g += 1
            for j in (C_V, C_O):
                c.wait_chunk(pe, j)
                for m in range(TT):
                    last = mm_tokens(nc.tensor, fresh_bank(), hT, m, c.chunk(j))
                    last.then_inc(product, 1)
                    g += 1

        @block.scalar
        def _(act):
            for i in range(24):
                g = i + 2
                if i == 4:
                    act.wait_ge(x_ready, 1)
                    s_act.then_wait(act, nc.scalar.activation(row(T1), row(T1), ACT.Exp, scale=-1.0))
                    nc.scalar.activation(row(T1), row(T1), ACT.Ln, bias=1.0).then_inc(logf_ready, 1)
                if i == 15:
                    act.wait_ge(m_ready, 1)
                    nc.scalar.activation(row(T1), row(T1), ACT.Exp)
                    for ch in range(4):
                        act.wait_ge(conv_done, ch + 1)
                        nc.scalar.activation(qkT[:, ch, :], qkT[:, ch, :], ACT.Silu, bias=c.k["conv1_b"][:, ch:ch + 1]).then_inc(silu_done, 1)
                act.wait_ge(product, g + 1)
                if i in (7, 15, 23):
                    act.sem_inc(c.used, 1)
                b = c.bank(g % NB)
                if i < 8:
                    dst = qk_raw[:, i // 2, PAD + (i % 2) * BANK:PAD + (i % 2 + 1) * BANK]
                elif i < 16:
                    dst, b = v_sb[:, i - 8, :, 0:M_V], b.rearrange("p (h v) -> p h v", h=M_HEADS)
                else:
                    dst = og[:, i - 16, :]
                nc.scalar.activation(dst, b, ACT.Sigmoid if i >= 16 else ACT.Copy).then_inc(copied, 1)

        @block.vector
        def _(dve):
            s_dve.done(nc.vector.memset(qk_raw[:, :, 0:PAD], 0.0))
            s_dve.done(nc.vector.memset(qk_raw[:, :, PAD + S:], 0.0))
            nc.vector.memset(v_sb[:, :, :, M_V:M_V + 1], 1.0)
            for th in range(2):
                cols = slice(th * BANK, (th + 1) * BANK)
                dve.wait_ge(product, th + 1)
                s_dve.done(nc.vector.tensor_scalar(row(I)[:, cols], c.bank(th, parts=8), c.k["b_if"][:, 0:1], None, ALU.add))
                nc.vector.tensor_copy(row(X)[:, cols], c.psum[32:40, th, :]).then_inc(rows_taken, 1)
            dve.wait_ge(rows_taken, 2)
            s_dve.then_wait(dve, nc.vector.tensor_scalar(row(X), row(X), c.k["b_if"][:, 1:2], None, ALU.add))
            nc.vector.scalar_tensor_tensor(row(T1), row(X), -1.0, row(X), ALU.mult, ALU.max).then_inc(x_ready, 1)
            dve.wait_ge(logf_ready, 1)
            s_dve.then_wait(dve, nc.vector.scalar_tensor_tensor(row(X), row(X), 0.0, row(T1), ALU.min, ALU.subtract))
            s_dve.then_wait(dve, nc.vector.tensor_tensor_scan(row(DCUM), c.k["ones"][0:8, 0:1].to_broadcast([8, S]), row(X), 0.0, ALU.mult, ALU.add))
            s_dve.then_wait(dve, nc.vector.scalar_tensor_tensor(row(DCUM), row(X), c.k["dir8"][:, 1:2], row(DCUM), ALU.mult, ALU.add))
            s_dve.then_wait(dve, nc.vector.scalar_tensor_tensor(row(A), row(DCUM), c.k["dir8"][:, 0:1], row(I), ALU.mult, ALU.add))
            s_dve.done(nc.vector.tensor_tensor_scan(row(T1), row(A), row(A), -3.0e38, ALU.max, ALU.max))
            s_dve.done(nc.vector.tensor_tensor_scan(row(X)[:, ::-1], row(A)[:, ::-1], row(A)[:, ::-1], -3.0e38, ALU.max, ALU.max))
            s_dve.settle(dve)
            s_dve.then_wait(dve, nc.vector.tensor_scalar(row(T1), row(T1), c.k["dir8"][:, 2:3], None, ALU.mult))
            s_dve.then_wait(dve, nc.vector.scalar_tensor_tensor(row(M), row(X), c.k["dir8"][:, 3:4], row(T1), ALU.mult, ALU.add))
            nc.vector.scalar_tensor_tensor(row(T1), row(DCUM), c.k["dir8"][:, 0:1], row(M), ALU.mult, ALU.subtract).then_inc(m_ready, 1)
            dve.wait_ge(copied, 8)
            for ch in range(4):
                for i in range(M_CONV):
                    src = qk_raw[:, ch, i:i + S]
                    if i == 0:
                        ins = nc.vector.tensor_scalar(qkT[:, ch, :], src, c.k["conv1"][:, ch, 0:1], None, ALU.mult)
                    else:
                        ins = nc.vector.scalar_tensor_tensor(qkT[:, ch, :], src, c.k["conv1"][:, ch, i:i + 1],
                                                             qkT[:, ch, :], ALU.mult, ALU.add)
                    if i < M_CONV - 1:
                        s_dve.then_wait(dve, ins)
                ins.then_inc(conv_done, 1)
            for m in range(TT):
                dve.wait_ge(copied, 16 + m + 1)
                nc.vector.tensor_tensor(og[:, m, :], og[:, m, :], c.k["g_mlstm"][:, :], ALU.mult)


def mlstm(c, qk_raw, qkT, v_sb, og, m_row, Pt, row, q_wide):
    nc = c.nc
    PAD = M_CONV // 2
    with ExitStack() as mem:
        a_col = c.sb(mem, "ml_a_col", [P, TT, 8])
        em_col = c.sb(mem, "ml_em_col", [P, TT, 8])
        r_den = c.sb(mem, "ml_den", [P, 2, 2])
        ss = c.sb(mem, "ml_ss", [P, TT * M_HEADS])
        ms = c.sb(mem, "ml_ms", [P, TT * M_HEADS])
        rstd = c.sb(mem, "ml_rstd", [P, TT * M_HEADS])
        junk = c.sb(mem, "ml_junk", [P, M_V])
        half = c.sb(mem, "ml_half", [P, 1])
        hs = qk_raw[:, :, PAD:PAD + S].rearrange("p c (t n) -> p c t n", n=BANK)

        s_dve = Steps(nc, mem, "ml_dve_steps")
        s_act = Steps(nc, mem, "ml_act_steps")
        s_pool = Steps(nc, mem, "ml_pool_steps")
        q_widened = c.sem(mem, "ml_q_widened")
        cols_there = c.sem(mem, "ml_cols_there")
        cols_copied = c.sem(mem, "ml_cols_copied")
        mrow_there = c.sem(mem, "ml_mrow_there")
        exp_done = c.sem(mem, "ml_exp_done")
        masked = c.sem(mem, "ml_masked")
        scores_there = c.sem(mem, "ml_scores_there")
        weighted = c.sem(mem, "ml_weighted")
        out_there = c.sem(mem, "ml_out_there")
        out_taken = c.sem(mem, "ml_out_taken")
        rstd_ready = c.sem(mem, "ml_rstd_ready")
        ss_ready = c.sem(mem, "ml_ss_ready")
        gated = c.sem(mem, "ml_gated")
        hT_there = c.sem(mem, "ml_hT_there")
        hT_copied = c.sem(mem, "ml_hT_copied")
        I, X, T1, DCUM, A, M = range(6)

        def w_at(d, j, t):
            base = j * (TT + 1) * P
            return base + t * P if d == 1 else base + (j + 1) * P + (t - j) * P

        def out_index(h, d, t):
            return (2 * h + d) * TT + t

        def copy_out(dve, m):
            dve.wait_ge(hT_there, m + 1)
            nc.vector.tensor_copy(qkT[:, :, m * P:(m + 1) * P],
                                  c.bank(m % 2).rearrange("p (a b) -> p a b", a=4)).then_inc(hT_copied, 1)

        block = mem.enter_context(nc.Block())

        @block.tensor
        def _(pe):
            for which, r in ((0, A), (1, T1)):
                for m in range(TT):
                    last = nc.tensor.transpose(c.bank(4)[:, which * 64 + m * 8:which * 64 + m * 8 + 8],
                                               row(r)[:, m * P:(m + 1) * P], c.k["ident"][0:8, 0:8])
            last.then_inc(cols_there, 1)

            def m_rows(h):
                if h:
                    pe.wait_ge(exp_done, 2 * TT * h)
                for d in range(2):
                    for th in range(2):
                        last = nc.tensor.matmul(c.bank(2 * d + th), c.k["pick8"][:, d * 4 + h, :],
                                                row(M)[:, th * BANK:(th + 1) * BANK], start=True, stop=True)
                last.then_inc(mrow_there, 1)

            def values(h, d, t):
                n = out_index(h, d, t)
                if n >= 2:
                    pe.wait_ge(out_taken, n - 1)
                js = range(t + 1) if d == 0 else range(t, TT)
                for j in js:
                    at = w_at(d, j, t)
                    last = nc.tensor.matmul(c.bank(6 + n % 2)[:, 0:M_V + 1], Pt[:, at:at + P],
                                            v_sb[:, j, h, :], start=(j == js[0]), stop=(j == js[-1]))
                last.then_inc(out_there, 1)

            m_rows(0)
            for h in range(M_HEADS):
                pe.wait_ge(q_widened, h + 1)
                for j in range(TT):
                    n = h * TT + j
                    if n:
                        pe.wait_ge(weighted, 2 * n)
                    else:
                        pe.wait_ge(cols_copied, 2)
                    for th in range(2):
                        last = nc.tensor.matmul(c.bank(4 + th), qkT[:, 2 + h // 2, j * P:(j + 1) * P],
                                                q_wide[:, h % 2, th * BANK:(th + 1) * BANK], start=True, stop=True)
                    last.then_inc(scores_there, 1)
                    if j:
                        values(h, 0, j - 1)
                pe.wait_ge(weighted, 2 * TT * (h + 1))
                values(h, 0, TT - 1)
                if h + 1 < M_HEADS:
                    m_rows(h + 1)
                for t in range(TT):
                    values(h, 1, t)
            for m in range(TT):
                pe.wait_ge(gated, m + 1)
                if m >= 2:
                    pe.wait_ge(hT_copied, m - 1)
                for k in range(4):
                    last = nc.tensor.transpose(c.bank(m % 2)[:, k * P:(k + 1) * P],
                                               hs[:, m // 2, m % 2, k * P:(k + 1) * P], c.k["ident"][:, :])
                last.then_inc(hT_there, 1)

        @block.vector
        def _(dve):
            dve.wait_ge(cols_there, 1)
            nc.vector.tensor_copy(a_col[:, :, :], c.bank(4)[:, 0:64].rearrange("p (t c) -> p t c", c=8)).then_inc(cols_copied, 1)
            nc.vector.tensor_copy(em_col[:, :, :], c.bank(4)[:, 64:128].rearrange("p (t c) -> p t c", c=8)).then_inc(cols_copied, 1)

            def finish(h, d, t):
                n = out_index(h, d, t)
                dve.wait_ge(out_there, n + 1)
                o, r = c.bank(6 + n % 2), r_den[:, n % 2, 0:1]
                s_dve.then_wait(dve, nc.vector.scalar_tensor_tensor(r, o[:, M_V:M_V + 1], -1.0, em_col[:, t, 4 * d + h:4 * d + h + 1],
                                                                    ALU.mult, ALU.max))
                s_dve.then_wait(dve, nc.vector.tensor_tensor(r, o[:, M_V:M_V + 1], r, ALU.max))
                s_dve.then_wait(dve, nc.vector.reciprocal(r, r))
                dst = hs[:, t // 2, t % 2, h * M_V:(h + 1) * M_V]
                if d == 0:
                    nc.vector.tensor_scalar(dst, o[:, 0:M_V], r, None, ALU.mult).then_inc(out_taken, 1)
                else:
                    dve.wait_ge(out_taken, out_index(h, 0, t) + 1)
                    nc.vector.scalar_tensor_tensor(dst, o[:, 0:M_V], r, dst, ALU.mult, ALU.add).then_inc(out_taken, 1)

            for h in range(M_HEADS):
                for j in range(TT):
                    n = h * TT + j
                    dve.wait_ge(scores_there, n + 1)
                    dve.wait_ge(masked, 2 * n + 2)
                    base = j * (TT + 1) * P
                    back = Pt[:, base:base + (j + 1) * P]
                    nc.vector.scalar_tensor_tensor(
                        back, c.psum[:, 4:6, :].rearrange("p b n -> p (b n)")[:, 0:(j + 1) * P],
                        M_QK ** -0.5, back, ALU.mult, ALU.mult).then_inc(weighted, 1)
                    forth = Pt[:, base + (j + 1) * P:base + (TT + 1) * P]
                    nc.vector.scalar_tensor_tensor(
                        forth, c.psum[:, 4:6, :].rearrange("p b n -> p (b n)")[:, j * P:],
                        M_QK ** -0.5, forth, ALU.mult, ALU.mult).then_inc(weighted, 1)
                    if j:
                        finish(h, 0, j - 1)
                finish(h, 0, TT - 1)
                for t in range(TT):
                    finish(h, 1, t)
            for t in range(TT):
                dve.wait_ge(rstd_ready, 1)
                for h in range(M_HEADS):
                    dst = hs[:, t // 2, t % 2, h * M_V:(h + 1) * M_V]
                    i = h * TT + t
                    ins = nc.vector.scalar_tensor_tensor(dst, dst, rstd[:, i:i + 1], og[:, t, h * M_V:(h + 1) * M_V],
                                                         ALU.mult, ALU.mult)
                ins.then_inc(gated, 1)
                if t:
                    copy_out(dve, t - 1)
            copy_out(dve, TT - 1)

        @block.scalar
        def _(act):
            act.wait_ge(cols_copied, 1)

            def squares(h):
                for t in range(TT):
                    i = h * TT + t
                    act.wait_ge(out_taken, out_index(h, 1, t) + 1)
                    s_act.settle(act)
                    s_act.done(nc.scalar.activation(junk[:, :], hs[:, t // 2, t % 2, h * M_V:(h + 1) * M_V], ACT.Square,
                                                    accum_out=ss[:, i:i + 1]))

            for h in range(M_HEADS):
                act.wait_ge(mrow_there, h + 1)
                for j in range(TT):
                    if h:
                        act.wait_ge(out_taken, out_index(h - 1, 1, j) + 1)
                    base = j * (TT + 1) * P
                    for d, at, lo, hi in ((1, base, 0, (j + 1) * P), (0, base + (j + 1) * P, j * P, S)):
                        nc.scalar.activation(
                            Pt[:, at:at + hi - lo],
                            c.psum[:, 2 * d:2 * d + 2, :].rearrange("p b n -> p (b n)")[:, lo:hi],
                            ACT.Exp, bias=a_col[:, j, d * 4 + h:d * 4 + h + 1], scale=-1.0).then_inc(exp_done, 1)
                if h:
                    squares(h - 1)
            squares(M_HEADS - 1)
            s_act.settle(act)
            nc.scalar.activation(ms[:, :], ss[:, :], ACT.Copy, scale=1.0 / M_V).then_inc(ss_ready, 1)

        @block.gpsimd
        def _(pl):
            s_pool.done(nc.gpsimd.memset(q_wide, 0.0))
            s_pool.then_wait(pl, nc.gpsimd.memset(half[:, :], -0.5))

            def widen(h):
                hp = M_QK * (h % 2)
                if h >= 2:
                    pl.wait_ge(scores_there, TT * (h - 1))
                nc.gpsimd.tensor_copy(q_wide[hp:hp + M_QK, h % 2, :], qkT[hp:hp + M_QK, h // 2, :]).then_inc(q_widened, 1)
                pl.wait_ge(q_widened, h + 1)

            widen(0)
            for h in range(M_HEADS):
                for j in range(TT):
                    if j == 4 and h + 1 < M_HEADS:
                        pl.wait_ge(masked, 2 * (h * TT + j))
                        widen(h + 1)
                    n = h * TT + j
                    pl.wait_ge(exp_done, 2 * n + 1)
                    at = w_at(1, j, j)
                    nc.gpsimd.affine_select(out=Pt[:, at:at + P], in_=Pt[:, at:at + P], compare_op=ALU.is_ge, fill=0.0,
                                            base=0, pattern=[[-1, P]], channel_multiplier=1).then_inc(masked, 1)
                    pl.wait_ge(exp_done, 2 * n + 2)
                    at = w_at(0, j, j)
                    nc.gpsimd.affine_select(out=Pt[:, at:at + P], in_=Pt[:, at:at + P], compare_op=ALU.is_ge, fill=0.0,
                                            base=0, pattern=[[1, P]], channel_multiplier=-1).then_inc(masked, 1)
            pl.wait_ge(ss_ready, 1)
            s_pool.then_wait(pl, nc.gpsimd.tensor_scalar(ms[:, :], ms[:, :], EPS, None, ALU.add))
            nc.gpsimd.tensor_tensor(rstd[:, :], ms[:, :], half[:, :].to_broadcast([P, TT * M_HEADS]), ALU.pow).then_inc(rstd_ready, 1)


def attention_inputs(c, hT, memT, naT, v_na, qmT, kmT, v_mem):
    nc = c.nc
    units = [(C_NAQK, hT, m, 512, NA_HD, naT, 0) for m in range(TT)]
    units += [(C_NAV, hT, m, 256, MEM_HD, qmT, 4) for m in range(TT)]
    units += [(C_MEMKV, memT, m, 256, MEM_HD, kmT, 6) for m in range(MEM // P)]
    n = len(units)
    NB, NR, G = 4, 3, 512 // NA_HD
    with ExitStack() as mem:
        raw = c.sb(mem, "at_raw", [P, NR, BANK])
        sq = c.sb(mem, "at_squares", [P, NR, BANK])
        ss = c.sb(mem, "at_ss", [P, n, G])
        ms = c.sb(mem, "at_ms", [P, n, G])
        rstd = c.sb(mem, "at_rstd", [P, n, G])
        half = c.sb(mem, "at_half", [P, 1])
        pool = Steps(nc, mem, "at_pool_steps")
        product = c.sem(mem, "at_product")
        taken = c.sem(mem, "at_taken")
        summed = c.sem(mem, "at_summed")
        rstd_ready = c.sem(mem, "at_rstd_ready")
        normed = c.sem(mem, "at_normed")
        turned = c.sem(mem, "at_turned")
        turned_copied = c.sem(mem, "at_turned_copied")
        block = mem.enter_context(nc.Block())

        @block.sync
        def _(sp):
            c.load_chunks(sp, C_BRANCH + 1)

        @block.tensor
        def _(pe):
            def turn(i):
                w = units[i][3]
                pe.wait_ge(normed, i + 1)
                if i >= 2:
                    pe.wait_ge(turned_copied, i - 1)
                for k in range(w // P):
                    last = nc.tensor.transpose(c.bank(NB + i % 2)[:, k * P:(k + 1) * P],
                                               raw[:, i % NR, k * P:(k + 1) * P], c.k["ident"][:, :])
                last.then_inc(turned, 1)

            for i, (j, acts, m, *_) in enumerate(units):
                if m == 0:
                    c.wait_chunk(pe, j)
                if i >= NB:
                    pe.wait_ge(taken, i - NB + 1)
                mm_tokens(nc.tensor, c.bank(i % NB), acts, m, c.chunk(j)).then_inc(product, 1)
                if i >= 2:
                    turn(i - 2)
            turn(n - 2)
            turn(n - 1)

        @block.scalar
        def _(act):
            for i, (j, _, m, w, *_) in enumerate(units):
                act.wait_ge(product, i + 1)
                if i + 1 == n or units[i + 1][0] != j:
                    act.sem_inc(c.used, 1)
                if i >= NR:
                    act.wait_ge(turned, i - NR + 1)
                b = c.bank(i % NB)
                part = b[:, 0:w] if j != C_NAV else b[:, 256:512]
                nc.scalar.activation(raw[:, i % NR, 0:w], part, ACT.Copy)
                if j == C_NAV:
                    nc.scalar.activation(v_na[:, m, :], b[:, 0:256], ACT.Copy)
                if j == C_MEMKV:
                    nc.scalar.activation(v_mem[:, m, :], b[:, 256:512], ACT.Copy)
                nc.scalar.activation(sq[:, i % NR, 0:w], part, ACT.Square).then_inc(taken, 1)

        @block.gpsimd
        def _(pl):
            pool.then_wait(pl, nc.gpsimd.memset(half[:, :], -0.5))
            for i, (_, _, _, w, hd, *_) in enumerate(units):
                g = w // hd
                pl.wait_ge(summed, i + 1)
                pool.then_wait(pl, nc.gpsimd.tensor_scalar(ms[:, i, 0:g], ss[:, i, 0:g], 1.0 / hd, EPS, ALU.mult, ALU.add))
                nc.gpsimd.tensor_tensor(rstd[:, i, 0:g], ms[:, i, 0:g], half[:, :].to_broadcast([P, g]), ALU.pow).then_inc(rstd_ready, 1)

        @block.vector
        def _(dve):
            def copy(i):
                _, _, m, w, _, dst, gain = units[i]
                dve.wait_ge(turned, i + 1)
                nb = w // P
                nc.vector.tensor_tensor(dst[:, 0:nb, m * P:(m + 1) * P],
                                        c.bank(NB + i % 2)[:, 0:w].rearrange("p (a b) -> p a b", a=nb),
                                        c.k["g_heads"][:, gain:gain + nb].unsqueeze(2).to_broadcast([P, nb, P]),
                                        ALU.mult).then_inc(turned_copied, 1)

            for i, (j, _, m, w, hd, *_) in enumerate(units):
                g = w // hd
                dve.wait_ge(taken, i + 1)
                nc.vector.tensor_reduce(ss[:, i, 0:g], sq[:, i % NR, 0:w].rearrange("p (g d) -> p g d", d=hd),
                                        AX.X, ALU.add).then_inc(summed, 1)
                if i >= 2:
                    copy(i - 2)
                dve.wait_ge(rstd_ready, i + 1)
                for lo, hi, q in ((0, 256, j != C_MEMKV), (256, 512, False)):
                    if lo < w:
                        v = raw[:, i % NR, lo:hi].rearrange("p (g d) -> p g d", d=hd)
                        r = rstd[:, i, lo // hd:hi // hd].unsqueeze(2).to_broadcast([P, 256 // hd, hd])
                        ins = nc.vector.scalar_tensor_tensor(v, v, hd ** -0.5 if q else 1.0, r, ALU.mult, ALU.mult)
                ins.then_inc(normed, 1)
            copy(n - 2)
            copy(n - 1)


def window_tiles(t):
    rows_n = S // GRID_W
    lo = min(max(2 * t - WIN_R // 2, 0), rows_n - WIN_R)
    hi = min(max(2 * t + 1 - WIN_R // 2, 0), rows_n - WIN_R) + WIN_R
    return lo // 2, (hi + 1) // 2


NA_WIDE = 5 * P
NA_EDGE = [0, 1, TT - 2, TT - 1]
NA_TABLE = NA_WIDE + len(NA_EDGE) * 4 * P


def bias_at(t):
    return NA_WIDE + NA_EDGE.index(t) * 4 * P if t in NA_EDGE else 0


def neighbourhood(c, naT, v_na, h_tok, q_wide):
    nc = c.nc
    units = [(h, t) for h in range(NA_HEADS) for t in range(TT)]
    n = len(units)
    NS = 4
    with ExitStack() as mem:
        bias = c.sb(mem, "na_bias", [P, 2, NA_TABLE])
        sc = c.sb(mem, "na_scores", [P, NS, NA_WIDE])
        pT = c.sb(mem, "na_pT", [P, 2, NA_WIDE])
        mx = c.sb(mem, "na_max", [P, n])
        nmx = c.sb(mem, "na_negmax", [P, n])
        den = c.sb(mem, "na_den", [P, n])
        rden = c.sb(mem, "na_rden", [P, n])
        bias_there = [c.sem(mem, f"na_bias_there_{i}") for i in range(2)]
        zeroed = c.sem(mem, "na_zeroed")
        q_widened = c.sem(mem, "na_q_widened")
        scores = c.sem(mem, "na_scores_there")
        biased = c.sem(mem, "na_biased")
        max_ready = c.sem(mem, "na_max_ready")
        exp_done = c.sem(mem, "na_exp_done")
        turned = c.sem(mem, "na_turned")
        turned_copied = c.sem(mem, "na_turned_copied")
        out_there = c.sem(mem, "na_out_there")
        rden_ready = c.sem(mem, "na_rden_ready")
        out_taken = c.sem(mem, "na_out_taken")
        block = mem.enter_context(nc.Block())

        def pair(i):
            return c.psum[:, 2 * i:2 * i + 2, :].rearrange("p b n -> p (b n)")

        @block.gpsimd
        def _(pl):
            nc.gpsimd.memset(q_wide, 0.0).then_inc(zeroed, 1)
            pl.wait_ge(zeroed, 1)
            for h in range(NA_HEADS):
                hp = NA_HD * (h % 4)
                if h >= 4:
                    pl.wait_ge(scores, TT * (h - 3))
                nc.gpsimd.tensor_copy(q_wide[hp:hp + NA_HD, h % 4, :], naT[hp:hp + NA_HD, h // 4, :]).then_inc(q_widened, 1)
                pl.wait_ge(q_widened, h + 1)

        @block.sync
        def _(sp):
            for h in range(NA_HEADS):
                if h >= 2:
                    sp.wait_ge(biased, TT * (h - 1))
                sp.dma_start(bias[:, h % 2, :], c.io["na_bias"][h]).then_inc(bias_there[h % 2], 16)

        @block.tensor
        def _(pe):
            def score(i):
                h, t = units[i]
                k0, k1 = window_tiles(t)
                if t == 0:
                    pe.wait_ge(q_widened, h + 1)
                if i >= 2:
                    pe.wait_ge(biased, i - 1)
                keys = (k1 - k0) * P
                for lo in range(0, keys, BANK):
                    hi = min(lo + BANK, keys)
                    last = nc.tensor.matmul(pair(i % 2)[:, lo:hi], q_wide[:, h % 4, t * P:(t + 1) * P],
                                            naT[:, 2 + h // 4, k0 * P + lo:k0 * P + hi], start=True, stop=True)
                last.then_inc(scores, 1)

            def turn(i):
                h, t = units[i]
                k0, k1 = window_tiles(t)
                pe.wait_ge(exp_done, i + 1)
                if i >= 2:
                    pe.wait_ge(out_taken, i - 1)
                for k in range(k1 - k0):
                    last = nc.tensor.transpose(pair(2 + i % 2)[:, k * P:(k + 1) * P], sc[:, i % NS, k * P:(k + 1) * P], c.k["ident"][:, :])
                last.then_inc(turned, 1)

            def values(i):
                h, t = units[i]
                k0, k1 = window_tiles(t)
                pe.wait_ge(turned_copied, i + 1)
                for k in range(k1 - k0):
                    last = nc.tensor.matmul(pair(2 + i % 2)[:, 768:768 + NA_HD], pT[:, i % 2, k * P:(k + 1) * P],
                                            v_na[:, k0 + k, h * NA_HD:(h + 1) * NA_HD], start=(k == 0), stop=(k == k1 - k0 - 1))
                last.then_inc(out_there, 1)

            for i in range(n + 3):
                if i < n:
                    score(i)
                if 2 <= i < n + 2:
                    turn(i - 2)
                if i >= 3:
                    values(i - 3)

        @block.vector
        def _(dve):
            def finish(i):
                h, t = units[i]
                dve.wait_ge(exp_done, i + 1)
                nc.vector.reciprocal(rden[:, i:i + 1], den[:, i:i + 1]).then_inc(rden_ready, 1)
                dve.wait_ge(rden_ready, i + 1)
                dve.wait_ge(out_there, i + 1)
                nc.vector.tensor_scalar(h_tok[:, t, h * NA_HD:(h + 1) * NA_HD], pair(2 + i % 2)[:, 768:768 + NA_HD],
                                        rden[:, i:i + 1], None, ALU.mult).then_inc(out_taken, 1)

            for i, (h, t) in enumerate(units):
                k0, k1 = window_tiles(t)
                w, at = (k1 - k0) * P, bias_at(t)
                if t == 0:
                    dve.wait_ge(bias_there[h % 2], 16 * (h // 2 + 1))
                dve.wait_ge(scores, i + 1)
                if i >= NS:
                    dve.wait_ge(turned, i - NS + 1)
                nc.vector.tensor_tensor_reduce(sc[:, i % NS, 0:w], pair(i % 2)[:, 0:w], bias[:, h % 2, at:at + w],
                                               1.0, -3.0e38, ALU.add, ALU.max, mx[:, i:i + 1]).then_inc(biased, 1)
                dve.wait_ge(biased, i + 1)
                nc.vector.tensor_scalar(nmx[:, i:i + 1], mx[:, i:i + 1], -1.0, None, ALU.mult).then_inc(max_ready, 1)
                if i >= 3:
                    finish(i - 3)
            for i in range(n - 3, n):
                finish(i)

        @block.scalar
        def _(act):
            def copy(i):
                k0, k1 = window_tiles(units[i][1])
                w = (k1 - k0) * P
                act.wait_ge(turned, i + 1)
                if i >= 2:
                    act.wait_ge(out_there, i - 1)
                nc.scalar.activation(pT[:, i % 2, 0:w], pair(2 + i % 2)[:, 0:w], ACT.Copy).then_inc(turned_copied, 1)

            for i, (h, t) in enumerate(units):
                k0, k1 = window_tiles(t)
                w = (k1 - k0) * P
                act.wait_ge(max_ready, i + 1)
                nc.scalar.activation(sc[:, i % NS, 0:w], sc[:, i % NS, 0:w], ACT.Exp, bias=nmx[:, i:i + 1],
                                     accum_out=den[:, i:i + 1]).then_inc(exp_done, 1)
                if i >= 2:
                    copy(i - 2)
            copy(n - 2)
            copy(n - 1)


def memory_attention(c, qmT, kmT, v_mem, h_tok, q_wide):
    nc = c.nc
    MK = MEM // P
    with ExitStack() as mem:
        pr = c.sb(mem, "me_p", [P, 2, MEM_HEADS, MEM])
        pT = c.sb(mem, "me_pT", [P, 2, MEM_HEADS * MEM])
        nmx = c.sb(mem, "me_negmax", [P, TT, MEM_HEADS])
        den = c.sb(mem, "me_den", [P, TT, MEM_HEADS])
        rden = c.sb(mem, "me_rden", [P, TT, MEM_HEADS])
        scores = c.sem(mem, "me_scores_there")
        zeroed = c.sem(mem, "me_zeroed")
        q_widened = c.sem(mem, "me_q_widened")
        max_ready = c.sem(mem, "me_max_ready")
        exp_done = c.sem(mem, "me_exp_done")
        turned = c.sem(mem, "me_turned")
        turned_copied = c.sem(mem, "me_turned_copied")
        out_there = c.sem(mem, "me_out_there")
        rden_ready = c.sem(mem, "me_rden_ready")
        out_taken = c.sem(mem, "me_out_taken")
        block = mem.enter_context(nc.Block())

        def pair(i):
            return c.psum[:, 2 * i:2 * i + 2, :].rearrange("p b n -> p (b n)")

        @block.tensor
        def _(pe):
            for i in range(TT + 1):
                if i < TT:
                    if i >= 2:
                        pe.wait_ge(exp_done, MEM_HEADS * (i - 1))
                    else:
                        pe.wait_ge(q_widened, MEM_HEADS)
                        pe.wait_ge(zeroed, MEM_HEADS)
                    for h in range(MEM_HEADS):
                        last = nc.tensor.matmul(pair(i % 2)[:, h * MEM:(h + 1) * MEM], q_wide[:, h, i * P:(i + 1) * P],
                                                kmT[:, h // 2, :], start=True, stop=True)
                    last.then_inc(scores, 1)
                if i:
                    u = i - 1
                    pe.wait_ge(exp_done, MEM_HEADS * i)
                    if u:
                        pe.wait_ge(turned_copied, u)
                    for h in range(MEM_HEADS):
                        for k in range(MK):
                            at = (h * MK + k) * P
                            last = nc.tensor.transpose(pair(2)[:, at:at + P], pr[:, u % 2, h, k * P:(k + 1) * P], c.k["ident"][:, :])
                    last.then_inc(turned, 1)
                    pe.wait_ge(turned_copied, u + 1)
                    if u >= 2:
                        pe.wait_ge(out_taken, u - 1)
                    for h in range(MEM_HEADS):
                        for k in range(MK):
                            at = (h * MK + k) * P
                            last = nc.tensor.matmul(c.bank(6 + u % 2)[:, h * MEM_HD:(h + 1) * MEM_HD], pT[:, u % 2, at:at + P],
                                                    v_mem[:, k, h * MEM_HD:(h + 1) * MEM_HD], start=(k == 0), stop=(k == MK - 1))
                    last.then_inc(out_there, 1)

        @block.vector
        def _(dve):
            for h in range(MEM_HEADS):
                other = MEM_HD * (1 - h % 2)
                nc.vector.memset(q_wide[other:other + MEM_HD, h, :], 0.0).then_inc(zeroed, 1)
            for i in range(TT + 1):
                if i < TT:
                    dve.wait_ge(scores, i + 1)
                    nc.vector.tensor_reduce(nmx[:, i, :], pair(i % 2).rearrange("p (h k) -> p h k", k=MEM), AX.X, ALU.max,
                                            negate=True).then_inc(max_ready, 1)
                if i:
                    u = i - 1
                    dve.wait_ge(exp_done, MEM_HEADS * i)
                    nc.vector.reciprocal(rden[:, u, :], den[:, u, :]).then_inc(rden_ready, 1)
                    dve.wait_ge(rden_ready, i)
                    dve.wait_ge(out_there, i)
                    nc.vector.tensor_tensor(h_tok[:, u, :].rearrange("p (h d) -> p h d", d=MEM_HD),
                                            c.bank(6 + u % 2)[:, 0:256].rearrange("p (h d) -> p h d", d=MEM_HD),
                                            rden[:, u, :].unsqueeze(2).to_broadcast([P, MEM_HEADS, MEM_HD]),
                                            ALU.mult).then_inc(out_taken, 1)

        @block.scalar
        def _(act):
            for h in range(MEM_HEADS):
                hp = MEM_HD * (h % 2)
                nc.scalar.activation(q_wide[hp:hp + MEM_HD, h, :], qmT[hp:hp + MEM_HD, h // 2, :], ACT.Copy).then_inc(q_widened, 1)
            for i in range(TT + 1):
                if i < TT:
                    act.wait_ge(max_ready, i + 1)
                    if i >= 2:
                        act.wait_ge(turned, i - 1)
                    for h in range(MEM_HEADS):
                        nc.scalar.activation(pr[:, i % 2, h, :], pair(i % 2)[:, h * MEM:(h + 1) * MEM], ACT.Exp,
                                             bias=nmx[:, i, h:h + 1],
                                             accum_out=den[:, i, h:h + 1]).then_inc(exp_done, 1)
                if i:
                    u = i - 1
                    act.wait_ge(turned, i)
                    if u >= 2:
                        act.wait_ge(out_there, u - 1)
                    nc.scalar.activation(pT[:, u % 2, :], pair(2), ACT.Copy).then_inc(turned_copied, 1)


def transpose_tokens(c, name, pairs, upper=None):
    nc = c.nc
    units = [(src, dst, m, w) for src, dst, w in pairs for m in range(TT)]
    NB = 4
    with ExitStack() as mem:
        turned = c.sem(mem, name + "_turned")
        copied = c.sem(mem, name + "_copied")
        upper_taken = c.sem(mem, name + "_upper_taken")
        block = mem.enter_context(nc.Block())

        @block.tensor
        def _(pe):
            for i, (src, dst, m, w) in enumerate(units):
                if i >= NB:
                    pe.wait_ge(copied, i - NB + 1)
                for k in range(w // P):
                    last = nc.tensor.transpose(c.bank(i % NB)[:, k * P:(k + 1) * P], src[:, m, k * P:(k + 1) * P], c.k["ident"][:, :])
                last.then_inc(turned, 1)

        @block.vector
        def _(dve):
            for i, (src, dst, m, w) in enumerate(units):
                dve.wait_ge(turned, i + 1)
                to = dst[:, 0:w // P, m * P:(m + 1) * P]
                b = c.bank(i % NB)[:, 0:w].rearrange("p (a b) -> p a b", b=P)
                if upper is None:
                    nc.vector.tensor_copy(to, b).then_inc(copied, 1)
                else:
                    up = upper[i // TT][:, 0:w // P, m * P:(m + 1) * P]
                    take_upper(nc.vector, up, b).then_inc(upper_taken, 1)
                    dve.wait_ge(upper_taken, i + 1)
                    take_lower(nc.vector, to, b, up).then_inc(copied, 1)


def gated_branches(c, whole, hT, branches, yT):
    nc = c.nc
    parts = [(n, b, ch, th) for n in range(4) for b in range(3) for ch in range(2) for th in range(2)]
    NB = 4
    with ExitStack() as mem:
        pw = c.sb(mem, "br_proj", [P, 2, 4, HALF])
        gate = c.sb(mem, "br_gate", [P, 3, BANK])
        prod = c.sb(mem, "br_product", [P, 2, BANK])
        pw_there = [c.sem(mem, f"br_proj_there_{i}") for i in range(2)]
        gate_there = c.sem(mem, "br_gate_there")
        V = Steps(nc, mem, "br_dve_steps")
        h_split = c.sem(mem, "br_h_split")
        proj_there = c.sem(mem, "br_proj_out_there")
        gate_done = c.sem(mem, "br_gate_done")
        multiplied = c.sem(mem, "br_multiplied")
        added = c.sem(mem, "br_added")
        block = mem.enter_context(nc.Block())

        @block.sync
        def _(sp):
            for i in range(12):
                n, b = i // 3, i % 3
                w = branches[b][1]
                if i >= 2:
                    sp.wait_ge(multiplied, 4 * (i - 1))
                sp.dma_start(pw[:, i % 2, 0:w.shape[0] // P, :],
                             w[:, n * HALF:(n + 1) * HALF].rearrange("(k p) n -> p k n", p=P)).then_inc(pw_there[i % 2], 16)
                c.load_chunks(sp, C_BRANCH + i + 2)
            c.load_chunks(sp, C_OUT + 2)

        @block.tensor
        def _(pe):
            for i, (n, b, ch, th) in enumerate(parts):
                q = i // 4
                if i % 4 == 0:
                    c.wait_split(pe, C_BRANCH + q)
                    pe.wait_ge(pw_there[q % 2], 16 * (q // 2 + 1))
                if i >= NB:
                    pe.wait_ge(multiplied, i - NB + 1)
                if i < 2:
                    pe.wait_ge(h_split, i + 1)
                split_channels(nc.tensor, c.bank(i % NB), hT, th * BANK, BANK, c.parts(C_BRANCH + q), ch * P).then_inc(gate_there, 1)
                acts, w = branches[b]
                mm_channels(nc.tensor, c.bank(NB + i % NB), acts, th * BANK, BANK, pw[:, q % 2, :, :], ch * P,
                            kt=w.shape[0] // P).then_inc(proj_there, 1)

        @block.scalar
        def _(act):
            for i in range(len(parts)):
                act.wait_ge(gate_there, i + 1)
                if i % 4 == 3:
                    act.sem_inc(c.used, 1)
                if i >= 3:
                    act.wait_ge(multiplied, i - 2)
                nc.scalar.activation(gate[:, i % 3, :], c.bank(i % NB), ACT.Sigmoid).then_inc(gate_done, 1)

        @block.vector
        def _(dve):
            n_added = 0
            c.split_chunk(dve, C_BRANCH)
            for th in range(2):
                cols = slice(th * BANK, (th + 1) * BANK)
                split(dve, nc.vector, V, whole[:, :, cols], hT[0][:, :, cols], hT[1][:, :, cols]).then_inc(h_split, 1)
            for i, (n, b, ch, th) in enumerate(parts):
                y = yT[:, 2 * n + ch, th * BANK:(th + 1) * BANK]
                dve.wait_ge(gate_done, i + 1)
                dve.wait_ge(proj_there, i + 1)
                dst = y if b == 0 else prod[:, i % 2, :]
                if n_added >= 2:
                    dve.wait_ge(added, n_added - 1)
                nc.vector.tensor_tensor(dst, gate[:, i % 3, :], c.bank(NB + i % NB), ALU.mult).then_inc(multiplied, 1)
                if b:
                    dve.wait_ge(multiplied, i + 1)
                    nc.vector.tensor_tensor(y, y, prod[:, i % 2, :], ALU.add).then_inc(added, 1)
                    n_added += 1
                if i % 4 == 1:
                    c.split_chunk(dve, C_BRANCH + i // 4 + 1)


def project_add(c, name, acts, j0, x_sb, load_to, first_load=None, whole=None):
    nc = c.nc
    NB = 4
    PAIRS = TT // 2
    with ExitStack() as mem:
        product = c.sem(mem, name + "_product")
        added = c.sem(mem, name + "_added")
        x_there = c.sem(mem, name + "_x_there")
        V = Steps(nc, mem, name + "_dve_steps")
        acts_split = c.sem(mem, name + "_acts_split")
        block = mem.enter_context(nc.Block())

        @block.sync
        def _(sp):
            if first_load is not None:
                sp.dma_start(x_sb[:, :, :], first_load.rearrange("(t p) n -> p t n", p=P)).then_inc(x_there, 16)
            c.load_chunks(sp, load_to)

        @block.tensor
        def _(pe):
            for i in range(4 * PAIRS):
                n, m = i // PAIRS, i % PAIRS
                if m == 0:
                    c.wait_split(pe, j0 + n)
                if whole is not None and n == 0:
                    pe.wait_ge(acts_split, 2 * m + 2)
                if i >= NB:
                    pe.wait_ge(added, i - NB + 1)
                split_tokens(nc.tensor, c.bank(i % NB), acts, m, c.parts(j0 + n)).then_inc(product, 1)

        @block.vector
        def _(dve):
            if whole is not None:
                for m in range(TT):
                    cols = slice(m * P, (m + 1) * P)
                    split(dve, nc.vector, V, whole[:, :, cols], acts[0][:, :, cols], acts[1][:, :, cols]).then_inc(acts_split, 1)
            if first_load is not None:
                dve.wait_ge(x_there, 16)
            for i in range(4 * PAIRS):
                n, m = i // PAIRS, i % PAIRS
                dve.wait_ge(product, i + 1)
                if m == PAIRS - 1:
                    dve.sem_inc(c.used, 1)
                x = x_sb[:, 2 * m:2 * m + 2, n * HALF:(n + 1) * HALF]
                nc.vector.tensor_tensor(x, x, c.bank(i % NB).rearrange("p (t n) -> p t n", t=2), ALU.add).then_inc(added, 1)
                if m == 1 and n < 3:
                    c.split_chunk(dve, j0 + n + 1)


def ffn(c, hT, x_sb, uT):
    nc = c.nc
    NB = 6
    with ExitStack() as mem:
        r = c.sb(mem, "ff_relu", [P, 2, BANK])
        product = c.sem(mem, "ff_product")
        relu_done = c.sem(mem, "ff_relu_done")
        squared = c.sem(mem, "ff_squared")
        added = c.sem(mem, "ff_added")
        V = Steps(nc, mem, "ff_dve_steps")
        block = mem.enter_context(nc.Block())
        QUARTERS = D_FF // D

        @block.sync
        def _(sp):
            c.load_chunks(sp, C_IN2 + 2)

        @block.tensor
        def _(pe):
            for f in range(QUARTERS):
                for i in range(32):
                    g = 32 * f + i
                    j = C_FFN + 8 * f + i // 4
                    if i % 4 == 0:
                        c.wait_split(pe, j)
                    if g >= NB:
                        q, k = divmod(g - NB, 32)
                        if k < 16:
                            pe.wait_ge(relu_done, 16 * q + k + 1)
                        else:
                            pe.wait_ge(added, 16 * q + k - 16 + 1)
                    if i == 16:
                        pe.wait_ge(squared, 16 * (f + 1))
                    if i < 16:
                        ins = split_channels(nc.tensor, c.bank(g % NB), hT, (i % 2) * BANK, BANK, c.parts(j), (i // 2 % 2) * P)
                    else:
                        ins = split_tokens(nc.tensor, c.bank(g % NB), uT, i % 4, c.parts(j))
                    ins.then_inc(product, 1)

        @block.scalar
        def _(act):
            for f in range(QUARTERS):
                for i in range(16):
                    g, u = 32 * f + i, 16 * f + i
                    act.wait_ge(product, g + 1)
                    if i % 4 == 3:
                        if i == 3 and f:
                            act.wait_ge(added, 16 * f)
                        act.sem_inc(c.used, 1)
                    if u >= 2:
                        act.wait_ge(squared, u - 1)
                    nc.scalar.activation(r[:, u % 2, :], c.bank(g % NB), ACT.Relu).then_inc(relu_done, 1)

        @block.vector
        def _(dve):
            for f in range(QUARTERS):
                for i in range(16):
                    u = 16 * f + i
                    dve.wait_ge(relu_done, u + 1)
                    upper, lower = (p[:, i // 2, (i % 2) * BANK:(i % 2 + 1) * BANK] for p in uT)
                    square = r[:, u % 2, :]
                    V.then_wait(dve, nc.vector.tensor_tensor(square, square, square, ALU.mult))
                    split(dve, nc.vector, V, square, upper, lower).then_inc(squared, 1)
                    if i % 4 == 1:
                        c.split_chunk(dve, C_FFN + 8 * f + i // 4 + 1)
                for i in range(16):
                    g, u = 32 * f + 16 + i, 16 * f + i
                    dve.wait_ge(product, g + 1)
                    if i % 4 == 3:
                        dve.sem_inc(c.used, 1)
                    x = x_sb[:, i % 4 * 2:i % 4 * 2 + 2, (i // 4) * HALF:(i // 4 + 1) * HALF]
                    if u >= 16:
                        dve.wait_ge(added, u - 15)
                    nc.vector.tensor_tensor(x, x, c.bank(g % NB).rearrange("p (t n) -> p t n", t=2), ALU.add).then_inc(added, 1)
                    if i % 4 == 1:
                        c.split_chunk(dve, C_FFN + 8 * f + 4 + i // 4 + 1)


def spill(c, name, sb_ap, dram, clear, cleared):
    nc = c.nc
    with ExitStack() as mem:
        stored = c.sem(mem, name + "_stored")
        block = mem.enter_context(nc.Block())

        @block.sync
        def _(sp):
            sp.dma_start(dram.rearrange("(t p) n -> p t n", p=P), sb_ap).then_inc(stored, 16)
            sp.dma_start(clear.rearrange("(p t) (a n) -> p (t a) n", p=P, n=256),
                         c.k["zeros"][:, :].unsqueeze(1).to_broadcast([P, clear.shape[0] // P * D // 256, 256])).then_inc(cleared, 16)
            sp.wait_ge(stored, 16)


def delta_inputs(c, hT, qkv, gate, small, ss, conv):
    nc = c.nc
    PAD = A_CONV_K - 1
    NCH = 12
    with ExitStack() as mem:
        raw = c.sb(mem, "di_raw", [P, 2, PAD + S])
        cv = [conv[:, 2 * i:2 * i + 2, :] for i in range(2)]
        zeroed = c.sem(mem, "di_zeroed")
        wba_split = c.sem(mem, "di_beta_alpha_weights_split")
        w_ba = [c.sb(mem, "di_w_ba_" + n, [P, KT, 8])[:, :, :] for n in ("upper", "lower")]
        small_T = c.sb(mem, "di_beta_alpha_rows", [8, S])
        product = c.sem(mem, "di_product")
        copied = c.sem(mem, "di_copied")
        tap = Steps(nc, mem, "di_taps")
        conv_done = c.sem(mem, "di_conv_done")
        silu_done = c.sem(mem, "di_silu_done")
        turned = c.sem(mem, "di_turned")
        turned_copied = c.sem(mem, "di_turned_copied")
        squared = c.sem(mem, "di_squared")
        junk = c.sb(mem, "di_junk", [P, G_DIM])
        block = mem.enter_context(nc.Block())
        NB = 4

        @block.sync
        def _(sp):
            c.load_chunks(sp, C_IN2 + 9)

        @block.tensor
        def _(pe):
            def turn(ch):
                pe.wait_ge(silu_done, ch + 1)
                for g in range(2):
                    b = 2 * ch + g
                    if b >= 4:
                        pe.wait_ge(turned_copied, b - 3)
                    for k in range(4):
                        last = nc.tensor.transpose(c.bank(NB + b % 4)[:, k * P:(k + 1) * P],
                                                   cv[ch % 2][:, g, k * P:(k + 1) * P], c.k["ident"][:, :])
                    last.then_inc(turned, 1)

            g = 0
            for ch in range(NCH):
                if ch % 2 == 0:
                    c.wait_split(pe, C_IN2 + ch // 2)
                for th in range(2):
                    if g >= NB:
                        pe.wait_ge(copied, g - NB + 1)
                    split_channels(nc.tensor, c.bank(g % NB), hT, th * BANK, BANK, c.parts(C_IN2 + ch // 2), ch % 2 * P).then_inc(product, 1)
                    g += 1
                if ch:
                    turn(ch - 1)
            for m in range(TT):
                pe.wait_ge(copied, g - NB + 1)
                if m % 4 == 0:
                    c.wait_split(pe, C_IN2 + 6 + m // 4)
                split_tokens(nc.tensor, c.bank(g % NB), hT, m % 4, c.parts(C_IN2 + 6 + m // 4)).then_inc(product, 1)
                g += 1
                if m == 0:
                    turn(NCH - 1)
            pe.wait_ge(wba_split, 1)
            for th in range(2):
                pe.wait_ge(copied, g - NB + 1)
                for k in range(KT):
                    for x, y in PASSES:
                        last = nc.tensor.matmul(c.bank(g % NB, parts=8), w_ba[x][:, k, :].bitcast(F32R),
                                                hT[y][:, k, th * BANK:(th + 1) * BANK].bitcast(F32R),
                                                start=(k == 0 and x == y), stop=(k == KT - 1 and x == 1))
                last.then_inc(product, 1)
                g += 1
            pe.wait_ge(copied, g)
            for m in range(TT):
                last = nc.tensor.transpose(c.bank(g % NB)[:, m * 8:(m + 1) * 8], small_T[:, m * P:(m + 1) * P], c.k["ident"][0:8, 0:8])
            last.then_inc(product, 1)

        @block.scalar
        def _(act):
            act.wait_ge(zeroed, 1)

            def squares(ch):
                for g in range(2):
                    b = 2 * ch + g
                    act.wait_ge(turned_copied, b + 1)
                    for k in range(4):
                        if 4 * b + k:
                            act.wait_ge(squared, 4 * b + k)
                        nc.scalar.activation(junk[:, :], qkv[:, 4 * g + k, ch * P:(ch + 1) * P], ACT.Square,
                                             accum_out=ss[:, 4 * g + k, ch:ch + 1]).then_inc(squared, 1)

            def silu(ch):
                act.wait_ge(conv_done, ch + 1)
                nc.scalar.activation(cv[ch % 2], cv[ch % 2], ACT.Silu).then_inc(silu_done, 1)

            for ch in range(NCH):
                for th in range(2):
                    g = 2 * ch + th
                    act.wait_ge(product, g + 1)
                    if g % 4 == 3:
                        act.sem_inc(c.used, 1)
                    if ch >= 2 and th == 0:
                        act.wait_ge(conv_done, ch - 1)
                    nc.scalar.activation(raw[:, ch % 2, PAD + th * BANK:PAD + (th + 1) * BANK], c.bank(g % NB), ACT.Copy).then_inc(copied, 1)
                    if ch and th == 0:
                        silu(ch - 1)
                if 2 <= ch < 10:
                    squares(ch - 2)
            silu(NCH - 1)
            for m in range(TT):
                g = 2 * NCH + m
                act.wait_ge(product, g + 1)
                if m % 4 == 3:
                    act.sem_inc(c.used, 1)
                nc.scalar.activation(gate[:, m % 4 * 2:m % 4 * 2 + 2, m // 4 * HALF:(m // 4 + 1) * HALF],
                                     c.bank(g % NB).rearrange("p (t n) -> p t n", t=2), ACT.Silu).then_inc(copied, 1)
            g = 2 * NCH + TT
            for th in range(2):
                act.wait_ge(product, g + 1)
                nc.scalar.activation(small_T[:, th * BANK:(th + 1) * BANK], c.bank(g % NB, parts=8), ACT.Copy).then_inc(copied, 1)
                g += 1
            act.wait_ge(product, g + 1)
            nc.scalar.activation(small[:, :, :], c.bank(g % NB)[:, 0:8 * TT].rearrange("p (t n) -> p t n", n=8), ACT.Copy).then_inc(copied, 1)

        @block.vector
        def _(dve):
            nc.vector.memset(raw[:, :, 0:PAD], 0.0).then_inc(zeroed, 1)
            dve.wait_ge(zeroed, 1)
            split(dve, nc.vector, tap, c.k["w_ba"][:, :, :], w_ba[0], w_ba[1]).then_inc(wba_split, 1)

            def copy(ch):
                for g in range(2):
                    b = 2 * ch + g
                    dve.wait_ge(turned, b + 1)
                    nc.vector.tensor_copy(qkv[:, 4 * g:4 * g + 4, ch * P:(ch + 1) * P],
                                          c.bank(NB + b % 4).rearrange("p (a b) -> p a b", a=4)).then_inc(turned_copied, 1)

            for ch in range(NCH):
                if ch % 2 == 0:
                    c.split_chunk(dve, C_IN2 + ch // 2 + 1)
                dve.wait_ge(copied, 2 * ch + 2)
                if ch >= 2:
                    dve.wait_ge(turned, 2 * (ch - 1))
                dst = cv[ch % 2]
                for i in range(A_CONV_K):
                    src = raw[:, ch % 2, i:i + S].rearrange("p (a b) -> p a b", a=2)
                    w = c.k["conv2"][:, ch, i:i + 1]
                    if i == 0:
                        ins = nc.vector.tensor_scalar(dst, src, w, None, ALU.mult)
                    else:
                        ins = nc.vector.scalar_tensor_tensor(dst, src, w, dst, ALU.mult, ALU.add)
                    if i < A_CONV_K - 1:
                        tap.then_wait(dve, ins)
                ins.then_inc(conv_done, 1)
                if ch:
                    copy(ch - 1)
            copy(NCH - 1)
            for n in range(2):
                c.split_chunk(dve, C_IN2 + 7 + n)
            for m in range(TT):
                dve.wait_ge(copied, 2 * NCH + 4 + m // 2 + 1)
                v = gate[:, m, :].rearrange("p (h d) -> p h d", d=P)
                nc.vector.tensor_tensor(v, v, c.k["norm_a"][:, :].unsqueeze(1).to_broadcast([P, 4, P]), ALU.mult)


def heads(ap):
    return ap.rearrange("p (h d) -> p h d", d=G_DIM)


def per_head(col):
    return col.unsqueeze(2).to_broadcast([P, 4, G_DIM])


def same_for_heads(ap):
    return ap.unsqueeze(1).to_broadcast([P, 4, G_DIM])


def head(ap, h):
    return ap[:, h * G_DIM:(h + 1) * G_DIM]


LEVELS = 7
GROUPS = 2
GW = 2 * G_DIM


def delta_rule(c, qkv, o, small, ss, scratch):
    nc = c.nc
    H, C = A_HEADS, TT
    with ExitStack() as mem:
        def tile(name):
            return c.sb(mem, "dr_" + name, [P, BANK])[:, :]

        kT, qT, kbT, qdT = (tile(n) for n in ("kT", "qT", "kbT", "qdT"))
        kb, kbg, kdec, state = (c.raw[:, 2 * i:2 * i + 2, :].rearrange("p a b -> p (a b)") for i in range(4))
        qd, decT, attnT, AT, M, X, T, U = (scratch[:, i, :] for i in range(8))
        gmask = qd
        wTn, vnew = kT, kbT
        rs = c.sb(mem, "dr_rs", [P, C, 8])
        half = c.sb(mem, "dr_half", [P, 1])
        beta = c.sb(mem, "dr_beta", [P, C, H])
        g = c.sb(mem, "dr_g", [P, C, H])
        t1 = c.sb(mem, "dr_t1", [P, C, H])
        t2 = c.sb(mem, "dr_t2", [P, C, H])
        ea = c.sb(mem, "dr_ea", [P, H])
        eg = c.sb(mem, "dr_eg", [P, 3, C, H])
        oss = c.sb(mem, "dr_oss", [P, C, H])
        ors = c.sb(mem, "dr_ors", [P, C, H])
        junk = c.sb(mem, "dr_junk", [P, G_DIM])
        V = Steps(nc, mem, "dr_dve_steps")
        A = Steps(nc, mem, "dr_act_steps")
        G = Steps(nc, mem, "dr_pool_steps")
        names = ["alpha", "abs", "log", "g", "g_sums", "eg", "rs", "kn", "qn", "kdec", "vb", "gmask", "decay_sum", "dec_exp",
                 "decT", "kb", "kbg", "qd", "turned", "turned_copied", "A_there", "attn_there", "AT", "attnT", "M", "U",
                 "T_there", "T", "X_there", "X", "TX_there", "XU_there", "w_there", "wT", "v_there", "vnew", "o_there",
                 "o_squared", "ors", "s_there", "state", "o_done"]
        s = {n: c.sem(mem, "dr_" + n) for n in names}
        block = mem.enter_context(nc.Block())

        def cols(ap, gr):
            return ap[:, gr * GW:(gr + 1) * GW]

        def n_u(m, level, gr):
            return m * 2 * LEVELS + 2 * level + gr + 1

        def n_x(m, level, gr):
            return m * 2 * (LEVELS - 1) + 2 * (level - 1) + gr + 1

        def n_t(m, level, gr):
            return m * 2 * (LEVELS - 1) + 2 * level + gr + 1

        @block.tensor
        def _(pe):
            pe.wait_ge(s["g"], 1)
            for i, mask in enumerate((c.k["mask_le"], c.k["mask_gt"], c.k["ones"])):
                last = nc.tensor.matmul(c.bank(7)[:, i * C * H:(i + 1) * C * H], mask[:, :],
                                        g[:, :, :].rearrange("p c h -> p (c h)"), start=True, stop=True)
            last.then_inc(s["g_sums"], 1)
            for m in range(C):
                pe.wait_ge(s["gmask"], m + 1)
                if m:
                    pe.wait_ge(s["dec_exp"], m)
                nc.tensor.matmul(c.bank(6), c.k["mask_gt"][:, :], gmask, start=True, stop=True).then_inc(s["decay_sum"], 1)
                k, q = qkv[:, m, BANK:2 * BANK], qkv[:, m, 0:BANK]
                if m:
                    pe.wait_ge(s["wT"], 2 * m)
                for i, (src, ready) in enumerate(((k, "kn"), (kb, "kb"), (q, "qn"), (qd, "qd"))):
                    pe.wait_ge(s[ready], m + 1)
                    for h in range(H):
                        last = nc.tensor.transpose(head(c.bank(i), h), head(src, h), c.k["ident"][:, :])
                    last.then_inc(s["turned"], 1)
                pe.wait_ge(s["turned_copied"], 4 * m + 2)
                if m:
                    pe.wait_ge(s["state"], m)
                for h in range(H):
                    last = nc.tensor.matmul(head(c.bank(4), h), head(kT, h), head(kbT, h), start=True, stop=True)
                last.then_inc(s["A_there"], 1)
                pe.wait_ge(s["turned_copied"], 4 * m + 3)
                for h in range(H):
                    last = nc.tensor.matmul(head(c.bank(5), h), head(kT, h), head(qT, h), start=True, stop=True)
                last.then_inc(s["attn_there"], 1)
                pe.wait_ge(s["turned_copied"], 4 * m + 4)
                for gr in range(GROUPS):
                    pe.wait_ge(s["U"], n_u(m, 0, gr))
                    for h in range(2):
                        last = nc.tensor.transpose(head(c.bank(2 + gr), h), head(cols(U, gr), h), c.k["ident"][:, :])
                    last.then_inc(s["T_there"], 1)
                for level in range(1, LEVELS):
                    for gr in range(GROUPS):
                        pe.wait_ge(s["M"], n_u(m, level, gr))
                        pe.wait_ge(s["T"], n_t(m, level - 1, gr))
                        for h in range(2):
                            last = nc.tensor.matmul(head(c.bank(gr), h), head(cols(M, gr), h), head(cols(T, gr), h), start=True, stop=True)
                        last.then_inc(s["X_there"], 1)
                    for gr in range(GROUPS):
                        pe.wait_ge(s["X"], n_x(m, level, gr))
                        pe.wait_ge(s["U"], n_u(m, level - 1, gr))
                        if level == 1:
                            pe.wait_ge(s["attnT"], m + 1)
                        for h in range(2):
                            last = nc.tensor.matmul(head(c.bank(4 + gr), h), head(cols(X, gr), h), head(cols(U, gr), h), start=True, stop=True)
                        last.then_inc(s["XU_there"], 1)
                        if level < LEVELS - 1:
                            for h in range(2):
                                last = nc.tensor.matmul(head(c.bank(2 + gr), h), head(cols(U, gr), h), head(cols(X, gr), h), start=True, stop=True)
                            last.then_inc(s["TX_there"], 1)
                vb = qkv[:, m, 2 * BANK:3 * BANK]
                pe.wait_ge(s["kbg"], m + 1)
                for gr in range(GROUPS):
                    pe.wait_ge(s["U"], n_u(m, LEVELS - 1, gr))
                    for h in range(2):
                        last = nc.tensor.matmul(head(c.bank(gr), h), head(cols(kbg, gr), h), head(cols(U, gr), h), start=True, stop=True)
                    last.then_inc(s["w_there"], 1)
                pe.wait_ge(s["vb"], m + 1)
                pe.wait_ge(s["state"], m + 1)
                for gr in range(GROUPS):
                    pe.wait_ge(s["wT"], 2 * m + gr + 1)
                    for h in range(2):
                        v = head(c.bank(2 + gr), h)
                        nc.tensor.matmul(v, head(cols(U, gr), h), head(cols(vb, gr), h), start=True, stop=False)
                        last = nc.tensor.matmul(v, head(cols(wTn, gr), h), head(cols(state, gr), h), start=False, stop=True)
                    last.then_inc(s["v_there"], 1)
                if m:
                    pe.wait_ge(s["o_done"], 4 * m)
                pe.wait_ge(s["kdec"], m + 1)
                pe.wait_ge(s["vnew"], 2 * m + 2)
                for h in range(H):
                    nc.tensor.matmul(head(c.bank(7), h), head(qdT, h), head(state, h), start=True, stop=False)
                    last = nc.tensor.matmul(head(c.bank(7), h), head(attnT, h), head(vnew, h), start=False, stop=True)
                last.then_inc(s["o_there"], 1)
                for h in range(H):
                    last = nc.tensor.matmul(head(c.bank(4), h), head(kdec, h), head(vnew, h), start=True, stop=True)
                last.then_inc(s["s_there"], 1)

        @block.vector
        def _(dve):
            nc.vector.memset(state, 0.0).then_inc(s["state"], 1)
            x = small[:, :, H:2 * H]
            V.then_wait(dve, nc.vector.tensor_tensor(t1[:, :, :], x, c.k["dt_bias"][:, :].unsqueeze(1).to_broadcast([P, C, H]), ALU.add))
            nc.vector.scalar_tensor_tensor(t2[:, :, :], t1[:, :, :], -1.0, t1[:, :, :], ALU.mult, ALU.max).then_inc(s["abs"], 1)
            dve.wait_ge(s["log"], 1)
            V.then_wait(dve, nc.vector.scalar_tensor_tensor(t1[:, :, :], t1[:, :, :], 0.0, t2[:, :, :], ALU.max, ALU.add))
            nc.vector.scalar_tensor_tensor(g[:, :, :], t1[:, :, :], -1.0, ea[:, :].unsqueeze(1).to_broadcast([P, C, H]),
                                           ALU.mult, ALU.mult).then_inc(s["g"], 1)
            dve.wait_ge(s["g"], 1)
            for m in range(C):
                if m:
                    dve.wait_ge(s["turned"], 4 * m)
                nc.vector.tensor_tensor(heads(gmask), same_for_heads(c.k["mask_le"][:, :]), per_head(g[:, m, :]), ALU.mult).then_inc(s["gmask"], 1)
                dve.wait_ge(s["kn"], m + 1)
                nc.vector.tensor_tensor(heads(kb), heads(qkv[:, m, BANK:2 * BANK]), per_head(beta[:, m, :]), ALU.mult).then_inc(s["kb"], 1)
                dve.wait_ge(s["qn"], m + 1)
                dve.wait_ge(s["eg"], 1)
                dve.wait_ge(s["decay_sum"], m + 1)
                nc.vector.tensor_tensor(heads(qd), heads(qkv[:, m, 0:BANK]), per_head(eg[:, 0, m, :]), ALU.mult).then_inc(s["qd"], 1)
                dve.wait_ge(s["kb"], m + 1)
                if m:
                    dve.wait_ge(s["w_there"], 2 * m)
                nc.vector.tensor_tensor(heads(kbg), heads(kb), per_head(eg[:, 0, m, :]), ALU.mult).then_inc(s["kbg"], 1)
                dve.wait_ge(s["A_there"], m + 1)
                dve.wait_ge(s["decT"], m + 1)
                nc.vector.tensor_tensor(AT, c.bank(4), decT, ALU.mult).then_inc(s["AT"], 1)
                dve.wait_ge(s["attn_there"], m + 1)
                nc.vector.tensor_tensor(attnT, c.bank(5), decT, ALU.mult).then_inc(s["attnT"], 1)
                for gr in range(GROUPS):
                    dve.wait_ge(s["M"], n_u(m, 0, gr))
                    nc.vector.tensor_tensor(cols(U, gr).rearrange("p (h d) -> p h d", h=2),
                                            c.k["ident"][:, :].unsqueeze(1).to_broadcast([P, 2, P]),
                                            cols(M, gr).rearrange("p (h d) -> p h d", h=2), ALU.subtract).then_inc(s["U"], 1)
                for gr in range(GROUPS):
                    dve.wait_ge(s["T_there"], 2 * m + gr + 1)
                    nc.vector.tensor_copy(cols(T, gr), c.bank(2 + gr)[:, 0:GW]).then_inc(s["T"], 1)
                for level in range(1, LEVELS):
                    for gr in range(GROUPS):
                        dve.wait_ge(s["XU_there"], n_x(m, level, gr))
                        if level < LEVELS - 1:
                            n = m * 2 * (LEVELS - 2) + 2 * (level - 1) + gr + 1
                            dve.wait_ge(s["TX_there"], n)
                            dve.wait_ge(s["T"], n_t(m, level - 1, gr))
                            nc.vector.tensor_tensor(cols(T, gr), cols(T, gr), c.bank(2 + gr)[:, 0:GW], ALU.subtract).then_inc(s["T"], 1)
                        dve.wait_ge(s["U"], n_u(m, level - 1, gr))
                        nc.vector.tensor_tensor(cols(U, gr), cols(U, gr), c.bank(4 + gr)[:, 0:GW], ALU.subtract).then_inc(s["U"], 1)
                dve.wait_ge(s["ors"], m + 1)
                for h in range(H):
                    nc.vector.scalar_tensor_tensor(head(o[:, m, :], h), head(c.bank(7), h), ors[:, m, h:h + 1], head(o[:, m, :], h),
                                                   ALU.mult, ALU.mult).then_inc(s["o_done"], 1)
                dve.wait_ge(s["s_there"], m + 1)
                for h in range(H):
                    ins = nc.vector.scalar_tensor_tensor(head(state, h), head(state, h), eg[:, 2, m, h:h + 1], head(c.bank(4), h),
                                                         ALU.mult, ALU.add)
                ins.then_inc(s["state"], 1)
                dve.wait_ge(s["state"], m + 2)

        @block.scalar
        def _(act):
            nc.scalar.activation(beta[:, :, :], small[:, :, 0:H], ACT.Sigmoid).then_inc(s["alpha"], 1)
            A.done(nc.scalar.activation(ea[:, :], c.k["a_log"][:, :], ACT.Exp))
            act.wait_ge(s["abs"], 1)
            A.then_wait(act, nc.scalar.activation(t2[:, :, :], t2[:, :, :], ACT.Exp, scale=-1.0))
            nc.scalar.activation(t2[:, :, :], t2[:, :, :], ACT.Ln, bias=1.0).then_inc(s["log"], 1)
            act.wait_ge(s["g_sums"], 1)
            nc.scalar.activation(eg[:, :, :, :].rearrange("p a c h -> p (a c h)"), c.bank(7)[:, 0:3 * C * H], ACT.Exp).then_inc(s["eg"], 1)
            for m in range(C):
                act.wait_ge(s["decay_sum"], m + 1)
                nc.scalar.activation(decT, c.bank(6), ACT.Exp).then_inc(s["dec_exp"], 1)
                if m:
                    act.wait_ge(s["s_there"], m)
                for i, dst in enumerate((kT, kbT, qT, qdT)):
                    act.wait_ge(s["turned"], 4 * m + i + 1)
                    nc.scalar.activation(dst, c.bank(i), ACT.Copy).then_inc(s["turned_copied"], 1)
                for level in range(1, LEVELS):
                    for gr in range(GROUPS):
                        act.wait_ge(s["X_there"], n_x(m, level, gr))
                        nc.scalar.activation(cols(X, gr), c.bank(gr)[:, 0:GW], ACT.Copy).then_inc(s["X"], 1)
                for gr in range(GROUPS):
                    act.wait_ge(s["w_there"], 2 * m + gr + 1)
                    nc.scalar.activation(cols(wTn, gr), c.bank(gr)[:, 0:GW], ACT.Copy, scale=-1.0).then_inc(s["wT"], 1)
                for gr in range(GROUPS):
                    act.wait_ge(s["v_there"], 2 * m + gr + 1)
                    nc.scalar.activation(cols(vnew, gr), c.bank(2 + gr)[:, 0:GW], ACT.Copy).then_inc(s["vnew"], 1)
                act.wait_ge(s["o_there"], m + 1)
                for h in range(H):
                    if 4 * m + h:
                        act.wait_ge(s["o_squared"], 4 * m + h)
                    nc.scalar.activation(junk[:, :], head(c.bank(7), h), ACT.Square, accum_out=oss[:, m, h:h + 1]).then_inc(s["o_squared"], 1)

        @block.gpsimd
        def _(pl):
            G.then_wait(pl, nc.gpsimd.memset(half[:, :], -0.5))
            G.then_wait(pl, nc.gpsimd.tensor_scalar(rs[:, :, :], ss[:, :, :], EPS, None, ALU.add))
            flat = rs[:, :, :].rearrange("p c h -> p (c h)")
            G.then_wait(pl, nc.gpsimd.tensor_tensor(flat, flat, half[:, :].to_broadcast([P, C * 8]), ALU.pow))
            G.then_wait(pl, nc.gpsimd.tensor_scalar(rs[:, :, 0:4], rs[:, :, 0:4], G_DIM ** -0.5, None, ALU.mult))
            pl.wait_ge(s["alpha"], 1)
            pl.wait_ge(s["eg"], 1)

            def normed_keys_queries(m):
                q, k = (qkv[:, m, i * BANK:(i + 1) * BANK] for i in range(2))
                nc.gpsimd.tensor_tensor(heads(k), heads(k), per_head(rs[:, m, 4:8]), ALU.mult).then_inc(s["kn"], 1)
                nc.gpsimd.tensor_tensor(heads(q), heads(q), per_head(rs[:, m, 0:4]), ALU.mult).then_inc(s["qn"], 1)

            normed_keys_queries(0)
            for m in range(C):
                k, v = (qkv[:, m, i * BANK:(i + 1) * BANK] for i in (1, 2))
                pl.wait_ge(s["dec_exp"], m + 1)
                nc.gpsimd.tensor_tensor(heads(decT), heads(decT), same_for_heads(c.k["mask_le"][:, :]), ALU.mult).then_inc(s["decT"], 1)
                for level in range(LEVELS):
                    for gr in range(GROUPS):
                        if level == 0:
                            pl.wait_ge(s["AT"], m + 1)
                        elif level == 1:
                            pl.wait_ge(s["U"], n_u(m, 0, gr))
                        else:
                            pl.wait_ge(s["X_there"], n_x(m, level - 1, gr))
                        nc.gpsimd.tensor_tensor(cols(M, gr).rearrange("p (h d) -> p h d", h=2),
                                                cols(AT, gr).rearrange("p (h d) -> p h d", h=2),
                                                c.k["level_masks"][:, level, :].unsqueeze(1).to_broadcast([P, 2, P]), ALU.mult).then_inc(s["M"], 1)
                    if level == 2:
                        if m:
                            pl.wait_ge(s["s_there"], m)
                        pl.wait_ge(s["kn"], m + 1)
                        nc.gpsimd.tensor_tensor(heads(kdec), heads(k), per_head(eg[:, 1, m, :]), ALU.mult).then_inc(s["kdec"], 1)
                    if level == 3:
                        nc.gpsimd.tensor_tensor(heads(v), heads(v), per_head(beta[:, m, :]), ALU.mult).then_inc(s["vb"], 1)
                    if level == 4 and m + 1 < C:
                        normed_keys_queries(m + 1)
                pl.wait_ge(s["o_squared"], 4 * m + 4)
                G.then_wait(pl, nc.gpsimd.tensor_scalar(ors[:, m, :], oss[:, m, :], 1.0 / G_DIM, EPS, ALU.mult, ALU.add))
                nc.gpsimd.tensor_tensor(ors[:, m, :], ors[:, m, :], half[:, :].to_broadcast([P, H]), ALU.pow).then_inc(s["ors"], 1)


def retention_inputs(c, hT, q, k, v, gate, tables):
    nc = c.nc
    NB = 4
    cos, sin = tables
    GROUPS = TT // 2
    with ExitStack() as mem:
        tmp = c.sb(mem, "ri_tmp", [P, 2, BANK])
        tables_there = c.sem(mem, "ri_tables_there")
        product = c.sem(mem, "ri_product")
        taken = c.sem(mem, "ri_taken")
        turned = c.sem(mem, "ri_rotated")
        V = Steps(nc, mem, "ri_dve_steps")
        block = mem.enter_context(nc.Block())

        def place(t, i):
            n, m = i // GROUPS % 2, i % GROUPS
            return t[:, 2 * m:2 * m + 2, n * HALF:(n + 1) * HALF]

        def bank(i):
            return c.bank(i % NB).rearrange("p (t n) -> p t n", t=2)

        @block.sync
        def _(sp):
            sp.dma_start(cos[:, :, :], c.io["t_cos"]).then_inc(tables_there, 16)
            sp.dma_start(sin[:, :, :], c.io["t_sin"]).then_inc(tables_there, 16)
            c.load_chunks(sp, C_OUT2 + 1)

        @block.tensor
        def _(pe):
            for i in range(8 * GROUPS):
                j = C_IN2 + 8 + i // GROUPS
                if i % GROUPS == 0:
                    c.wait_split(pe, j)
                if i >= NB:
                    pe.wait_ge(taken, i - NB + 1)
                split_tokens(nc.tensor, c.bank(i % NB), hT, i % GROUPS, c.parts(j)).then_inc(product, 1)

        def chunk_used(eng, i):
            if i % GROUPS == GROUPS - 1:
                eng.sem_inc(c.used, 1)

        @block.vector
        def _(dve):
            def split_next(i):
                if i % GROUPS == 1:
                    c.split_chunk(dve, C_IN2 + 9 + i // GROUPS)

            dve.wait_ge(tables_there, 32)
            for i in range(4 * GROUPS):
                m = i % GROUPS
                dst = place((q, k)[i // (2 * GROUPS)], i)
                dve.wait_ge(product, i + 1)
                chunk_used(dve, i)
                half = tmp[:, i % 2, :].rearrange("p (t n) -> p t n", t=2)
                for t in range(2):
                    two = lambda ap: ap.rearrange("p (h d) -> p h d", h=2)
                    b = bank(i)[:, t, :]
                    V.done(nc.vector.tensor_tensor(two(dst[:, t, :]), two(b),
                                                   cos[:, 2 * m + t, :].unsqueeze(1).to_broadcast([P, 2, P]), ALU.mult))
                    halves = b.rearrange("p (h two d) -> p h two d", h=2, two=2)[:, :, ::-1, :]
                    for x in range(2):
                        ins = nc.vector.tensor_tensor(two(half[:, t, :])[:, :, x * 64:(x + 1) * 64], halves[:, :, x, :],
                                                      sin[:, 2 * m + t, x * 64:(x + 1) * 64].unsqueeze(1).to_broadcast([P, 2, 64]),
                                                      ALU.mult)
                        if t and x:
                            ins.then_inc(taken, 1)
                        else:
                            V.done(ins)
                V.settle(dve)
                dve.wait_ge(taken, i + 1)
                nc.vector.tensor_tensor(dst, dst, half, ALU.add).then_inc(turned, 1)
                split_next(i)
            for i in range(4 * GROUPS, 6 * GROUPS):
                dve.wait_ge(product, i + 1)
                chunk_used(dve, i)
                nc.vector.tensor_copy(place(v, i), bank(i)).then_inc(taken, 1)
                split_next(i)
            for i in range(6 * GROUPS, 8 * GROUPS):
                dve.wait_ge(taken, i + 1)
                g = place(gate, i)
                norm = c.k["norm_b"][:, i // GROUPS % 2 * HALF:(i // GROUPS % 2 + 1) * HALF]
                nc.vector.tensor_tensor(g, g, norm.unsqueeze(1).to_broadcast([P, 2, HALF]), ALU.mult)
                split_next(i)

        @block.scalar
        def _(act):
            act.wait_ge(taken, 6 * GROUPS)
            for i in range(6 * GROUPS, 8 * GROUPS):
                act.wait_ge(product, i + 1)
                chunk_used(act, i)
                nc.scalar.activation(place(gate, i), bank(i), ACT.Silu).then_inc(taken, 1)


def retention_decay(h):
    return 1.0 - 2.0 ** (-5.0 - h)


def retention(c, q, k, v, o):
    nc = c.nc
    H, C = A_HEADS, TT
    with ExitStack() as mem:
        kT, qdT, attnT = (c.sb(mem, "rt_" + n, [P, BANK])[:, :] for n in ("kT", "qdT", "attnT"))
        kd = c.sb(mem, "rt_kd", [P, 2, BANK])
        state = c.sb(mem, "rt_state", [P, BANK])[:, :]
        decay = c.sb(mem, "rt_decay", [P, H, P])
        oss = c.sb(mem, "rt_oss", [P, C, H])
        ors = c.sb(mem, "rt_ors", [P, C, H])
        half = c.sb(mem, "rt_half", [P, 1])
        junk = c.raw[:, 0, 0:G_DIM]
        G = Steps(nc, mem, "rt_pool_steps")
        names = ["decay", "qd", "kd", "turned", "turned_copied", "attn_there", "attnT", "o_there", "o_squared", "ors", "o_done",
                 "s_there", "state"]
        s = {n: c.sem(mem, "rt_" + n) for n in names}
        block = mem.enter_context(nc.Block())

        @block.sync
        def _(sp):
            sp.dma_start(decay[:, :, :], c.io["t_decay"]).then_inc(s["decay"], 16)

        @block.gpsimd
        def _(pl):
            G.then_wait(pl, nc.gpsimd.memset(half[:, :], -0.5))

            def norm(m):
                pl.wait_ge(s["o_squared"], 4 * m + 4)
                G.then_wait(pl, nc.gpsimd.tensor_scalar(ors[:, m, :], oss[:, m, :], 1.0 / G_DIM, EPS, ALU.mult, ALU.add))
                nc.gpsimd.tensor_tensor(ors[:, m, :], ors[:, m, :], half[:, :].to_broadcast([P, H]), ALU.pow).then_inc(s["ors"], 1)

            for m in range(C):
                nc.gpsimd.tensor_tensor(heads(q[:, m, :]), heads(q[:, m, :]), per_head(c.k["q_decay"][:, :]), ALU.mult).then_inc(s["qd"], 1)
                if m >= 2:
                    pl.wait_ge(s["s_there"], m - 1)
                nc.gpsimd.tensor_tensor(heads(kd[:, m % 2, :]), heads(k[:, m, :]), per_head(c.k["k_decay"][:, :]), ALU.mult).then_inc(s["kd"], 1)
                if m:
                    norm(m - 1)
            norm(C - 1)

        @block.tensor
        def _(pe):
            for m in range(C):
                pe.wait_ge(s["qd"], m + 1)
                for i, src in enumerate((k, q)):
                    if m:
                        pe.wait_ge(s["turned_copied"], 2 * m - 1 + i)
                    for h in range(H):
                        last = nc.tensor.transpose(head(c.bank(i), h), head(src[:, m, :], h), c.k["ident"][:, :])
                    last.then_inc(s["turned"], 1)
                pe.wait_ge(s["turned_copied"], 2 * m + 2)
                if m:
                    pe.wait_ge(s["attnT"], m)
                for h in range(H):
                    last = nc.tensor.matmul(head(c.bank(2), h), head(kT, h), head(qdT, h), start=True, stop=True)
                last.then_inc(s["attn_there"], 1)
                pe.wait_ge(s["kd"], m + 1)
                if m:
                    pe.wait_ge(s["state"], m)
                for h in range(H):
                    last = nc.tensor.matmul(head(c.bank(6 + m % 2), h), head(kd[:, m % 2, :], h), head(v[:, m, :], h), start=True, stop=True)
                last.then_inc(s["s_there"], 1)
                pe.wait_ge(s["attnT"], m + 1)
                pe.wait_ge(s["state"], m + 1)
                if m >= 2:
                    pe.wait_ge(s["o_done"], m - 1)
                for h in range(H):
                    nc.tensor.matmul(head(c.bank(4 + m % 2), h), head(qdT, h), head(state, h), start=True, stop=False)
                    last = nc.tensor.matmul(head(c.bank(4 + m % 2), h), head(attnT, h), head(v[:, m, :], h), start=False, stop=True)
                last.then_inc(s["o_there"], 1)

        @block.scalar
        def _(act):
            for m in range(C):
                if m:
                    act.wait_ge(s["o_there"], m)
                for i, dst in enumerate((kT, qdT)):
                    act.wait_ge(s["turned"], 2 * m + i + 1)
                    nc.scalar.activation(dst, c.bank(i), ACT.Copy).then_inc(s["turned_copied"], 1)
                act.wait_ge(s["o_there"], m + 1)
                for h in range(H):
                    if 4 * m + h:
                        act.wait_ge(s["o_squared"], 4 * m + h)
                    nc.scalar.activation(junk, head(c.bank(4 + m % 2), h), ACT.Square, accum_out=oss[:, m, h:h + 1]).then_inc(s["o_squared"], 1)

        @block.vector
        def _(dve):
            nc.vector.memset(state, 0.0).then_inc(s["state"], 1)
            dve.wait_ge(s["decay"], 16)
            dve.wait_ge(s["state"], 1)

            def finish(m):
                dve.wait_ge(s["ors"], m + 1)
                for h in range(H):
                    ins = nc.vector.scalar_tensor_tensor(head(o[:, m, :], h), head(c.bank(4 + m % 2), h), ors[:, m, h:h + 1],
                                                         head(o[:, m, :], h), ALU.mult, ALU.mult)
                ins.then_inc(s["o_done"], 1)

            for m in range(C):
                dve.wait_ge(s["attn_there"], m + 1)
                nc.vector.tensor_tensor(attnT, c.bank(2), decay[:, :, :].rearrange("p h k -> p (h k)"), ALU.mult).then_inc(s["attnT"], 1)
                dve.wait_ge(s["o_there"], m + 1)
                dve.wait_ge(s["s_there"], m + 1)
                for h in range(H):
                    ins = nc.vector.scalar_tensor_tensor(head(state, h), head(state, h), retention_decay(h) ** P,
                                                         head(c.bank(6 + m % 2), h), ALU.mult, ALU.add)
                ins.then_inc(s["state"], 1)
                dve.wait_ge(s["state"], m + 2)
                finish(m)


GR = N_GROUPS + N_EXPERTS
ROWS = 64
OVERFLOW = S * 2 // ROWS
PAIRS_AT = OVERFLOW + 2
BLOCKS = N_EXPERTS + OVERFLOW
SLOTS = 4
NEVER = 1.0e30


class Experts:

    def __init__(self, c, mem, places):
        self.c = c
        self.landed = [c.sem(mem, f"expert_landed_{i}") for i in range(SLOTS)]
        self.gate, self.up, self.down = [], [], []
        for p in places:
            self.gate.append(p[:, 0:KT * D_EXPERT].rearrange("p (k n) -> p k n", k=KT))
            self.up.append(p[:, KT * D_EXPERT:2 * KT * D_EXPERT].rearrange("p (k n) -> p k n", k=KT))
            self.down.append(p[:, 2 * KT * D_EXPERT:2 * KT * D_EXPERT + 2 * D].rearrange("p (k n) -> p k n", k=2))

    def load(self, sp, slot, expert):
        io = self.c.io
        pick = slice(expert, expert + 1) if isinstance(expert, int) else bass.ds(expert, 1)
        for dst, w, k in ((self.gate, "w_gate_2", KT), (self.up, "w_up_2", KT), (self.down, "w_down_2", 2)):
            src = io[w][pick, :, :].rearrange("e (k p) n -> p (e k) n", p=P)
            sp.dma_start(dst[slot], src).then_inc(self.landed[slot], 16)

    def there(self, pe, slot, uses):
        pe.wait_ge(self.landed[slot], uses * 48)


def route(c, hT, experts, weights, slots, perm, overflow):
    nc = c.nc
    with ExitStack() as mem:
        def t(name, *shape, dt=F32):
            return c.sb(mem, "ro_" + name, [P, *shape], dt)

        E, NG, PG = N_EXPERTS, N_GROUPS, PER_GROUP
        lg = t("logits", TT, GR)
        gtop, gsum, top1, top2 = (t(n, TT, 1) for n in ("gtop", "gsum", "top1", "top2"))
        gdiff, gfirst, goh = (t(n, TT, NG) for n in ("gdiff", "gfirst", "goh"))
        pick = t("pick", TT, 1)
        tmp = t("tmp", TT, E)
        esel, efirst, oh1, oh2 = (t(n, TT, PG) for n in ("esel", "efirst", "oh1", "oh2"))
        e21 = t("e21", TT, 1)
        OH = t("OH", 2, TT, E)
        M = t("M", TT, E)
        pos = t("pos", TT, E)
        cnt, ov, ovend, ovplace = (t(n, E) for n in ("cnt", "ov", "ovend", "ovplace"))
        over = t("over", E, 16)
        rank, place, place2, slotf = (t(n, TT, 2) for n in ("rank", "place", "place2", "slotf"))
        sloti, blocki, rowi = (t(n, TT * 2, dt=I32) for n in ("sloti", "blocki", "rowi"))
        blockf, rowf = (t(n, TT * 2) for n in ("blockf", "rowf"))
        ohb = t("ohb", 2, BLOCKS + 2)
        ohr = t("ohr", 2, ROWS)
        ovexp = t("ovexp", 1)
        pairs = t("pairs", 1)
        V = Steps(nc, mem, "ro_dve_steps")
        logits_there = c.sem(mem, "ro_logits_there")
        logits_copied = c.sem(mem, "ro_logits_copied")
        logits_turned = c.sem(mem, "ro_logits_turned")
        lgT = c.sb(mem, "ro_logits_by_channel", [GR, S])
        gdiff_ready = c.sem(mem, "ro_gdiff_ready")
        e21_ready = c.sem(mem, "ro_e21_ready")
        exps_ready = c.sem(mem, "ro_exps_ready")
        picks_ready = c.sem(mem, "ro_picks_ready")
        counted = c.sem(mem, "ro_counted")
        onehots = c.sem(mem, "ro_onehots")
        permuted = c.sem(mem, "ro_permuted")
        ovexp_ready = c.sem(mem, "ro_ovexp_ready")
        ovrow_there = c.sem(mem, "ro_ovrow_there")
        block = mem.enter_context(nc.Block())

        @block.sync
        def _(sp):
            sp.wait_ge(logits_there, 2)
            experts.load(sp, 0, 0)

        @block.tensor
        def _(pe):
            for th in range(2):
                for k in range(KT):
                    last = nc.tensor.matmul(c.bank(th, parts=GR), c.k["w_router"][:, k, :], hT[:, k, th * BANK:(th + 1) * BANK],
                                            start=(k == 0), stop=(k == KT - 1))
                last.then_inc(logits_there, 1)
            for th in range(2):
                pe.wait_ge(logits_copied, th + 1)
                for i in range(4):
                    last = nc.tensor.transpose(c.bank(2 + th)[:, i * GR:(i + 1) * GR], lgT[:, (4 * th + i) * P:(4 * th + i + 1) * P],
                                               c.k["ident"][0:GR, 0:GR])
                last.then_inc(logits_turned, 1)
            pe.wait_ge(picks_ready, 1)
            for m in range(TT):
                for j in range(m + 1):
                    nc.tensor.matmul(c.bank(4)[:, m * E:(m + 1) * E], (c.k["mask_lt"] if j == m else c.k["ones"])[:, :], M[:, j, :],
                                     start=(j == 0), stop=(j == m))
            for j in range(TT):
                last = nc.tensor.matmul(c.bank(5)[:, 0:E], c.k["ones"][:, :], M[:, j, :], start=(j == 0), stop=(j == TT - 1))
            last.then_inc(counted, 1)
            pe.wait_ge(ovexp_ready, 1)
            nc.tensor.matmul(c.bank(6)[0:1, 0:P], ovexp[:, :], c.k["ident"][:, :], start=True, stop=True).then_inc(ovrow_there, 1)
            for i in range(2 * TT):
                pe.wait_ge(onehots, i + 1)
                last = nc.tensor.matmul(c.bank(7)[0:ROWS, 0:BLOCKS + 2], ohr[:, i % 2, :], ohb[:, i % 2, :],
                                        start=(i == 0), stop=(i == 2 * TT - 1))
                last.then_inc(permuted, 1)

        @block.scalar
        def _(act):
            for th in range(2):
                act.wait_ge(logits_there, th + 1)
                nc.scalar.activation(lgT[:, th * BANK:(th + 1) * BANK], c.bank(th, parts=GR), ACT.Copy).then_inc(logits_copied, 1)
            for th in range(2):
                act.wait_ge(logits_turned, th + 1)
                nc.scalar.activation(lg[:, 4 * th:4 * th + 4, :], c.bank(2 + th)[:, 0:4 * GR].rearrange("p (t n) -> p t n", n=GR),
                                     ACT.Copy).then_inc(logits_copied, 1)
            act.wait_ge(gdiff_ready, 1)
            nc.scalar.activation(gdiff[:, :, :], gdiff[:, :, :], ACT.Exp).then_inc(exps_ready, 1)
            act.wait_ge(e21_ready, 1)
            nc.scalar.activation(e21[:, :, :], e21[:, :, :], ACT.Exp).then_inc(exps_ready, 1)

        @block.vector
        def _(dve):
            v = nc.vector

            def do(ins):
                V.then_wait(dve, ins)

            def wide(ap, n):
                return ap.to_broadcast([P, TT, n])

            def first_of(dst, values, top, first):
                do(v.tensor_tensor(first, values, wide(top, PG), ALU.is_equal))
                do(v.scalar_tensor_tensor(first, first, -float(PG), c.k["iota"][:, 0:PG].unsqueeze(1).to_broadcast([P, TT, PG]),
                                          ALU.mult, ALU.add))
                do(v.tensor_reduce(pick[:, :, :], first, AX.X, ALU.min))
                do(v.tensor_tensor(dst, first, wide(pick[:, :, :], PG), ALU.is_equal))

            dve.wait_ge(logits_copied, 4)
            gl = lg[:, :, 0:NG]
            do(v.tensor_reduce(gtop[:, :, :], gl, AX.X, ALU.max))
            v.tensor_tensor(gdiff[:, :, :], gl, wide(gtop[:, :, :], NG), ALU.subtract).then_inc(gdiff_ready, 1)
            first_of(goh[:, :, :], gl, gtop[:, :, :], gfirst[:, :, :])
            for m in range(TT):
                V.done(v.tensor_tensor(tmp[:, m, :].rearrange("p (g e) -> p g e", g=NG),
                                       lg[:, m, NG:GR].rearrange("p (g e) -> p g e", g=NG),
                                       goh[:, m, :].unsqueeze(2).to_broadcast([P, NG, PG]), ALU.mult))
            V.settle(dve)
            do(v.tensor_reduce(esel[:, :, :], tmp[:, :, :].rearrange("p t (g e) -> p t e g", g=NG), AX.X, ALU.add))
            do(v.tensor_reduce(top1[:, :, :], esel[:, :, :], AX.X, ALU.max))
            first_of(oh1[:, :, :], esel[:, :, :], top1[:, :, :], efirst[:, :, :])
            do(v.scalar_tensor_tensor(esel[:, :, :], oh1[:, :, :], -NEVER, esel[:, :, :], ALU.mult, ALU.add))
            do(v.tensor_reduce(top2[:, :, :], esel[:, :, :], AX.X, ALU.max))
            v.tensor_tensor(e21[:, :, :], top2[:, :, :], top1[:, :, :], ALU.subtract).then_inc(e21_ready, 1)
            first_of(oh2[:, :, :], esel[:, :, :], top2[:, :, :], efirst[:, :, :])
            for m in range(TT):
                for k, oh in enumerate((oh1, oh2)):
                    V.done(v.tensor_tensor(OH[:, k, m, :].rearrange("p (g e) -> p g e", g=NG),
                                           goh[:, m, :].unsqueeze(2).to_broadcast([P, NG, PG]),
                                           oh[:, m, :].unsqueeze(1).to_broadcast([P, NG, PG]), ALU.mult))
            V.settle(dve)
            v.tensor_tensor(M[:, :, :], OH[:, 0, :, :], OH[:, 1, :, :], ALU.add).then_inc(picks_ready, 1)
            dve.wait_ge(exps_ready, 2)
            do(v.tensor_reduce(gsum[:, :, :], gdiff[:, :, :], AX.X, ALU.add))
            do(v.scalar_tensor_tensor(gsum[:, :, :], e21[:, :, :], 1.0, gsum[:, :, :], ALU.add, ALU.mult))
            do(v.reciprocal(weights[:, 0, :], gsum[:, :, :].rearrange("p t o -> p (t o)")))
            do(v.tensor_tensor(weights[:, 1, :], weights[:, 0, :], e21[:, :, :].rearrange("p t o -> p (t o)"), ALU.mult))
            dve.wait_ge(counted, 1)
            do(v.tensor_copy(pos[:, :, :], c.bank(4).rearrange("p (t e) -> p t e", e=E)))
            do(v.tensor_copy(cnt[:, :], c.bank(5)[:, 0:E]))
            do(v.tensor_tensor(over[:, :, :], cnt[:, :].unsqueeze(2).to_broadcast([P, E, 16]),
                               c.k["thresholds"][:, :].unsqueeze(1).to_broadcast([P, E, 16]), ALU.is_gt))
            do(v.tensor_reduce(ov[:, :], over[:, :, :], AX.X, ALU.add))
            do(v.tensor_tensor_scan(ovend[:, :], c.k["ones"][:, 0:1].to_broadcast([P, E]), ov[:, :], 0.0, ALU.mult, ALU.add))
            do(v.scalar_tensor_tensor(ovplace[:, :], ovend[:, :], float(N_EXPERTS - 1), ov[:, :], ALU.add, ALU.subtract))
            do(v.tensor_scalar(cnt[:, :], ovend[:, :], c.k["iota_p"][:, 0:1], None, ALU.is_le))
            do(v.tensor_reduce(ovexp[:, :], cnt[:, :], AX.X, ALU.add))
            v.tensor_scalar(ovexp[:, :], ovexp[:, :], float(E - 1), None, ALU.min).then_inc(ovexp_ready, 1)
            do(v.tensor_scalar(pairs[:, :], ovend[:, E - 1:E], 1.0, None, ALU.add))
            do(v.tensor_scalar(pairs[:, :], pairs[:, :], 4.0, None, ALU.max))
            do(v.tensor_copy(sloti[:, 0:1], pairs[:, :]))
            do(v.tensor_scalar(pairs[:, :], pairs[:, :], -2.0, None, ALU.add))
            do(v.tensor_copy(sloti[:, 1:2], pairs[:, :]))
            do(v.tensor_scalar(overflow[0:1, PAIRS_AT:PAIRS_AT + 2], sloti[0:1, 0:2], 1, None, ALU.arith_shift_right))
            for dst, table in ((rank, None), (place, c.k["iota"]), (place2, ovplace)):
                for k in range(2):
                    other = pos[:, :, :] if table is None else table[:, 0:E].unsqueeze(1).to_broadcast([P, TT, E])
                    do(v.tensor_tensor(tmp[:, :, :], OH[:, k, :, :], other, ALU.mult))
                    do(v.tensor_reduce(dst[:, :, k:k + 1], tmp[:, :, :], AX.X, ALU.add))
            do(v.tensor_tensor(place2[:, :, :], place2[:, :, :], place[:, :, :], ALU.subtract))
            do(v.scalar_tensor_tensor(place2[:, :, :], rank[:, :, :], float(ROWS), place2[:, :, :], ALU.is_ge, ALU.mult))
            do(v.tensor_tensor(place[:, :, :], place[:, :, :], place2[:, :, :], ALU.add))
            do(v.scalar_tensor_tensor(slotf[:, :, :], place[:, :, :], float(ROWS), rank[:, :, :], ALU.mult, ALU.add))
            flat = slotf[:, :, :].rearrange("p t k -> p (t k)")
            do(v.tensor_copy(sloti[:, :], flat))
            do(v.tensor_copy(slots[:, :], flat))
            do(v.tensor_scalar(blocki[:, :], sloti[:, :], 6, None, ALU.arith_shift_right))
            do(v.tensor_scalar(rowi[:, :], sloti[:, :], ROWS - 1, None, ALU.bitwise_and))
            do(v.tensor_copy(blockf[:, :], blocki[:, :]))
            do(v.tensor_copy(rowf[:, :], rowi[:, :]))
            for i in range(2 * TT):
                if i >= 2:
                    dve.wait_ge(permuted, i - 1)
                do(v.tensor_scalar(ohr[:, i % 2, :], c.k["iota"][:, 0:ROWS], rowf[:, i:i + 1], c.k["token"][:, i // 2:i // 2 + 1],
                                   ALU.is_equal, ALU.mult))
                v.tensor_scalar(ohb[:, i % 2, :], c.k["iota"][:, 0:BLOCKS + 2], blockf[:, i:i + 1], None, ALU.is_equal).then_inc(onehots, 1)
            dve.wait_ge(ovrow_there, 1)
            do(v.tensor_copy(overflow[0:1, 0:PAIRS_AT], c.bank(6)[0:1, 0:PAIRS_AT]))
            dve.wait_ge(permuted, 2 * TT)
            do(v.tensor_copy(perm[:, :], c.bank(7)[0:ROWS, 0:BLOCKS + 2]))


def run_experts(c, experts, h_rows, y_rows, perm, overflow):
    nc = c.nc
    HT = D_EXPERT // P
    with ExitStack() as mem:
        idx = c.sb(mem, "ex_idx", [ROWS, 2], U32)
        xg = c.sb(mem, "ex_x", [ROWS, 2, D])
        xT = c.sb(mem, "ex_xT", [P, 2, KT, ROWS])
        sg = c.sb(mem, "ex_silu", [P, 2, HT * ROWS])
        h = c.sb(mem, "ex_h", [P, 2, HT * ROWS])
        y = c.sb(mem, "ex_y", [ROWS, 2, D])
        idx_ready = c.sem(mem, "ex_idx_ready")
        x_there = [c.sem(mem, f"ex_x_there_{i}") for i in range(2)]
        turned = c.sem(mem, "ex_turned")
        xT_ready = c.sem(mem, "ex_xT_ready")
        gate_up = c.sem(mem, "ex_gate_up_there")
        silu_done = c.sem(mem, "ex_silu_done")
        h_ready = c.sem(mem, "ex_h_ready")
        y_there = c.sem(mem, "ex_y_there")
        y_act = c.sem(mem, "ex_y_first_half_copied")
        y_dve = c.sem(mem, "ex_y_second_half_copied")
        stored = [c.sem(mem, f"ex_y_stored_{i}") for i in range(2)]
        passed_act, passed_pe, passed_pool = (c.sem(mem, "ex_passed_" + n) for n in ("act", "pe", "pool"))
        block = mem.enter_context(nc.Block())
        FIRST = N_EXPERTS // SLOTS

        def n_pairs(eng):
            return eng.value_load(overflow[0:1, PAIRS_AT:PAIRS_AT + 1], min_val=1, max_val=OVERFLOW // 2)

        def started(b, n):
            return not isinstance(b, int) or b >= n

        @block.sync
        def _(sp):
            for u in range(SLOTS):
                sp.wait_ge(y_there, u + 1)
                experts.load(sp, u, SLOTS + u)
            with sp.Fori(2, FIRST) as i:
                for u in range(SLOTS):
                    sp.wait_ge(y_there, i * SLOTS + (u - SLOTS + 1))
                    experts.load(sp, u, i * SLOTS + u)
            for u in range(2):
                sp.wait_ge(y_there, N_EXPERTS - SLOTS + u + 1)
                experts.load(sp, u, sp.value_load(overflow[0:1, u:u + 1], min_val=0, max_val=N_EXPERTS - 1))
            more = sp.value_load(overflow[0:1, PAIRS_AT + 1:PAIRS_AT + 2], min_val=1, max_val=OVERFLOW // 2 - 1)
            with sp.Fori(0, more) as i:
                for u in range(2):
                    e = sp.value_load(overflow[0:1, bass.ds(i * 2 + (2 + u), 1)], min_val=0, max_val=N_EXPERTS - 1)
                    sp.wait_ge(y_there, i * 2 + (N_EXPERTS + u + 1))
                    experts.load(sp, u, e)
            sp.wait_ge(y_there, N_EXPERTS)

        @block.gpsimd
        def _(pl):
            def gather(b, s):
                if started(b, 2):
                    pl.wait_ge(turned, b - 1)
                col = slice(b, b + 1) if isinstance(b, int) else bass.ds(b, 1)
                nc.gpsimd.tensor_copy(idx[:, s:s + 1], perm[:, col]).then_inc(idx_ready, 1)
                pl.wait_ge(idx_ready, b + 1)
                pl.sem_inc(passed_pool, 1)
                nc.gpsimd.indirect_dma_start(
                    out=xg[:, s, :], out_offset=None, in_=h_rows,
                    in_offset=bass.IndirectOffsetOnAxis(ap=idx[:, s:s + 1], axis=0)).then_inc(x_there[s], 16)

            gather(0, 0)
            for u in range(SLOTS):
                gather(u + 1, (u + 1) % 2)
            with pl.Fori(1, FIRST) as i:
                for u in range(SLOTS):
                    gather(i * SLOTS + (u + 1), (u + 1) % 2)
            with pl.Fori(0, n_pairs(pl)) as i:
                for u in range(2):
                    gather(i * 2 + (N_EXPERTS + u + 1), (u + 1) % 2)

        @block.tensor
        def _(pe):
            def turn(b, s, n):
                if started(b, 2):
                    pe.wait_ge(xT_ready, b - 1)
                pe.wait_ge(x_there[s], n * 16)
                pe.sem_inc(passed_pe, 1)
                for k in range(KT):
                    last = nc.tensor.transpose(c.bank(s)[:, k * ROWS:(k + 1) * ROWS], xg[:, s, k * P:(k + 1) * P],
                                               c.k["ident"][0:ROWS, 0:ROWS])
                last.then_inc(turned, 1)

            def one(b, u, uses):
                s = u % 2
                experts.there(pe, u, uses)
                pe.wait_ge(xT_ready, b + 1)
                if started(b, 2):
                    pe.wait_ge(h_ready, b - 1)
                for i, w in enumerate((experts.gate, experts.up)):
                    for f in range(HT):
                        for k in range(KT):
                            at = (i * HT + f) * ROWS
                            last = nc.tensor.matmul(c.bank(2 + s)[:, at:at + ROWS], w[u][:, k, f * P:(f + 1) * P], xT[:, s, k, :],
                                                    start=(k == 0), stop=(k == KT - 1))
                last.then_inc(gate_up, 1)
                turn(b + 1, 1 - s, count_of(b + 1))
                pe.wait_ge(h_ready, b + 1)
                if started(b, 2):
                    pe.wait_ge(y_act, b - 1)
                    pe.wait_ge(y_dve, b - 1)
                for n in range(2):
                    for f in range(HT):
                        last = nc.tensor.matmul(c.bank(4 + 2 * s + n)[0:ROWS, :], h[:, s, f * ROWS:(f + 1) * ROWS],
                                                experts.down[u][:, f, n * BANK:(n + 1) * BANK], start=(f == 0), stop=(f == HT - 1))
                last.then_inc(y_there, 1)

            def count_of(b):
                return counts[0]

            counts = [None]
            turn(0, 0, 1)
            for u in range(SLOTS):
                counts[0] = (u + 1) // 2 + 1
                one(u, u, 1)
            with pe.Fori(1, FIRST) as i:
                for u in range(SLOTS):
                    counts[0] = i * 2 + ((u + 1) // 2 + 1)
                    one(i * SLOTS + u, u, i + 1)
            with pe.Fori(0, n_pairs(pe)) as i:
                for u in range(2):
                    counts[0] = i + (N_EXPERTS // 2 + (u + 1) // 2 + 1)
                    one(i * 2 + (N_EXPERTS + u), u, i + (FIRST + 1))

        @block.scalar
        def _(act):
            def copy_x(b, s):
                act.wait_ge(turned, b + 1)
                if started(b, 2):
                    act.wait_ge(gate_up, b - 1)
                nc.scalar.activation(xT[:, s, :, :].rearrange("p k r -> p (k r)"), c.bank(s), ACT.Copy).then_inc(xT_ready, 1)

            def one(b, u):
                s = u % 2
                act.wait_ge(gate_up, b + 1)
                if started(b, 2):
                    act.wait_ge(h_ready, b - 1)
                nc.scalar.activation(sg[:, s, :], c.bank(2 + s)[:, 0:HT * ROWS], ACT.Silu).then_inc(silu_done, 1)
                copy_x(b + 1, 1 - s)
                act.wait_ge(y_there, b + 1)
                if started(b, 2):
                    act.wait_ge(stored[s], (store_count[0] - 1) * 16)
                nc.scalar.activation(y[:, s, 0:BANK], c.bank(4 + 2 * s)[0:ROWS, :], ACT.Copy).then_inc(y_act, 1)
                act.wait_ge(y_act, b + 1)
                act.wait_ge(y_dve, b + 1)
                rows_ = slice(b * ROWS, (b + 1) * ROWS) if isinstance(b, int) else bass.ds(b * ROWS, ROWS)
                act.dma_start(y_rows[rows_, :], y[:, s, :]).then_inc(stored[s], 16)

            store_count = [None]
            copy_x(0, 0)
            for u in range(SLOTS):
                store_count[0] = u // 2 + 1
                one(u, u)
            with act.Fori(1, FIRST) as i:
                for u in range(SLOTS):
                    store_count[0] = i * 2 + (u // 2 + 1)
                    one(i * SLOTS + u, u)
            with act.Fori(0, n_pairs(act)) as i:
                for u in range(2):
                    store_count[0] = i + (N_EXPERTS // 2 + 1)
                    one(i * 2 + (N_EXPERTS + u), u)
            n = n_pairs(act)
            for s in range(2):
                act.wait_ge(stored[s], n * 16 + N_EXPERTS // 2 * 16)
                act.sem_inc(passed_act, 1)

        @block.vector
        def _(dve):
            def one(b, u, store_uses):
                s = u % 2
                dve.wait_ge(silu_done, b + 1)
                if started(b, 2):
                    dve.wait_ge(y_there, b - 1)
                nc.vector.tensor_tensor(h[:, s, :], sg[:, s, :], c.bank(2 + s)[:, HT * ROWS:2 * HT * ROWS], ALU.mult).then_inc(h_ready, 1)
                dve.wait_ge(y_there, b + 1)
                if started(b, 2):
                    dve.wait_ge(stored[s], store_uses * 16)
                nc.vector.tensor_copy(y[:, s, BANK:D], c.bank(5 + 2 * s)[0:ROWS, :]).then_inc(y_dve, 1)

            for u in range(SLOTS):
                one(u, u, u // 2)
            with dve.Fori(1, FIRST) as i:
                for u in range(SLOTS):
                    one(i * SLOTS + u, u, i * 2 + u // 2)
            with dve.Fori(0, n_pairs(dve)) as i:
                for u in range(2):
                    one(i * 2 + (N_EXPERTS + u), u, i + N_EXPERTS // 2)


def combine(c, x_sb, y_rows, weights, slots, out):
    nc = c.nc
    with ExitStack() as mem:
        g = c.sb(mem, "co_rows", [P, 4, D])
        junk = c.sb(mem, "co_squares", [P, 2, D])
        ss = c.sb(mem, "co_ss", [P, TT])
        rstd = c.sb(mem, "co_rstd", [P, TT])
        half = c.sb(mem, "co_half", [P, 1])
        G = Steps(nc, mem, "co_pool_steps")
        rows_there = [c.sem(mem, f"co_rows_there_{i}") for i in range(4)]
        summed = c.sem(mem, "co_summed")
        squared = c.sem(mem, "co_squared")
        rstd_ready = c.sem(mem, "co_rstd_ready")
        normed = c.sem(mem, "co_normed")
        stored = c.sem(mem, "co_stored")
        block = mem.enter_context(nc.Block())

        @block.gpsimd
        def _(pl):
            G.then_wait(pl, nc.gpsimd.memset(half[:, :], -0.5))

            def gather(i):
                if i >= 4:
                    pl.wait_ge(summed, i - 3)
                nc.gpsimd.indirect_dma_start(
                    out=g[:, i % 4, :], out_offset=None, in_=y_rows,
                    in_offset=bass.IndirectOffsetOnAxis(ap=slots[:, i:i + 1], axis=0)).then_inc(rows_there[i % 4], 16)

            for i in range(4):
                gather(i)
            for m in range(TT):
                pl.wait_ge(squared, m + 1)
                G.then_wait(pl, nc.gpsimd.tensor_scalar(rstd[:, m:m + 1], ss[:, m:m + 1], 1.0 / D, EPS, ALU.mult, ALU.add))
                nc.gpsimd.tensor_tensor(rstd[:, m:m + 1], rstd[:, m:m + 1], half[:, :], ALU.pow).then_inc(rstd_ready, 1)
                for i in (2 * m + 4, 2 * m + 5):
                    if i < 2 * TT:
                        gather(i)

        @block.vector
        def _(dve):
            def norm(m):
                dve.wait_ge(rstd_ready, m + 1)
                x = x_sb[:, m, :]
                nc.vector.scalar_tensor_tensor(x, x, rstd[:, m:m + 1], c.k["final_norm"][:, :], ALU.mult, ALU.mult).then_inc(normed, 1)

            for m in range(TT):
                for k in range(2):
                    i = 2 * m + k
                    dve.wait_ge(rows_there[i % 4], 16 * (i // 4 + 1))
                    if k:
                        dve.wait_ge(summed, i)
                    x = x_sb[:, m, :]
                    nc.vector.scalar_tensor_tensor(x, g[:, i % 4, :], weights[:, k, m:m + 1], x, ALU.mult, ALU.add).then_inc(summed, 1)
                if m:
                    norm(m - 1)
            norm(TT - 1)

        @block.scalar
        def _(act):
            for m in range(TT):
                act.wait_ge(summed, 2 * m + 2)
                if m >= 2:
                    act.wait_ge(squared, m - 1)
                nc.scalar.activation(junk[:, m % 2, :], x_sb[:, m, :], ACT.Square, accum_out=ss[:, m:m + 1]).then_inc(squared, 1)

        @block.sync
        def _(sp):
            for m in range(TT):
                sp.wait_ge(normed, m + 1)
                sp.dma_start(out[0, m * P:(m + 1) * P, :], x_sb[:, m, :]).then_inc(stored, 16)
            sp.wait_ge(stored, 16 * TT)


def recycle_semaphores(c, after=None):
    nc = c.nc
    ids = sorted(nc.released_uncleared_semaphores)
    with nc.Block() as block:
        @block.gpsimd
        def _(pl):
            if after is not None:
                pl.wait_ge(after, 16)
            start = 0
            for i in range(1, len(ids) + 1):
                if i == len(ids) or ids[i] != ids[i - 1] + 1:
                    pl.sem_clear(range(ids[start], ids[i - 1] + 1))
                    start = i


def build(nc, io, out):
    with ExitStack() as ctx:
        c = Chip(nc, ctx, io)
        load_consts(c, ctx, [("ident", [P, P]), ("ones", [P, P]), ("mask_le", [P, P]), ("mask_gt", [P, P])])
        x_rows, mem_rows = io["x"][0], io["mem"][0]
        x_sb = c.sb(ctx, "x", [P, TT, D])
        flat = x_sb[:, :, :].rearrange("p t n -> p (t n)")

        def part_places(mem, name):
            c.split_ring = c.sb(mem, "split_weights_" + name, [P, RING, 2, KT, HALF])
            return [c.sb(mem, "hT_%s_%s" % (part, name), [P, KT, S])[:, :, :] for part in ("upper", "lower")]

        hmT = flat[:, 0:4 * S].rearrange("p (k n) -> p k n", k=4)
        memT = flat[:, 4 * S:6 * S].rearrange("p (k n) -> p k n", k=KT)
        hnT = flat[:, 4 * S:6 * S].rearrange("p (k n) -> p k n", k=2)
        hcT = flat[:, 6 * S:8 * S].rearrange("p (k n) -> p k n", k=2)
        with ExitStack() as b1:
            hT = c.sb(b1, "hT", [P, KT, S])
            with ExitStack() as rg:
                c.ring = c.sb(rg, "weight_ring", [P, RING, KT, BANK])
                with ExitStack() as ml:
                    load_consts(c, ml, [
                        ("pick8", [8, 8, P]), ("dir8", [8, 4]), ("b_if", [8, 2]), ("g_mix", [P, KT]), ("g_mem", [P, KT]),
                        ("w_if", [P, KT, 40]), ("conv1", [P, 4, M_CONV]), ("conv1_b", [P, 4]), ("g_mlstm", [P, BANK])])
                    tiles = [(x_rows[i * P:(i + 1) * P, :], c.k["g_mix"], hT, i * P) for i in range(TT)]
                    tiles += [(mem_rows[i * P:(i + 1) * P, :], c.k["g_mem"], memT, i * P) for i in range(MEM // P)]
                    norm_transpose(c, "n1", tiles, RING, source="dram")
                    qk_raw = c.sb(ml, "qk_raw", [P, 4, S + M_CONV - 1])
                    v_sb = c.sb(ml, "v_m", [P, TT, M_HEADS, M_V + 1])
                    og = c.sb(ml, "og", [P, TT, BANK])
                    m_row = c.sb(ml, "ml_m_row", [8, S])
                    Pt = c.sb(ml, "ml_weights", [P, TT * (TT + 1) * P])

                    def row(i):
                        return m_row[:, :] if i == 5 else Pt[0:8, i * S:(i + 1) * S]

                    mlstm_inputs(c, hT, qk_raw, hmT, v_sb, og, row)
                    mlstm(c, qk_raw, hmT, v_sb, og, m_row, Pt, row, hcT)
                with ExitStack() as at:
                    load_consts(c, at, [("g_heads", [P, 8])])
                    naT = c.sb(at, "naT", [P, 4, S])
                    v_na = c.sb(at, "v_na", [P, TT, 256])
                    qmT = c.sb(at, "qmT", [P, 2, S])
                    kmT = c.sb(at, "kmT", [P, 2, MEM])
                    v_mem = c.sb(at, "v_mem", [P, MEM // P, 256])
                    na_tok = c.sb(at, "na_tok", [P, TT, 256])
                    me_tok = c.sb(at, "me_tok", [P, TT, 256])
                    attention_inputs(c, hT, memT, naT, v_na, qmT, kmT, v_mem)
                    q_wide = flat[:, 4 * S:8 * S].rearrange("p (k n) -> p k n", k=4)
                    neighbourhood(c, naT, v_na, na_tok, q_wide)
                    memory_attention(c, qmT, kmT, v_mem, me_tok, q_wide)
                    transpose_tokens(c, "tr1", [(na_tok, hnT, 256), (me_tok, hcT, 256)])
            h_parts = part_places(b1, "1")
            gated_branches(c, hT, h_parts, [(hmT, io["w_proj_mlstm"]), (hnT, io["w_proj_na"]), (hcT, io["w_proj_mem"])], hT)
            project_add(c, "out1", h_parts, C_OUT, x_sb, C_FFN + 1, first_load=x_rows, whole=hT)
        parts = ctx.enter_context(ExitStack())
        h_parts = part_places(parts, "2")
        with ExitStack() as n2:
            load_consts(c, n2, [("g_ffn_row", [P, D])])
            tiles = [(x_sb[:, i, :], c.k["g_ffn_row"][:, :], h_parts[1], i * P) for i in range(TT)]
            norm_transpose(c, "n2", tiles, 0, upper=h_parts[0], then_split=C_FFN)
        with ExitStack() as ff:
            u_parts = [c.sb(ff, "uT_" + part, [P, KT, S])[:, :, :] for part in ("upper", "lower")]
            ffn(c, h_parts, x_sb, u_parts)
        recycle_semaphores(c)
        second = ctx.enter_context(ExitStack())
        load_consts(c, second, [
            ("level_masks", [P, LEVELS, P]), ("w_ba", [P, KT, 8]), ("conv2", [P, 12, A_CONV_K]),
            ("norm_a", [P, P]), ("norm_b", [P, BANK]), ("a_log", [P, 4]), ("dt_bias", [P, 4]), ("q_decay", [P, 4]),
            ("k_decay", [P, 4]), ("zeros", [P, 256])])
        y_rows = nc.dram_tensor("y_rows", (BLOCKS * ROWS, D), F32, kind="Internal").ap()
        x2_dram = nc.dram_tensor("x2_rows", (S, D), F32, kind="Internal").ap()
        with ExitStack() as n3:
            load_consts(c, n3, [("attn_norm_row", [P, D])])
            tiles = [(x_sb[:, i, :], c.k["attn_norm_row"][:, :], h_parts[1], i * P) for i in range(TT)]
            norm_transpose(c, "n3", tiles, 0, upper=h_parts[0])
        rows_cleared = c.sem(ctx, "y_rows_cleared")
        spill(c, "x2", x_sb[:, :, :], x2_dram, clear=y_rows[N_EXPERTS * ROWS:, :], cleared=rows_cleared)
        o_a, o_b = x_sb[:, :, 0:BANK], x_sb[:, :, BANK:D]
        with ExitStack() as dr:
            qkv = c.sb(dr, "qkv_a", [P, TT, 3 * BANK])
            small = c.sb(dr, "beta_alpha", [P, TT, 8])
            ss = c.sb(dr, "dr_ss", [P, TT, 8])
            delta_inputs(c, h_parts, qkv, o_a, small, ss, o_b)
            delta_rule(c, qkv, o_a, small, ss, o_b)
        with ExitStack() as rt:
            q, k, v = (c.sb(rt, "rt_" + n, [P, TT, BANK]) for n in "qkv")
            with ExitStack() as tb:
                tables = c.sb(tb, "t_cos", [P, TT, P]), c.sb(tb, "t_sin", [P, TT, P])
                retention_inputs(c, h_parts, q, k, v, o_b, tables)
            retention(c, q, k, v, o_b)
        transpose_tokens(c, "tr2", [(o_a, h_parts[1][:, 0:4, :], BANK), (o_b, h_parts[1][:, 4:8, :], BANK)],
                         upper=[h_parts[0][:, 0:4, :], h_parts[0][:, 4:8, :]])
        project_add(c, "out2", h_parts, C_OUT2, x_sb, len(c.chunks), first_load=x2_dram)
        recycle_semaphores(c, after=rows_cleared)
        second.close()
        parts.close()
        load_consts(c, ctx, [
            ("ffn_norm", [P, KT]), ("ffn_norm_row", [P, D]), ("final_norm", [P, D]), ("mask_lt", [P, P]),
            ("w_router", [P, KT, GR]), ("iota", [P, BLOCKS + 2]), ("iota_p", [P, 1]), ("thresholds", [P, 16]),
            ("token", [P, TT])])
        h_rows = nc.dram_tensor("h_rows", (S, D), F32, kind="Internal").ap()
        with ExitStack() as moe:
            weights = c.sb(moe, "mo_weights", [P, 2, TT])
            slots = c.sb(moe, "mo_slots", [P, 2 * TT], U32)
            perm = c.sb(moe, "mo_perm", [ROWS, BLOCKS + 2], U32)
            overflow = c.sb(moe, "mo_overflow", [1, PAIRS_AT + 2], I32)
            with ExitStack() as ex:
                wide = 3 * KT * D_EXPERT
                hT = c.sb(ex, "hT_2", [P, KT, S])
                places = [hT[:, :, :].rearrange("p k n -> p (k n)")]
                places += [c.sb(ex, f"expert_{i}", [P, wide])[:, :] for i in range(1, SLOTS)]
                experts = Experts(c, ex, places)
                tiles = [(x_sb[:, i, :], c.k["ffn_norm"], hT, i * P) for i in range(TT)]
                norm_transpose(c, "n4", tiles, 0, keep=h_rows, keep_gain=c.k["ffn_norm_row"][:, :], experts=experts)
                route(c, hT, experts, weights, slots, perm, overflow)
                run_experts(c, experts, h_rows, y_rows, perm, overflow)
            combine(c, x_sb, y_rows, weights, slots, out)


def host_constants():
    k = {}
    k["k_ident"] = np.eye(P, dtype=np.float32)
    k["k_zeros"] = np.zeros((P, 256), np.float32)
    k["k_ones"] = np.ones((P, P), np.float32)
    pick = np.zeros((8, 8, P), np.float32)
    for r in range(8):
        pick[r, r, :] = 1.0
    k["k_pick8"] = pick
    dirs = np.zeros((8, 4), np.float32)
    dirs[0:4] = [-1.0, 0.0, 1.0, 0.0]
    dirs[4:8] = [1.0, -1.0, 0.0, 1.0]
    k["k_dir8"] = dirs
    i = np.arange(P)
    k["k_mask_le"] = (i[:, None] <= i[None]).astype(np.float32)
    k["k_mask_lt"] = (i[:, None] < i[None]).astype(np.float32)
    k["k_iota"] = np.tile(np.arange(BLOCKS + 2, dtype=np.float32), (P, 1))
    k["k_iota_p"] = i[:, None].astype(np.float32)
    k["k_thresholds"] = np.tile(np.array([ROWS * (j + 1) for j in range(16)], np.float32), (P, 1))
    k["k_token"] = (i[:, None] + P * np.arange(TT)[None]).astype(np.float32)
    k["k_mask_gt"] = (i[:, None] > i[None]).astype(np.float32)
    levels = [((i[:, None] >> (l + 1)) == (i[None] >> (l + 1))) & ((i[None] >> l) % 2 == 1) & ((i[:, None] >> l) % 2 == 0)
              for l in range(LEVELS)]
    k["k_level_masks"] = np.ascontiguousarray(np.stack(levels, axis=1).astype(np.float32))
    half = G_DIM // 2
    freq = np.float32(10000.0) ** (-np.arange(0, G_DIM, 2, dtype=np.float32) / np.float32(G_DIM))
    ang = (np.arange(S, dtype=np.float32)[:, None] * freq[None]).astype(np.float32)
    cos, sin = np.cos(ang).astype(np.float32), np.sin(ang).astype(np.float32)
    by_token = lambda a: np.ascontiguousarray(a.reshape(TT, P, -1).transpose(1, 0, 2))
    k["t_cos"] = by_token(np.concatenate([cos, cos], axis=1))
    k["t_sin"] = by_token(np.concatenate([-sin, sin], axis=1))
    gamma = np.array([retention_decay(h) for h in range(A_HEADS)])
    k["k_q_decay"] = (gamma[None] ** (i[:, None] + 1)).astype(np.float32)
    k["k_k_decay"] = (gamma[None] ** (P - 1 - i[:, None]) * G_DIM ** -0.5).astype(np.float32)
    table = gamma[None, :, None] ** -(i[:, None, None] + 1.0) * (i[:, None, None] <= i[None, None]) * G_DIM ** -0.5
    k["t_decay"] = np.ascontiguousarray(table.astype(np.float32))
    return k


def by_channel(g, tiles):
    return np.ascontiguousarray(np.asarray(g).reshape(tiles, P).T)


def rows(g):
    g = np.asarray(g).reshape(1, -1)
    return np.ascontiguousarray(np.repeat(g, P, axis=0))


def head_gains(a):
    names = ("g_na_q", "g_na_k", "g_mem_q", "g_mem_k")
    cols = [np.tile(a[n][0], P // a[n].shape[1]) for n in names for _ in range(2)]
    return np.ascontiguousarray(np.stack(cols, axis=1))


def window_bias(rpb):
    rows_n = S // GRID_W
    flat = rpb.reshape(NA_HEADS, -1)
    outside = flat.shape[1]
    flat = np.concatenate([flat, np.full((NA_HEADS, 1), -1.0e30, np.float32)], axis=1)
    index = np.full((P, NA_TABLE), outside, np.int64)
    p = np.arange(P)
    col = p % GRID_W
    c0 = np.clip(col - WIN_C // 2, 0, GRID_W - WIN_C)
    for t in [2] + NA_EDGE:
        k0, k1 = window_tiles(t)
        row = 2 * t + p // GRID_W
        r0 = np.clip(row - WIN_R // 2, 0, rows_n - WIN_R)
        key = k0 * P + np.arange((k1 - k0) * P)
        krow, kcol = key // GRID_W, key % GRID_W
        inside = ((krow[None] >= r0[:, None]) & (krow[None] < r0[:, None] + WIN_R)
                  & (kcol[None] >= c0[:, None]) & (kcol[None] < c0[:, None] + WIN_C))
        at = (krow[None] - row[:, None] + WIN_R - 1) * (2 * WIN_C - 1) + kcol[None] - col[:, None] + WIN_C - 1
        b = bias_at(t)
        index[:, b:b + len(key)] = np.where(inside, at, outside)
    return np.ascontiguousarray(flat[:, index])


def kernel(**inputs):
    import concourse.bacc as bacc
    from concourse.bass_utils import run_bass_kernel_spmd

    a = {k: np.asarray(v) for k, v in inputs.items()}
    arrays = host_constants()
    for name in ("x", "mem"):
        arrays[name] = a[name]
    for name in ("w_in", "w_proj_mlstm", "w_proj_na", "w_mem_kv", "w_proj_mem", "w_out", "w_up", "w_down",
                 "w_in_2", "w_out_2"):
        arrays[name] = a[name][0]
    arrays["k_b_if"] = np.ascontiguousarray(np.stack([a["b_igate"][0].reshape(8), a["b_fgate"][0].reshape(8)], axis=1))
    arrays["k_g_mix"] = by_channel(a["g_mix"][0], KT)
    arrays["k_g_mem"] = by_channel(a["g_mem"][0], KT)
    w_if = a["w_in"][0][:, IN1["gates_if"]:IN1["gates_if"] + 16].reshape(KT, P, 16).transpose(1, 0, 2)
    arrays["k_w_if"] = np.zeros((P, KT, 40), np.float32)
    arrays["k_w_if"][:, :, 0:8], arrays["k_w_if"][:, :, 32:40] = w_if[:, :, 0:8], w_if[:, :, 8:16]
    arrays["k_conv1"] = np.ascontiguousarray(a["conv_w"][0].T.reshape(4, P, M_CONV).transpose(1, 0, 2))
    arrays["k_conv1_b"] = by_channel(a["conv_b"][0], 4)
    arrays["k_g_ffn_row"] = rows(a["g_ffn"][0])
    arrays["k_g_heads"] = head_gains(a)
    arrays["na_bias"] = window_bias(a["rpb"][0])
    arrays["k_attn_norm_row"] = rows(a["attn_norm_2"][0])
    arrays["k_w_ba"] = np.ascontiguousarray(
        a["w_in_2"][0][:, IN2["beta_alpha"]:IN2["beta_alpha"] + 8].reshape(KT, P, 8).transpose(1, 0, 2))
    arrays["k_conv2"] = np.ascontiguousarray(a["conv_a_2"][0].T.reshape(12, P, A_CONV_K).transpose(1, 0, 2))
    arrays["k_norm_a"] = rows(a["norm_a_2"][0])
    arrays["k_norm_b"] = rows(a["norm_b_2"][0])
    arrays["k_a_log"] = rows(a["a_log_2"][0])
    arrays["k_dt_bias"] = rows(a["dt_bias_2"][0])
    arrays["k_ffn_norm"] = by_channel(a["ffn_norm_2"][0], KT)
    arrays["k_ffn_norm_row"] = rows(a["ffn_norm_2"][0])
    arrays["k_final_norm"] = rows(a["final_norm_2"])
    router = np.concatenate([a["w_router_group_2"][0], a["w_router_expert_2"][0]], axis=1)
    arrays["k_w_router"] = np.ascontiguousarray(router.reshape(KT, P, GR).transpose(1, 0, 2))
    for name in ("w_gate_2", "w_up_2", "w_down_2"):
        arrays[name] = a[name][0]
    arrays["k_g_mlstm"] = rows(a["g_mlstm"][0])

    nc = bacc.Bacc("TRN2", target_bir_lowering=False, num_devices=1)
    feeds, io = {}, {}
    for name, v in arrays.items():
        v = np.ascontiguousarray(v)
        feeds["in_" + name] = v
        io[name] = nc.dram_tensor("in_" + name, v.shape, mybir.dt.from_np(v.dtype), kind="ExternalInput").ap()
    out = nc.dram_tensor("out", (1, S, D), F32, kind="ExternalOutput").ap()
    build(nc, io, out)
    r = run_bass_kernel_spmd(nc, [feeds], core_ids=[0])
    return r.results[0]["out"]
```
